# Optimizing a Trainium2 kernel written in Bass

```python
import jax, jax.numpy as jnp
from jax import lax
import numpy as np

D_MODEL = 1024
BATCH = 1
SEQ = 1024
DEPTH = 2

CHUNK = 64
HEAD_DIM = 64
N_HEADS_A = 8
N_HEADS_B = 8
N_HEADS_C = 16
N_KV_HEADS_C = 2
LEFT_CHUNKS_A = 8
REL_CLIP = 256
Q_BLOCK = 128
WINDOW_C = 128
WINDOW_CHUNKS_C = WINDOW_C // CHUNK
ROPE_THETA = 10000.0
NORM_EPS = 1e-6
NEG_INF = -1e30

W_A = N_HEADS_A * HEAD_DIM
W_B = N_HEADS_B * HEAD_DIM
W_QC = N_HEADS_C * HEAD_DIM
W_KVC = N_KV_HEADS_C * HEAD_DIM
D_IN_AB = 3 * W_A + 3 * W_B + N_HEADS_B + (W_A + W_B)
D_IN_C = W_QC + 2 * W_KVC + W_QC

kernel_name = "hybrid_chunked_relbias_fox_swa_sink_encoder"

def rms_norm(x, g):
    xf = x.astype(jnp.float32)
    y = xf * lax.rsqrt(jnp.mean(xf * xf, axis=-1, keepdims=True) + NORM_EPS)
    return (y * g.astype(jnp.float32)).astype(x.dtype)

def split_cols(t, widths):
    offs = list(np.cumsum(widths)[:-1])
    return jnp.split(t, [int(o) for o in offs], axis=-1)

def chunk_band(t, n_left):
    b, s, h, d = t.shape
    nc = s // CHUNK
    tc = t.reshape(b, nc, CHUNK, h, d)
    tp = jnp.pad(tc, ((0, 0), (n_left, 0), (0, 0), (0, 0), (0, 0)))
    idx = jnp.arange(nc)[:, None] + jnp.arange(n_left + 1)[None, :]
    band = tp[:, idx]
    return band.reshape(b, nc, (n_left + 1) * CHUNK, h, d)

def band_valid(nc, n_left):
    slot_chunk = jnp.arange((n_left + 1) * CHUNK) // CHUNK
    key_chunk = jnp.arange(nc)[:, None] - n_left + slot_chunk[None, :]
    return key_chunk >= 0

def rope(x, pos):
    d = x.shape[-1]
    half = d // 2
    inv = ROPE_THETA ** (-jnp.arange(half, dtype=jnp.float32) / half)
    ang = pos.astype(jnp.float32)[:, None] * inv[None, :]
    cos = jnp.cos(ang)[None, :, None, :]
    sin = jnp.sin(ang)[None, :, None, :]
    xf = x.astype(jnp.float32)
    x1, x2 = xf[..., :half], xf[..., half:]
    out = jnp.concatenate([x1 * cos - x2 * sin, x2 * cos + x1 * sin], axis=-1)
    return out.astype(x.dtype)

def chunked_relbias_attention(q, k, v, rel_bias):
    b, s, h, d = q.shape
    nc = s // CHUNK
    band_len = (LEFT_CHUNKS_A + 1) * CHUNK
    qc = q.reshape(b, nc, CHUNK, h, d)
    kb = chunk_band(k, LEFT_CHUNKS_A)
    vb = chunk_band(v, LEFT_CHUNKS_A)
    sc = jnp.einsum('bcqhd,bckhd->bchqk', qc, kb).astype(jnp.float32) * (d ** -0.5)
    dist = LEFT_CHUNKS_A * CHUNK + jnp.arange(CHUNK)[:, None] - jnp.arange(band_len)[None, :]
    ridx = jnp.clip(dist, -REL_CLIP, REL_CLIP) + REL_CLIP
    bias = rel_bias.astype(jnp.float32)[:, ridx]
    valid = band_valid(nc, LEFT_CHUNKS_A)
    sc = jnp.where(valid[None, :, None, None, :], sc + bias[None, None], NEG_INF)
    p = jax.nn.softmax(sc, axis=-1).astype(v.dtype)
    out = jnp.einsum('bchqk,bckhd->bcqhd', p, vb)
    return out.reshape(b, s, h, d)

def forgetting_attention(q, k, v, log_f):
    b, s, h, d = q.shape
    nqb = s // Q_BLOCK
    scale = d ** -0.5
    cum = jnp.cumsum(log_f, axis=1)
    cum_k = cum.transpose(0, 2, 1)
    qb = q.reshape(b, nqb, Q_BLOCK, h, d).transpose(1, 0, 3, 2, 4)
    cq = cum.reshape(b, nqb, Q_BLOCK, h).transpose(1, 0, 3, 2)
    kpos = jnp.arange(s)

    def block(args):
        qi, ci, i = args
        qpos = i * Q_BLOCK + jnp.arange(Q_BLOCK)
        sc = jnp.einsum('bhqd,bshd->bhqs', qi, k).astype(jnp.float32) * scale
        sc = sc + ci[..., None] - cum_k[:, :, None, :]
        sc = jnp.where((kpos[None, :] <= qpos[:, None])[None, None], sc, NEG_INF)
        p = jax.nn.softmax(sc, axis=-1).astype(v.dtype)
        return jnp.einsum('bhqs,bshd->bqhd', p, v)

    out = lax.map(block, (qb, cq, jnp.arange(nqb)))
    return out.transpose(1, 0, 2, 3, 4).reshape(b, s, h, d)

def sliding_window_sink_gqa(q, k, v, sinks):
    b, s, hq, d = q.shape
    hkv = k.shape[2]
    g = hq // hkv
    nc = s // CHUNK
    n_left = WINDOW_CHUNKS_C - 1
    qc = q.reshape(b, nc, CHUNK, hkv, g, d)
    kb = chunk_band(k, n_left)
    vb = chunk_band(v, n_left)
    sc = jnp.einsum('bcqkgd,bcskd->bckgqs', qc, kb).astype(jnp.float32) * (d ** -0.5)
    valid = band_valid(nc, n_left)
    sc = jnp.where(valid[None, :, None, None, None, :], sc, NEG_INF)
    sink = jnp.broadcast_to(sinks.astype(jnp.float32).reshape(1, 1, hkv, g, 1, 1),
                            sc.shape[:-1] + (1,))
    p = jax.nn.softmax(jnp.concatenate([sc, sink], axis=-1), axis=-1)[..., :-1]
    out = jnp.einsum('bckgqs,bcskd->bcqkgd', p.astype(v.dtype), vb)
    return out.reshape(b, s, hq, d)

def layer_ab(x, norm_g, w_in, rel_bias, f_bias, w_out):
    b, s, _ = x.shape
    h = rms_norm(x, norm_g)
    proj = h @ w_in
    qa, ka, va, qb, kb, vb, f_logit, gate = split_cols(
        proj, [W_A, W_A, W_A, W_B, W_B, W_B, N_HEADS_B, W_A + W_B])
    heads = lambda t, n: t.reshape(b, s, n, HEAD_DIM)
    log_f = jax.nn.log_sigmoid((f_logit + f_bias).astype(jnp.float32))
    ya = chunked_relbias_attention(heads(qa, N_HEADS_A), heads(ka, N_HEADS_A),
                                   heads(va, N_HEADS_A), rel_bias)
    yb = forgetting_attention(heads(qb, N_HEADS_B), heads(kb, N_HEADS_B),
                              heads(vb, N_HEADS_B), log_f)
    y = jnp.concatenate([ya.reshape(b, s, W_A), yb.reshape(b, s, W_B)], axis=-1)
    y = y * jax.nn.silu(gate)
    return x + y @ w_out

def layer_c(x, norm_g, w_in, sinks, w_out):
    b, s, _ = x.shape
    h = rms_norm(x, norm_g)
    proj = h @ w_in
    q, k, v, gate = split_cols(proj, [W_QC, W_KVC, W_KVC, W_QC])
    pos = jnp.arange(s)
    q = rope(q.reshape(b, s, N_HEADS_C, HEAD_DIM), pos)
    k = rope(k.reshape(b, s, N_KV_HEADS_C, HEAD_DIM), pos)
    v = v.reshape(b, s, N_KV_HEADS_C, HEAD_DIM)
    y = sliding_window_sink_gqa(q, k, v, sinks).reshape(b, s, W_QC)
    y = y * jax.nn.silu(gate)
    return x + y @ w_out

def setup_inputs(seed: int = 0) -> dict:
    key = jax.random.key(seed)
    ks = jax.random.split(key, 12)
    f32 = jnp.float32
    x = jax.random.normal(ks[0], (BATCH, SEQ, D_MODEL), f32)
    norm_0 = 1.0 + 0.05 * jax.random.normal(ks[1], (D_MODEL,), f32)
    w_in_0 = jax.random.normal(ks[2], (D_MODEL, D_IN_AB), f32) * D_MODEL ** -0.5
    rel_bias_0 = 0.1 * jax.random.normal(ks[3], (N_HEADS_A, 2 * REL_CLIP + 1), f32)
    f_bias_0 = 2.0 + 0.5 * jax.random.normal(ks[4], (N_HEADS_B,), f32)
    w_out_0 = jax.random.normal(ks[5], (W_A + W_B, D_MODEL), f32) * (W_A + W_B) ** -0.5
    norm_1 = 1.0 + 0.05 * jax.random.normal(ks[6], (D_MODEL,), f32)
    w_in_1 = jax.random.normal(ks[7], (D_MODEL, D_IN_C), f32) * D_MODEL ** -0.5
    sinks_1 = 0.5 * jax.random.normal(ks[8], (N_HEADS_C,), f32)
    w_out_1 = jax.random.normal(ks[9], (W_QC, D_MODEL), f32) * W_QC ** -0.5
    norm_f = 1.0 + 0.05 * jax.random.normal(ks[10], (D_MODEL,), f32)
    return {"x": x, "norm_0": norm_0, "w_in_0": w_in_0, "rel_bias_0": rel_bias_0,
            "f_bias_0": f_bias_0, "w_out_0": w_out_0, "norm_1": norm_1,
            "w_in_1": w_in_1, "sinks_1": sinks_1, "w_out_1": w_out_1, "norm_f": norm_f}

def reference(x, norm_0, w_in_0, rel_bias_0, f_bias_0, w_out_0,
              norm_1, w_in_1, sinks_1, w_out_1, norm_f):
    layers = (
        lambda h: layer_ab(h, norm_0, w_in_0, rel_bias_0, f_bias_0, w_out_0),
        lambda h: layer_c(h, norm_1, w_in_1, sinks_1, w_out_1),
    )
    for i in range(DEPTH):
        x = layers[i % 2](x)
    return rms_norm(x, norm_f)


_drawn_inputs = setup_inputs


def setup_inputs(seed=0):
    import zlib

    import numpy as np

    out = dict(_drawn_inputs(seed))
    spreads = {}
    factors = {'norm_0': 3.143, 'rel_bias_0': 8.0, 'norm_1': 6.322, 'sinks_1': 8.0}
    for name, (base, spread) in spreads.items():
        noise = np.random.default_rng([zlib.crc32(name.encode()), seed]).standard_normal(out[name].shape)
        drawn = base * np.exp(spread * noise) if base else spread * noise
        out[name] = __import__('jax').numpy.asarray(drawn.astype(out[name].dtype))
    for name, factor in factors.items():
        out[name] = (out[name] * factor).astype(out[name].dtype)
    return out
```

```python
from contextlib import ExitStack

import concourse.bass as bass
from concourse import mybir

F32 = mybir.dt.float32
F32R = mybir.dt.float32r
ALU = mybir.AluOpType
ACT = mybir.ActivationFunctionType

P = 128
HD = 64
SEQ = 1024
DM = 1024
NT = SEQ // P
NK = DM // P
HALF = SEQ // 2
HEADS = 16
PAIRS = HEADS // 2
PAIRS_A = 4
CLIP = 256
EXT = 640
BIG = 1e30
EPS = 1e-6
W_A = 512
GATE0 = 3 * W_A + 3 * W_A + 8
F_COL = 3 * W_A + 3 * W_A
KC, VC, GATE1 = 1024, 1152, 1280

HI, LO = 0, 1
TERMS = ((HI, HI), (HI, LO), (LO, HI))


class WindowPlan:

    def __init__(self, steps, groups, proj_slots):
        self.steps = steps
        self.slots = len(steps) + 2
        weights = [w for w in groups for _ in range(NK * len(TERMS))]
        total, parts = sum(weights), 2 * proj_slots
        self.parts, self.ends = [], [[] for _ in range(2 * self.slots)]
        done, m = 0, 0
        for part in range(parts):
            first = m
            while m < len(weights) and done * parts < total * (part + 1):
                done += weights[m]
                m += 1
                if m % (NK * len(TERMS)) == 0:
                    self.ends[part].append(m // (NK * len(TERMS)) - 1)
            self.parts.append((first, m))
        while len(self.parts) < 2 * self.slots:
            self.parts.append((m, m))
        self.chunk_end, n = [], 0
        for chunks in steps:
            n += len(chunks)
            self.chunk_end.append(n)
        self.n_chunks = n

    def chunk0(self, s):
        return self.chunk_end[s - 1] if s else 0


def key_tiles(kind, i):
    n = min(i + 1, 5) if kind == "A" else i + 1
    return i + 1 - n, n


def key_chunks(n):
    return [(0, n)] if n <= 4 else [(0, (n + 1) // 2), ((n + 1) // 2, n // 2)]


def plan_ab(kind):
    steps = [key_chunks(key_tiles(kind, i)[1]) for _ in range(2) for i in range(NT)]
    return WindowPlan(steps, [2] * 4 + [1] * NT, 2 * NT + 2)


def plan_c():
    return WindowPlan([[(0, 1)]] * NT, [1] * NT, NT + 1)


def build_trunk(nc, x, norm_0, w_in_0, rel_bias_0, f_bias_0, w_out_0, norm_1, w_in_1, sinks_1,
                w_out_1, norm_f, c_ident, c_causal, c_window, c_rope, out):
    x = x[0]
    out = out[0]
    ext_dram = nc.dram_tensor("ext_bias", (8, EXT), F32, kind="Internal").ap()
    cum_dram = nc.dram_tensor("cum_forget", (8, SEQ), F32, kind="Internal").ap()
    y_dram = nc.dram_tensor("y_gated", (2, SEQ, DM), F32, kind="Internal").ap()
    x1_dram = nc.dram_tensor("x_mid", (SEQ, DM), F32, kind="Internal").ap()

    PLAN = {"A": plan_ab("A"), "B": plan_ab("B"), "C": plan_c()}
    CH_AB = PLAN["A"].n_chunks
    assert CH_AB == PLAN["B"].n_chunks and CH_AB % 6 == 0

    ctx = ExitStack()
    with ctx:
        def sem(name):
            return ctx.enter_context(nc.semaphore(name))

        base = nc.sbuf_base
        base += (-base) % 64
        top = [base]

        def at(name, shape, dt, offset):
            return nc.alloc_sbuf_tensor_at(name, shape, dt, offset=offset)

        def put(name, shape, dt=F32):
            size = 4
            for s in shape[1:]:
                size *= s
            t = at(name, shape, dt, top[0])
            top[0] += size + (-size) % 32
            return t

        R0 = top[0]
        hT0 = at("hT0", [P, 2, NK, SEQ], F32R, R0)
        Wo0 = at("Wo0", [P, 2, NK, DM], F32R, R0)
        QZ1 = [at(f"QZ1_{b}", [P, 2, SEQ], F32R, R0 + 8192 * b) for b in range(2)]
        KX1 = at("KX1", [P, 2, 2, SEQ], F32R, R0 + 16384)
        V1 = at("V1", [P, NT, 2, P], F32R, R0 + 32768)
        SG1 = [at(f"SG1_{b}", [P, NT, P], F32, R0 + 40960 + 4096 * b) for b in range(2)]
        ROPE = at("ROPE", [P, NT, 2, HD], F32, R0 + 49152)
        R1 = R0 + 65536
        xt0 = at("xt0", [P, NT, DM], F32, R1)
        QZ0 = [at(f"QZ0_{b}", [P, 2, SEQ], F32R, R1 + 8192 * b) for b in range(2)]
        KX0 = [at(f"KX0_{b}", [P, 2, 2, SEQ], F32R, R1 + 16384 + 16384 * b) for b in range(2)]
        V0 = [at(f"V0_{b}", [P, NT, 2, P], F32R, R1 + 49152 + 8192 * b) for b in range(2)]
        SG0 = [at(f"SG0_{b}", [P, NT, P], F32, R1 + 65536 + 4096 * b) for b in range(2)]
        hT1 = at("hT1", [P, 2, NK, SEQ], F32R, R1)
        Wo1 = at("Wo1", [P, 2, NK, DM], F32R, R1)
        R2 = R1 + 73728
        Wslot = [at(f"W_{b}", [P, 2, NK, 2 * P], F32R, R2 + 16384 * b) for b in range(2)]
        yT = [at(f"yT_{b}", [P, 2, NK, P], F32R, R2 + 16384 + 8192 * b) for b in range(2)]
        XR = at("XR", [P, 2, DM], F32, R1 + 65536)
        R3 = R2 + 32768
        raw = at("raw", [P, NK, 2 * P], F32, R3)
        rawo = raw[:].rearrange("p a b -> p (a b)").rearrange("p (k n) -> p k n", n=DM)
        R4 = R3 + 8192
        L = at("L", [P, 2, SEQ], F32, R4)
        YT = at("YT", [P, 2, DM], F32, R4)
        junk = at("junk", [P, DM], F32, R4)
        R5 = R4 + 8192
        PT = [at(f"PT_{b}", [P, 2, 512], F32R, R5 + 4096 * b) for b in range(2)]
        HN = at("HN", [P, 2, DM], F32, R5)
        X1 = at("X1", [P, 2, DM], F32, R5)
        R6 = R5 + 8192
        BIAS = at("BIAS", [P, 2, SEQ], F32, R6)
        GB = at("GB", [P, DM], F32, R6)
        HN1 = at("HN1", [P, 2, DM], F32, R6)
        fz = at("fz", [8, SEQ], F32, R4)
        fe = at("fe", [8, SEQ], F32, R4 + 4096)
        fa = at("fa", [8, SEQ], F32, R5)
        fl = at("fl", [8, SEQ], F32, R5 + 4096)
        Wf = at("Wf", [P, NK, 8], F32, R6 + 4096)
        WfR = at("WfR", [P, 2, NK, 8], F32R, R6 + 4096 + 512)
        extrow = at("extrow", [8, EXT], F32, R6 + 4096 + 1024)
        fb = at("fb", [8, 1], F32, R6 + 4096 + 1024 + 4 * EXT)
        R7 = R6 + 8192
        Y = at("Y", [P, NT, P], F32, R7)
        GB1 = at("GB1", [P, DM], F32, R7)
        top[0] = R7 + 4096
        ident = put("ident", [P, P])
        triR_at = top[0]
        triR = put("triR", [P, P], F32R)
        identR = put("identR", [P, P], F32R)
        HK = put("HK", [P, 384])
        QR = at("QR", [P, 2, P], F32, triR_at)
        QS = HK[:, 2 * P:3 * P]
        relc = put("relc", [P, 8])
        sinkc = put("sinkc", [P, HEADS])
        nsink = put("nsink", [P, HEADS])
        stats_at = top[0]
        ysum = put("ysum", [P, P])
        negm = put("negm", [P, 4, 2])
        nmpart = put("nmpart", [P, 1])
        rs = put("rs", [P, 4, 2])
        rinv = put("rinv", [P, 4, 2])
        snm = put("snm", [P, 4, 2])
        es = put("es", [P, 4, 2])
        ss = at("ss", [P, NT], F32, stats_at + 0)
        var = at("var", [P, NT], F32, stats_at + 32)
        sd = at("sd", [P, NT], F32, stats_at + 64)
        r0 = at("r0", [P, NT], F32, stats_at + 96)
        nt1 = at("nt1", [P, NT], F32, stats_at + 128)
        nt2 = at("nt2", [P, NT], F32, stats_at + 160)
        rstd = at("rstd", [P, NT], F32, stats_at + 192)
        assert top[0] <= nc.sbuf_usable_end, (top[0], nc.sbuf_usable_end)
        WM = HK[:, 0:2 * P]
        trif = HK[:, 0:P]

        def bank(name):
            return ctx.enter_context(nc.psum_tensor(name, [P, 512], F32))

        S = [bank(f"S{i}") for i in range(3)]
        T = [bank(f"T{i}") for i in range(2)]
        J = [bank(f"J{i}") for i in range(2)]
        PV = bank("PV")

        s_x = [sem(f"x_loaded{i}") for i in range(NT)]
        s_const = sem("consts_loaded")
        s_small = sem("small_inputs_loaded")
        s_square = sem("squares_summed")
        s_var = sem("variances_ready")
        s_sqrt = sem("roots_ready")
        s_norm = sem("norm_chain")
        s_hn = sem("normed_rows_ready")
        s_ht = sem("normed_transposed")
        s_hthi = sem("hT_hi_written")
        s_htlo = sem("hT_lo_written")
        s_idr = sem("rounded_consts_ready")
        s_wf = sem("forget_weights_split")
        s_f = sem("forget_logits_ready")
        s_fa = sem("forget_chain_act")
        s_fd = sem("forget_chain_dve")
        s_cum = sem("cum_stored")
        s_extf = sem("ext_row_filled")
        s_ext = sem("ext_row_stored")
        s_raw = sem("raw_weights_loaded")
        s_wh = sem("weights_hi_written")
        s_w = sem("weights_split")
        s_wo = sem("out_weights_split")
        s_woh = sem("out_weights_hi_written")
        s_gb = sem("norm_weights_loaded")
        s_jo = sem("residual_added")
        s_ytr = sem("y_transposed")
        s_ythi = sem("yT_hi_written")
        s_ytlo = sem("yT_lo_written")
        s_st = [sem(f"x1_tile_stored{b}") for b in range(2)]
        s_ot = [sem(f"out_tile_stored{b}") for b in range(2)]
        s_rope_c = sem("layer1_tables_loaded")
        s_hk = sem("hankel_loaded")
        s_biasp = sem("bias_chain")
        s_bias = sem("bias_built")
        s_ck = [sem(f"cum_row_broadcast{h}") for h in range(2)]
        s_proj = sem("projection_group_done")
        s_jhi = sem("projection_hi_written")
        s_j = sem("projection_evacuated")
        s_kdup = sem("k_duplicated")
        s_scores = sem("scores_ready")
        s_sdone = sem("rows_written")
        s_snm = sem("sink_shift_ready")
        s_probs = sem("probs_ready")
        s_tr = sem("transposed")
        s_hi = sem("transposed_hi_written")
        s_lo = sem("transposed_lo_written")
        s_pv = sem("pv_chunk_done")
        s_tot = sem("totals_ready")
        s_rinv = sem("reciprocals_ready")
        s_y = sem("y_written")
        s_ysum = sem("pv_halves_added")
        s_yst = sem("y_stored")
        s_qr = sem("rope_products")
        s_rope = sem("rotated_ready")
        s_yt = [sem(f"y_tile_loaded{b}") for b in range(2)]
        s_xr = [sem(f"x_tile_loaded{b}") for b in range(2)]
        s_x1st = sem("x1_stored")
        s_mm = sem("out_projection_done")
        s_x1 = sem("x1_ready")

        def raw_count(n):
            return 32 * (n + 1) + (64 if n >= 2 * PAIRS else 0)

        def load_w(sp, n, blocks):
            if n >= 1:
                sp.wait_ge(s_w, n)
            for b, src in enumerate(blocks):
                sp.dma_start(raw[:, :, P * b:P * b + P], src).then_inc(s_raw, 16)

        def split_w(pool, n, need):
            pool.wait_ge(s_raw, raw_count(n))
            if need is not None:
                pool.wait_ge(s_proj, need)
            nc.gpsimd.tensor_copy(Wslot[n % 2][:, HI], raw[:]).then_inc(s_wh, 1)
            pool.wait_ge(s_wh, n + 1)
            nc.gpsimd.tensor_tensor(Wslot[n % 2][:, LO], raw[:], Wslot[n % 2][:, HI].bitcast(F32),
                                    ALU.subtract).then_inc(s_w, 1)

        def cols(w, c):
            return w[:, c:c + P].rearrange("(k p) c -> p k c", p=P)

        def blocks_of(n):
            if n < 2 * PAIRS:
                p = n // 2
                o = P * p if p < PAIRS_A else 3 * W_A + P * (p - PAIRS_A)
                if n % 2 == 0:
                    return [cols(w_in_0, o), cols(w_in_0, o + W_A)]
                return [cols(w_in_0, o + 2 * W_A), cols(w_in_0, GATE0 + P * p)]
            if n == 2 * PAIRS:
                return [cols(w_in_1, KC), cols(w_in_1, VC)]
            p = n - 2 * PAIRS - 1
            return [cols(w_in_1, P * p), cols(w_in_1, GATE1 + P * p)]

        BLK1 = 2 * PAIRS
        GRP1 = 12 * PAIRS
        TR1 = CH_AB * PAIRS
        CH1 = CH_AB * PAIRS
        ST1 = 16 * PAIRS

        def rsqrt_chain(a, n):
            nc.vector.reciprocal(r0[:, a], sd[:, a]).then_inc(s_norm, 1)
            nc.vector.wait_ge(s_norm, 5 * n + 1)
            nc.vector.tensor_tensor(nt1[:, a], r0[:, a], r0[:, a], ALU.mult).then_inc(s_norm, 1)
            nc.vector.wait_ge(s_norm, 5 * n + 2)
            nc.vector.tensor_tensor(nt2[:, a], nt1[:, a], var[:, a], ALU.mult).then_inc(s_norm, 1)
            nc.vector.wait_ge(s_norm, 5 * n + 3)
            nc.vector.tensor_scalar(nt1[:, a], nt2[:, a], -0.5, 1.5, ALU.mult, ALU.add).then_inc(s_norm, 1)
            nc.vector.wait_ge(s_norm, 5 * n + 4)
            nc.vector.tensor_tensor(rstd[:, a], r0[:, a], nt1[:, a], ALU.mult).then_inc(s_norm, 1)
            nc.vector.wait_ge(s_norm, 5 * n + 5)

        with nc.Block() as block:
            @block.sync
            def _(sp):
                for i in range(NT):
                    sp.dma_start(xt0[:, i, :], x[P * i:P * i + P, :]).then_inc(s_x[i], 16)
                load_w(sp, 0, blocks_of(0))
                load_w(sp, 1, blocks_of(1))
                sp.wait_ge(s_extf, 2)
                sp.dma_start(ext_dram, extrow[:]).then_inc(s_ext, 16)
                sp.wait_ge(s_ext, 16)
                sp.wait_ge(s_fd, 5)
                sp.dma_start(cum_dram, fl[:]).then_inc(s_cum, 16)
                sp.wait_ge(s_cum, 16)

            @block.gpsimd
            def _(pool):
                pool.wait_ge(s_small, 16 * 5)
                nc.gpsimd.tensor_copy(WfR[:, HI], Wf[:]).then_inc(s_wf, 1)
                pool.wait_ge(s_wf, 1)
                nc.gpsimd.tensor_tensor(WfR[:, LO], Wf[:], WfR[:, HI].bitcast(F32),
                                        ALU.subtract).then_inc(s_wf, 1)
                nc.gpsimd.memset(extrow[:, 513:EXT], 0.0).then_inc(s_extf, 1)
                pool.wait_ge(s_extf, 1)
                nc.gpsimd.tensor_scalar(extrow[:, 513:EXT], extrow[:, 513:EXT], extrow[:, 512:513], None,
                                        ALU.add).then_inc(s_extf, 1)
                split_w(pool, 0, None)
                split_w(pool, 1, None)

            @block.scalar
            def _(act):
                act.dma_start(ident[:], c_ident).then_inc(s_const, 16)
                act.dma_start(trif, c_causal).then_inc(s_const, 16)
                bcast = bass.AP(norm_0.tensor, norm_0.offset, [[0, P], [1, DM]])
                act.dma_start(GB[:], bcast).then_inc(s_const, 16)
                act.dma_start(Wf[:], w_in_0[:, F_COL:F_COL + 8].rearrange("(k p) c -> p k c", p=P))\
                    .then_inc(s_small, 16)
                act.dma_start(extrow[:, 0:513], rel_bias_0).then_inc(s_small, 16)
                act.dma_start(relc[:], bass.AP(rel_bias_0.tensor, rel_bias_0.offset + 2 * CLIP,
                                               [[0, P], [2 * CLIP + 1, 8]]),
                              allow_slow_non_contiguous=True)\
                    .then_inc(s_small, 16)
                act.dma_start(fb[:], f_bias_0.rearrange("(h o) -> h o", o=1)).then_inc(s_small, 16)
                act.dma_start(sinkc[:], bass.AP(sinks_1.tensor, sinks_1.offset, [[0, P], [1, HEADS]]))\
                    .then_inc(s_small, 16)
                act.wait_ge(s_const, 48)
                nc.scalar.activation(identR[:], ident[:], ACT.Copy).then_inc(s_idr, 1)
                nc.scalar.activation(triR[:], trif, ACT.Copy).then_inc(s_idr, 1)
                for i in range(NT):
                    act.wait_ge(s_x[i], 16)
                    if i >= 1:
                        act.wait_ge(s_square, i)
                    nc.scalar.activation(junk[:], xt0[:, i, :], ACT.Square,
                                         accum_out=ss[:, i:i + 1]).then_inc(s_square, 1)
                act.wait_ge(s_var, 1)
                nc.scalar.activation(sd[:], var[:], ACT.Sqrt).then_inc(s_sqrt, 1)
                for i in range(NT):
                    for c in range(2):
                        act.wait_ge(s_ht, 2 * i + c + 1)
                        nc.scalar.activation(hT0[:, HI, 4 * c:4 * c + 4, P * i:P * i + P],
                                             T[c][:].rearrange("p (k t) -> p k t", k=4),
                                             ACT.Copy).then_inc(s_hthi, 1)
                act.wait_ge(s_fd, 2)
                nc.scalar.activation(fe[:], fa[:], ACT.Exp).then_inc(s_fa, 1)
                act.wait_ge(s_fa, 1)
                nc.scalar.activation(fa[:], fe[:], ACT.Ln, bias=1.0).then_inc(s_fa, 1)

            @block.vector
            def _(dve):
                dve.wait_ge(s_square, NT)
                nc.vector.tensor_scalar(var[:], ss[:], 1.0 / DM, EPS, ALU.mult, ALU.add).then_inc(s_var, 1)
                dve.wait_ge(s_sqrt, 1)
                rsqrt_chain(slice(0, NT), 0)
                dve.wait_ge(s_const, 48)

                def normed(i):
                    if i >= 2:
                        dve.wait_ge(s_ht, 2 * i - 2)
                    nc.vector.scalar_tensor_tensor(HN[:, i % 2, :], xt0[:, i, :], rstd[:, i:i + 1], GB[:],
                                                   ALU.mult, ALU.mult).then_inc(s_hn, 1)

                def lo(i):
                    for c in range(2):
                        dve.wait_ge(s_hthi, 2 * i + c + 1)
                        nc.vector.tensor_tensor(hT0[:, LO, 4 * c:4 * c + 4, P * i:P * i + P],
                                                T[c][:].rearrange("p (k t) -> p k t", k=4),
                                                hT0[:, HI, 4 * c:4 * c + 4, P * i:P * i + P].bitcast(F32),
                                                ALU.subtract).then_inc(s_htlo, 1)

                normed(0)
                for i in range(NT):
                    if i + 1 < NT:
                        normed(i + 1)
                    lo(i)
                for c in range(2):
                    dve.wait_ge(s_f, c + 1)
                    ins = nc.vector.tensor_scalar(fz[:, HALF * c:HALF * c + HALF], J[c][0:8, :], fb[:, 0:1],
                                                  None, ALU.add)
                ins.then_inc(s_fd, 1)
                dve.wait_ge(s_fd, 1)
                nc.vector.scalar_tensor_tensor(fa[:], fz[:], -1.0, fz[:], ALU.mult, ALU.min).then_inc(s_fd, 1)
                dve.wait_ge(s_fa, 2)
                nc.vector.scalar_tensor_tensor(fe[:], fz[:], 0.0, fa[:], ALU.min, ALU.subtract)\
                    .then_inc(s_fd, 1)
                dve.wait_ge(s_fd, 3)
                nc.vector.memset(fz[:], 1.0).then_inc(s_fd, 1)
                dve.wait_ge(s_fd, 4)
                nc.vector.tensor_tensor_scan(fl[:], fz[:], fe[:], 0.0, ALU.mult, ALU.add).then_inc(s_fd, 1)

            @block.tensor
            def _(pe):
                pe.wait_ge(s_const, 48)
                for i in range(NT):
                    pe.wait_ge(s_hn, i + 1)
                    for c in range(2):
                        if i >= 1:
                            pe.wait_ge(s_htlo, 2 * i - 1 + c)
                        for k in range(4):
                            mm = nc.tensor.transpose(T[c][:, P * k:P * k + P],
                                                     HN[:, i % 2, P * (4 * c + k):P * (4 * c + k) + P],
                                                     ident[:])
                        mm.then_inc(s_ht, 1)
                pe.wait_ge(s_wf, 2)
                pe.wait_ge(s_htlo, 2 * NT)
                for c in range(2):
                    for k in range(NK):
                        for n, (a, b) in enumerate(TERMS):
                            mm = nc.tensor.matmul(J[c][0:8, :], WfR[:, a, k, :],
                                                  hT0[:, b, k, HALF * c:HALF * c + HALF],
                                                  start=(k == 0 and n == 0), stop=(k == NK - 1 and n == 2))
                    mm.then_inc(s_f, 1)

        def pe_project(g0, m0, m1, layer, blk):
            hT = hT0 if layer == 0 else hT1
            per = NK * len(TERMS)
            for m in range(m0, m1):
                g, r = m // per, m % per
                k, (a, b) = r // len(TERMS), TERMS[r % len(TERMS)]
                transposed = layer == 0 and g < 4
                slot_par = 0 if transposed else 1
                if layer == 1:
                    slot_par = blk
                if r == 0:
                    if layer == 0 and g in (0, 4):
                        pe.wait_ge(s_w, g0 // 6 + (1 if g == 0 else 2))
                    if not (is_int(g0) and g0 + g < 2):
                        pe.wait_ge(s_j, g0 + g - 1)
                W = Wslot[slot_par]
                if transposed:
                    which, half = g // 2, g % 2
                    mm = nc.tensor.matmul(J[g % 2][:], W[:, a, k, P * which:P * which + P],
                                          hT[:, b, k, HALF * half:HALF * half + HALF],
                                          start=(r == 0), stop=(r == per - 1))
                else:
                    t = g - 4 if layer == 0 else g
                    mm = nc.tensor.matmul(J[g % 2][:, 0:2 * P], hT[:, a, k, P * t:P * t + P],
                                          W[:, b, k, :], start=(r == 0), stop=(r == per - 1))
                if r == per - 1:
                    mm.then_inc(s_proj, 1)

        pe = nc.tensor

        def is_int(v):
            return isinstance(v, int)

        def ring_wait(eng, s, local, ring, base):
            value = base + (local - ring + 1 if local >= ring else 0)
            if is_int(value) and value <= 0:
                return
            eng.wait_ge(s, value)

        def pe_window_ab(kind, w, par, attn, proj):
            plan = PLAN[kind]
            c0, st0 = CH_AB * w, 16 * w
            g0 = 12 * (w + 1)

            def scores(s):
                h, i = s // NT, s % NT
                k0, nk = key_tiles(kind, i)
                if s == 0:
                    pe.wait_ge(s_kdup, 32 * w + 32)
                    pe.wait_ge(s_j, 12 * w + 4)
                for n, (j0, nj) in enumerate(plan.steps[s]):
                    c = plan.chunk0(s) + n
                    ring_wait(pe, s_sdone, c, 3, c0)
                    o = S[c % 3][:, 0:P * nj]
                    q = QZ0[par][:, h, P * i:P * i + P]
                    diag = kind == "B" and j0 + nj == nk
                    for hl in range(2):
                        mm = nc.tensor.matmul(o, q, KX0[par][:, hl, h, P * (k0 + j0):P * (k0 + j0 + nj)],
                                              start=(hl == HI), stop=(hl == LO and not diag))
                    if diag:
                        mm = nc.tensor.matmul(S[c % 3][:, P * (nj - 1):P * nj], identR[:], triR[:],
                                              start=False, stop=True)
                    mm.then_inc(s_scores, 1)

            def transposes(s):
                pe.wait_ge(s_probs, st0 + s + 1)
                for n, (j0, nj) in enumerate(plan.steps[s]):
                    c = plan.chunk0(s) + n
                    ring_wait(pe, s_lo, c, 2, c0)
                    for b in range(nj):
                        mm = nc.tensor.transpose(T[c % 2][:, P * b:P * b + P],
                                                 L[:, s % 2, P * (j0 + b):P * (j0 + b) + P], ident[:])
                    mm.then_inc(s_tr, 1)

            def times_v(s):
                h, i = s // NT, s % NT
                k0, nk = key_tiles(kind, i)
                if s == 0:
                    pe.wait_ge(s_j, 12 * w + 12)
                ring_wait(pe, s_y, s, 1, st0)
                for n, (j0, nj) in enumerate(plan.steps[s]):
                    c = plan.chunk0(s) + n
                    pe.wait_ge(s_lo, c0 + c + 1)
                    for b in range(nj):
                        for pa in range(2):
                            mm = nc.tensor.matmul(PV[:, 0:P], PT[c % 2][:, pa, P * b:P * b + P],
                                                  V0[par][:, k0 + j0 + b, :, HD * h:HD * h + HD],
                                                  start=(j0 + b == 0 and pa == HI),
                                                  stop=(j0 + b == nk - 1 and pa == LO))
                    mm.then_inc(s_pv, 1)

            for slot in range(plan.slots):
                if attn and slot < 16:
                    scores(slot)
                if proj:
                    pe_project(g0, *plan.parts[2 * slot], 0, 0)
                if attn and 1 <= slot <= 16:
                    transposes(slot - 1)
                if proj:
                    pe_project(g0, *plan.parts[2 * slot + 1], 0, 0)
                if attn and slot >= 2:
                    times_v(slot - 2)

        act = nc.scalar

        def act_window_ab(kind, w, par, attn, proj):
            plan = PLAN[kind]
            c0 = CH_AB * w
            np_ = 1 - par
            g0 = 12 * (w + 1)
            def split(groups):
                for g in groups:
                    act.wait_ge(s_proj, g0 + g + 1)
                    if g < 4:
                        act_qk(g, np_)
                    else:
                        act_vg(g, g - 4, V0[np_], SG0[np_])

            for slot in range(plan.slots + 1):
                if proj and slot >= 1:
                    split(plan.ends[2 * slot - 1])
                if attn and slot < 16:
                    s, (k0, nk) = slot, key_tiles(kind, slot % NT)
                    act.wait_ge(s_sdone, c0 + plan.chunk_end[s])
                    nc.scalar.activation(L[:, s % 2, 0:P * nk], L[:, s % 2, 0:P * nk], ACT.Exp,
                                         bias=negm[:, s % 4, 0:1], scale=-1.0,
                                         accum_out=rs[:, s % 4, 0:1]).then_inc(s_probs, 1)
                if proj and slot < plan.slots:
                    split(plan.ends[2 * slot])
                if attn and 1 <= slot <= 16:
                    s = slot - 1
                    for n, (j0, nj) in enumerate(plan.steps[s]):
                        c = plan.chunk0(s) + n
                        act.wait_ge(s_tr, c0 + c + 1)
                        ring_wait(act, s_pv, c, 2, c0)
                        nc.scalar.activation(PT[c % 2][:, HI, 0:P * nj], T[c % 2][:, 0:P * nj],
                                             ACT.Copy).then_inc(s_hi, 1)

        def act_qk(g, np_):
            which, half = g // 2, g % 2
            for h in range(2):
                own = slice(HD * h, HD * h + HD)
                tok = slice(HALF * half, HALF * half + HALF)
                if which == 0:
                    ins = nc.scalar.activation(QZ0[np_][own, h, tok], J[g % 2][own, :], ACT.Copy,
                                               scale=-0.125)
                else:
                    ins = nc.scalar.activation(KX0[np_][own, HI, h, tok], J[g % 2][own, :], ACT.Copy)
            ins.then_inc(s_jhi, 1)

        def act_vg(g, t, V, SG):
            nc.scalar.activation(V[:, t, HI, :], J[g % 2][:, 0:P], ACT.Copy, scale=0.5)
            nc.scalar.activation(SG[:, t, :], J[g % 2][:, P:2 * P], ACT.Tanh, scale=0.5)\
                .then_inc(s_jhi, 1)

        dve = nc.vector

        def dve_window_ab(kind, w, par, attn, proj):
            plan = PLAN[kind]
            c0, st0 = CH_AB * w, 16 * w
            np_ = 1 - par
            g0 = 12 * (w + 1)

            def rows(s):
                h, i = s // NT, s % NT
                k0, nk = key_tiles(kind, i)
                if i == 0:
                    if kind == "A":
                        dve.wait_ge(s_bias, 2 * w + h + 1)
                    else:
                        dve.wait_ge(s_ck[h], 16 * (w - PAIRS_A + 1))
                value = c0 + (plan.chunk_end[s - 2] if s >= 2 else 0)
                if not (is_int(value) and value <= 0):
                    dve.wait_ge(s_tr, value)
                b0 = EXT - P * nk if kind == "A" else 0
                for n, (j0, nj) in enumerate(plan.steps[s]):
                    c = plan.chunk0(s) + n
                    last = n == len(plan.steps[s]) - 1
                    dve.wait_ge(s_scores, c0 + c + 1)
                    init = 3e38
                    if n == 1:
                        dve.wait_ge(s_sdone, c0 + c)
                        init = nmpart[:]
                    ins = nc.vector.tensor_tensor_reduce(
                        out=L[:, s % 2, P * j0:P * (j0 + nj)], in0=S[c % 3][:, 0:P * nj],
                        in1=BIAS[:, h, b0 + P * j0:b0 + P * (j0 + nj)], scale=1.0, scalar=init,
                        op0=ALU.add, op1=ALU.min,
                        accum_out=negm[:, s % 4, 0:1] if last else nmpart[:])
                    ins.then_inc(s_sdone, 1)

            def split(groups):
                for g in groups:
                    dve.wait_ge(s_jhi, g0 + g + 1)
                    if g < 4:
                        dve_qk(g, np_)
                    else:
                        dve_vg(g, g - 4, V0[np_], SG0[np_])

            for slot in range(plan.slots + 1):
                if attn and slot < 16:
                    rows(slot)
                if attn and slot >= 3:
                    s = slot - 3
                    h, i = s // NT, s % NT
                    if s == 0 and not (is_int(w) and w == 0):
                        dve.wait_ge(s_yst, 16 * NT * w)
                    dve.wait_ge(s_rinv, st0 + s + 1)
                    dve.wait_ge(s_pv, c0 + plan.chunk_end[s])
                    nc.vector.tensor_reduce(ysum[:, 0:HD], PV[:, 0:P].rearrange("p (x d) -> p d x", x=2),
                                            mybir.AxisListType.X, ALU.add).then_inc(s_ysum, 1)
                    dve.wait_ge(s_ysum, st0 + s + 1)
                    nc.vector.scalar_tensor_tensor(Y[:, i, HD * h:HD * h + HD], ysum[:, 0:HD],
                                                   rinv[:, s % 4, 0:1],
                                                   SG0[par][:, i, HD * h:HD * h + HD],
                                                   ALU.mult, ALU.mult).then_inc(s_y, 1)
                if proj and slot >= 1:
                    split(plan.ends[2 * slot - 1])
                if proj and slot < plan.slots:
                    split(plan.ends[2 * slot])
                if attn and 1 <= slot <= 16:
                    s = slot - 1
                    dve.wait_ge(s_probs, st0 + s + 1)
                    nc.vector.reciprocal(rinv[:, s % 4, 0:1], rs[:, s % 4, 0:1]).then_inc(s_rinv, 1)
                    for n, (j0, nj) in enumerate(plan.steps[s]):
                        c = plan.chunk0(s) + n
                        dve.wait_ge(s_hi, c0 + c + 1)
                        nc.vector.tensor_tensor(PT[c % 2][:, LO, 0:P * nj], T[c % 2][:, 0:P * nj],
                                                PT[c % 2][:, HI, 0:P * nj].bitcast(F32),
                                                ALU.subtract).then_inc(s_lo, 1)

        def dve_qk(g, np_):
            which, half = g // 2, g % 2
            for h in range(2):
                own = slice(HD * h, HD * h + HD)
                other = slice(HD - HD * h, P - HD * h)
                tok = slice(HALF * half, HALF * half + HALF)
                if which == 0:
                    ins = nc.vector.scalar_tensor_tensor(QZ0[np_][other, h, tok], J[g % 2][own, :], -0.125,
                                                         QZ0[np_][own, h, tok].bitcast(F32),
                                                         ALU.mult, ALU.subtract)
                else:
                    ins = nc.vector.tensor_tensor(KX0[np_][own, LO, h, tok], J[g % 2][own, :],
                                                  KX0[np_][own, HI, h, tok].bitcast(F32), ALU.subtract)
            ins.then_inc(s_j, 1)

        def dve_vg(g, t, V, SG):
            nc.vector.scalar_tensor_tensor(V[:, t, LO, :], J[g % 2][:, 0:P], 0.5,
                                           V[:, t, HI, :].bitcast(F32), ALU.mult, ALU.subtract)
            nc.vector.scalar_tensor_tensor(SG[:, t, :], SG[:, t, :], 1.0, J[g % 2][:, P:2 * P],
                                           ALU.add, ALU.mult).then_inc(s_j, 1)

        sp = nc.sync
        pool = nc.gpsimd

        def sp_dup(w):
            b = w % 2
            sp.wait_ge(s_j, 12 * w + 4)
            sp.dma_start(KX0[b][HD:P, :, 0, :].bitcast(F32), KX0[b][0:HD, :, 0, :].bitcast(F32)).then_inc(s_kdup, 16)
            sp.dma_start(KX0[b][0:HD, :, 1, :].bitcast(F32), KX0[b][HD:P, :, 1, :].bitcast(F32)).then_inc(s_kdup, 16)

        def sp_bias(hh):
            if hh < 2 * PAIRS_A:
                if hh >= 1:
                    sp.wait_ge(s_bias, hh)
                sp.dma_start(HK[:], bass.AP(ext_dram.tensor, EXT * hh + 129, [[1, P], [1, 384]]))\
                    .then_inc(s_hk, 16)
            else:
                sp.wait_ge(s_sdone, CH_AB // 2 * (hh - 1))
                sp.dma_start(BIAS[:, hh % 2, :], bass.AP(cum_dram.tensor, SEQ * (hh - 2 * PAIRS_A),
                                                         [[0, P], [1, SEQ]])).then_inc(s_ck[hh % 2], 16)

        def sp_window_ab(w):
            n = 2 * (w + 2)
            if n < 2 * PAIRS:
                load_w(sp, n, blocks_of(n))
            if w + 1 < PAIRS:
                sp_dup(w + 1)
                sp_bias(2 * w + 2)
            else:
                for m in range(4):
                    load_wo(m, w_out_0, 0)
            for i in range(NT):
                sp.wait_ge(s_y, 16 * w + NT + i + 1)
                sp.dma_start(y_dram[0, P * i:P * i + P, P * w:P * w + P], Y[:, i, :]).then_inc(s_yst, 16)
            if w + 1 < PAIRS:
                sp_bias(2 * w + 3)
            if n < 2 * PAIRS:
                load_w(sp, n + 1, blocks_of(n + 1))

        def load_wo(n, w_out, layer):
            if n == 0:
                sp.wait_ge(s_w, 2 * PAIRS if layer == 0 else 3 * PAIRS + 1)
            else:
                sp.wait_ge(s_wo, 4 * layer + n)
            sp.dma_start(rawo, w_out[2 * P * n:2 * P * n + 2 * P, :].rearrange("(k p) n -> p k n", p=P))\
                .then_inc(s_raw, 16)

        def split_wo(n, Wo, layer):
            pool.wait_ge(s_raw, raw_count(2 * PAIRS - 1 if layer == 0 else 3 * PAIRS) + 16 * (n + 1))
            nc.gpsimd.tensor_copy(Wo[:, HI, 2 * n:2 * n + 2, :], rawo).then_inc(s_woh, 1)
            pool.wait_ge(s_woh, 4 * layer + n + 1)
            nc.gpsimd.tensor_tensor(Wo[:, LO, 2 * n:2 * n + 2, :], rawo,
                                    Wo[:, HI, 2 * n:2 * n + 2, :].bitcast(F32), ALU.subtract)\
                .then_inc(s_wo, 1)

        def pool_bias(hh):
            h = hh % 2
            if hh >= 2:
                pool.wait_ge(s_sdone, CH_AB // 2 * (hh - 1))
            nc.gpsimd.memset(BIAS[:, h, 0:2 * P], 0.0).then_inc(s_biasp, 1)
            pool.wait_ge(s_hk, 16 * (hh + 1))
            nc.gpsimd.tensor_scalar(BIAS[:, h, 2 * P:EXT], HK[:, ::-1], -1.0, None, ALU.mult)
            pool.wait_ge(s_biasp, 3 * hh + 1)
            nc.gpsimd.tensor_scalar(BIAS[:, h, 0:2 * P], BIAS[:, h, 0:2 * P], relc[:, hh:hh + 1], None,
                                    ALU.subtract).then_inc(s_biasp, 1)
            pool.wait_ge(s_biasp, 3 * hh + 2)
            nc.gpsimd.memset(BIAS[HD:P, h, 0:HD], BIG).then_inc(s_biasp, 1)
            pool.wait_ge(s_biasp, 3 * hh + 3)
            nc.gpsimd.memset(BIAS[0:HD, h, EXT - HD:EXT], BIG).then_inc(s_bias, 1)
            pool.wait_ge(s_bias, hh + 1)

        with nc.Block() as block:
            @block.tensor
            def _(_pe):
                pe_window_ab("A", -1, 1, False, True)
                for w in range(PAIRS):
                    kind = "A" if w < PAIRS_A else "B"
                    pe_window_ab(kind, w, w % 2, True, w + 1 < PAIRS)

            @block.scalar
            def _(_act):
                act_window_ab("A", -1, 1, False, True)
                for w in range(PAIRS):
                    kind = "A" if w < PAIRS_A else "B"
                    act_window_ab(kind, w, w % 2, True, w + 1 < PAIRS)

            @block.vector
            def _(_dve):
                nc.vector.tensor_scalar(nsink[:], sinkc[:], -1.0, None, ALU.mult)
                dve_window_ab("A", -1, 1, False, True)
                for w in range(PAIRS):
                    kind = "A" if w < PAIRS_A else "B"
                    dve_window_ab(kind, w, w % 2, True, w + 1 < PAIRS)

            @block.sync
            def _(_sp):
                sp_bias(0)
                sp_bias(1)
                load_w(sp, 2, blocks_of(2))
                sp_dup(0)
                load_w(sp, 3, blocks_of(3))
                for w in range(PAIRS):
                    sp_window_ab(w)
                sp.wait_ge(s_yst, 16 * NT * PAIRS)

            @block.gpsimd
            def _(_pool):
                pool_bias(0)
                pool_bias(1)
                split_w(pool, 2, 4)
                split_w(pool, 3, 12)
                for w in range(PAIRS - 1):
                    n = 2 * (w + 2)
                    if w + 1 < PAIRS_A:
                        pool_bias(2 * w + 2)
                    if n < 2 * PAIRS:
                        split_w(pool, n, 12 * (w + 1) + 4)
                    if w + 1 < PAIRS_A:
                        pool_bias(2 * w + 3)
                    if n < 2 * PAIRS:
                        split_w(pool, n + 1, 12 * (w + 1) + 12)
                pool.wait_ge(s_proj, GRP1)
                for n in range(4):
                    split_wo(n, Wo0, 0)

        def out_phase(layer, Wo, w_norm, residual):
            b16, b8 = 16 * layer, 8 * layer
            last = layer == 1

            with nc.Block() as block:
                @block.tensor
                def _(_pe):
                    def y_transposes(i):
                        pe.wait_ge(s_yt[i % 2], 16 * (4 * layer + i // 2 + 1))
                        for c in range(2):
                            if i >= 1:
                                pe.wait_ge(s_ytlo, b16 + 2 * i - 1 + c)
                            for k in range(4):
                                mm = nc.tensor.transpose(T[c][:, P * k:P * k + P],
                                                         YT[:, i % 2, P * (4 * c + k):P * (4 * c + k) + P],
                                                         ident[:])
                            mm.then_inc(s_ytr, 1)

                    def product(i, c):
                        if c == 0:
                            pe.wait_ge(s_ytlo, b16 + 2 * i + 2)
                        if i == 0:
                            pe.wait_ge(s_wo, 4 * layer + 4)
                        else:
                            pe.wait_ge(s_jo, b16 + 2 * i - 1 + c)
                        for k in range(NK):
                            for n, (a, b) in enumerate(TERMS):
                                mm = nc.tensor.matmul(J[c][:], yT[i % 2][:, a, k, :],
                                                      Wo[:, b, k, HALF * c:HALF * c + HALF],
                                                      start=(k == 0 and n == 0),
                                                      stop=(k == NK - 1 and n == 2))
                        mm.then_inc(s_mm, 1)

                    def h_transposes(i):
                        pe.wait_ge(s_hn, 8 + i + 1)
                        for c in range(2):
                            if i >= 1:
                                pe.wait_ge(s_htlo, 16 + 2 * i - 1 + c)
                            for k in range(4):
                                mm = nc.tensor.transpose(S[c][:, P * k:P * k + P],
                                                         HN1[:, i % 2, P * (4 * c + k):P * (4 * c + k) + P],
                                                         ident[:])
                            mm.then_inc(s_ht, 1)

                    for j in range(NT + 2):
                        if j < NT:
                            y_transposes(j)
                        if 1 <= j <= NT:
                            product(j - 1, 0)
                            product(j - 1, 1)
                        if j >= 2 and not last:
                            h_transposes(j - 2)

                @block.scalar
                def _(_act):
                    act.dma_start(GB1[:], bass.AP(w_norm.tensor, w_norm.offset, [[0, P], [1, DM]]))\
                        .then_inc(s_gb, 16)
                    for j in range(NT + 2):
                        if j < NT:
                            if j >= 2:
                                act.wait_ge(s_mm, b16 + 2 * j - 2)
                            for c in range(2):
                                act.wait_ge(s_ytr, b16 + 2 * j + c + 1)
                                nc.scalar.activation(yT[j % 2][:, HI, 4 * c:4 * c + 4, :],
                                                     T[c][:].rearrange("p (k t) -> p k t", k=4),
                                                     ACT.Copy).then_inc(s_ythi, 1)
                        if j >= 2 and not last:
                            i = j - 2
                            for c in range(2):
                                act.wait_ge(s_ht, 16 + 2 * i + c + 1)
                                nc.scalar.activation(hT1[:, HI, 4 * c:4 * c + 4, P * i:P * i + P],
                                                     S[c][:].rearrange("p (k t) -> p k t", k=4),
                                                     ACT.Copy).then_inc(s_hthi, 1)
                        if 1 <= j <= NT:
                            i = j - 1
                            act.wait_ge(s_jo, b16 + 2 * i + 2)
                            if not last:
                                act.dma_start(x1_dram[P * i:P * i + P, :], X1[:, i % 2, :])\
                                    .then_inc(s_st[i % 2], 16)
                            if i >= 2 and last:
                                act.wait_ge(s_ot[i % 2], 16 * (i // 2))
                            nc.scalar.activation(HN1[:, i % 2, :], X1[:, i % 2, :], ACT.Square,
                                                 accum_out=ss[:, i:i + 1]).then_inc(s_square, 1)
                            act.wait_ge(s_var, b8 + i + 2)
                            nc.scalar.activation(sd[:, i:i + 1], var[:, i:i + 1], ACT.Sqrt)\
                                .then_inc(s_sqrt, 1)

                @block.vector
                def _(_dve):
                    dve.wait_ge(s_gb, 16 * (layer + 1))
                    for j in range(NT + 2):
                        if j < NT:
                            for c in range(2):
                                dve.wait_ge(s_ythi, b16 + 2 * j + c + 1)
                                nc.vector.tensor_tensor(yT[j % 2][:, LO, 4 * c:4 * c + 4, :],
                                                        T[c][:].rearrange("p (k t) -> p k t", k=4),
                                                        yT[j % 2][:, HI, 4 * c:4 * c + 4, :].bitcast(F32),
                                                        ALU.subtract).then_inc(s_ytlo, 1)
                        if j >= 2 and not last:
                            i = j - 2
                            for c in range(2):
                                dve.wait_ge(s_hthi, 16 + 2 * i + c + 1)
                                nc.vector.tensor_tensor(hT1[:, LO, 4 * c:4 * c + 4, P * i:P * i + P],
                                                        S[c][:].rearrange("p (k t) -> p k t", k=4),
                                                        hT1[:, HI, 4 * c:4 * c + 4, P * i:P * i + P]
                                                        .bitcast(F32), ALU.subtract).then_inc(s_htlo, 1)
                        if 1 <= j <= NT:
                            i = j - 1
                            dve.wait_ge(s_xr[i % 2], 16 * (4 * layer + i // 2 + 1))
                            if i >= 2 and not last:
                                dve.wait_ge(s_st[i % 2], 16 * (i // 2))
                            for c in range(2):
                                dve.wait_ge(s_mm, b16 + 2 * i + c + 1)
                                nc.vector.tensor_tensor(X1[:, i % 2, HALF * c:HALF * c + HALF], J[c][:],
                                                        XR[:, i % 2, HALF * c:HALF * c + HALF],
                                                        ALU.add).then_inc(s_jo, 1)
                            dve.wait_ge(s_square, 8 + b8 + i + 1)
                            nc.vector.tensor_scalar(var[:, i:i + 1], ss[:, i:i + 1], 1.0 / DM, EPS,
                                                    ALU.mult, ALU.add).then_inc(s_var, 1)
                            dve.wait_ge(s_sqrt, b8 + i + 2)
                            rsqrt_chain(slice(i, i + 1), 1 + b8 + i)
                            if i >= 2 and not last:
                                dve.wait_ge(s_ht, 16 + 2 * i - 2)
                            nc.vector.scalar_tensor_tensor(HN1[:, i % 2, :], X1[:, i % 2, :],
                                                           rstd[:, i:i + 1], GB1[:], ALU.mult,
                                                           ALU.mult).then_inc(s_hn, 1)

                @block.sync
                def _(_sp):
                    def loads(i):
                        if i >= 2:
                            sp.wait_ge(s_ytr, b16 + 2 * i - 2)
                        sp.dma_start(YT[:, i % 2, :], y_dram[layer, P * i:P * i + P, :])\
                            .then_inc(s_yt[i % 2], 16)
                        if i >= 2:
                            sp.wait_ge(s_jo, b16 + 2 * i - 2)
                        sp.dma_start(XR[:, i % 2, :], residual[P * i:P * i + P, :])\
                            .then_inc(s_xr[i % 2], 16)

                    loads(0)
                    loads(1)
                    if not last:
                        load_w(sp, BLK1, blocks_of(BLK1))
                    for i in range(2, NT):
                        loads(i)
                    for b in range(2):
                        sp.wait_ge(s_ot[b] if last else s_st[b], 16 * 4)

                @block.gpsimd
                def _(_pool):
                    if not last:
                        split_w(pool, BLK1, GRP1)
                    for i in range(NT if last else 0):
                        pool.wait_ge(s_hn, 16 + i + 1)
                        pool.dma_start(out[P * i:P * i + P, :], HN1[:, i % 2, :]).then_inc(s_ot[i % 2], 16)

        PLANC = PLAN["C"]

        def rotated(slot):
            return (PLANC.ends[2 * slot - 1] if slot >= 1 else []) + PLANC.ends[2 * slot]

        def t_uses(attn, proj):
            uses = []
            for slot in range(PLANC.slots):
                if attn and 1 <= slot <= NT:
                    uses.append(("a", slot - 1))
                if proj:
                    uses += [("q", t) for t in rotated(slot)]
            return uses

        def t_base(w):
            return TR1 + {-2: 0, -1: NT}.get(w, 2 * NT + 2 * NT * w) if is_int(w) \
                else TR1 + 2 * NT + 2 * NT * w

        def pe_window_c(w, par, kv, attn, proj):
            v = w + 2
            g0 = GRP1 + NT * v
            tb, uses = t_base(w), t_uses(attn, proj)
            c0, st0 = CH1 + NT * w, ST1 + NT * w

            def bank_free(use):
                ring_wait(pe, s_lo, use, 2, tb)

            def scores(s):
                nk = min(s + 1, 2)
                k0 = s + 1 - nk
                if s == 0:
                    pe.wait_ge(s_kdup, 32 * PAIRS + 32)
                    pe.wait_ge(s_lo, tb)
                ring_wait(pe, s_sdone, s, 2, c0)
                for h in range(2):
                    for hl in range(2):
                        mm = nc.tensor.matmul(S[s % 2][:, 2 * P * h:2 * P * h + P * nk],
                                              QZ1[par][:, h, P * s:P * s + P],
                                              KX1[:, hl, kv, P * k0:P * (k0 + nk)],
                                              start=(hl == HI), stop=(hl == LO))
                mm.then_inc(s_scores, 1)

            def transposes(s):
                nk = min(s + 1, 2)
                use = uses.index(("a", s))
                pe.wait_ge(s_probs, st0 + s + 1)
                bank_free(use)
                for h in range(2):
                    for b in range(nk):
                        o = P * (nk * h + b)
                        mm = nc.tensor.transpose(T[use % 2][:, o:o + P],
                                                 L[:, s % 2, 2 * P * h + P * b:2 * P * h + P * b + P],
                                                 ident[:])
                mm.then_inc(s_tr, 1)

            def q_transpose(t):
                use = uses.index(("q", t))
                pe.wait_ge(s_rope, NT * v + t + 1)
                bank_free(use)
                nc.tensor.transpose(T[use % 2][:, 0:P], QR[:, t % 2, :], ident[:]).then_inc(s_tr, 1)

            def times_v(s):
                nk = min(s + 1, 2)
                k0 = s + 1 - nk
                ring_wait(pe, s_y, s, 1, st0)
                pe.wait_ge(s_lo, tb + uses.index(("a", s)) + 1)
                for h in range(2):
                    for b in range(nk):
                        for pa in range(2):
                            mm = nc.tensor.matmul(PV[:, P * h:P * h + P],
                                                  PT[s % 2][:, pa, P * (nk * h + b):P * (nk * h + b) + P],
                                                  V1[:, k0 + b, :, HD * kv:HD * kv + HD],
                                                  start=(b == 0 and pa == HI),
                                                  stop=(b == nk - 1 and pa == LO))
                mm.then_inc(s_pv, 1)

            if proj:
                pe.wait_ge(s_w, BLK1 + v + 1)
            wpar = (BLK1 + w + 2) % 2 if is_int(w) else par
            for slot in range(PLANC.slots):
                if attn and slot < NT:
                    scores(slot)
                if proj:
                    pe_project(g0, *PLANC.parts[2 * slot], 1, wpar)
                if attn and 1 <= slot <= NT:
                    transposes(slot - 1)
                if proj:
                    pe_project(g0, *PLANC.parts[2 * slot + 1], 1, wpar)
                if attn and slot >= 2:
                    times_v(slot - 2)
                if proj:
                    for t in rotated(slot):
                        q_transpose(t)

        def act_window_c(w, par, attn, proj):
            v = w + 2
            g0 = GRP1 + NT * v
            tb, uses = t_base(w), t_uses(attn, proj)
            c0, st0 = CH1 + NT * w, ST1 + NT * w
            np_ = 1 - par
            kvset = is_int(w) and w == -2
            def split(tiles):
                for t in tiles:
                    act.wait_ge(s_proj, g0 + t + 1)
                    if kvset:
                        nc.scalar.activation(V1[:, t, HI, :], J[t % 2][:, P:2 * P], ACT.Copy, scale=0.5)\
                            .then_inc(s_jhi, 1)
                    else:
                        nc.scalar.activation(SG1[np_][:, t, :], J[t % 2][:, P:2 * P], ACT.Tanh, scale=0.5)\
                            .then_inc(s_jhi, 1)

            for slot in range(PLANC.slots + 1):
                if proj and slot >= 1:
                    split(PLANC.ends[2 * slot - 1])
                if attn and slot < NT:
                    s, nk = slot, min(slot + 1, 2)
                    act.wait_ge(s_snm, st0 - ST1 + s + 1)
                    for h in range(2):
                        r = L[:, s % 2, 2 * P * h:2 * P * h + P * nk]
                        nc.scalar.activation(r, r, ACT.Exp, bias=negm[:, s % 4, h:h + 1], scale=-1.0,
                                             accum_out=rs[:, s % 4, h:h + 1])
                    nc.scalar.activation(es[:, s % 4, :], snm[:, s % 4, :], ACT.Exp).then_inc(s_probs, 1)
                if proj and slot >= 1:
                    for t in rotated(slot - 1):
                        use = uses.index(("q", t))
                        act.wait_ge(s_tr, tb + use + 1)
                        for h in range(2):
                            own = slice(HD * h, HD * h + HD)
                            if kvset:
                                ins = nc.scalar.activation(KX1[own, HI, h, P * t:P * t + P],
                                                           T[use % 2][own, 0:P], ACT.Copy)
                            else:
                                ins = nc.scalar.activation(QZ1[np_][own, h, P * t:P * t + P],
                                                           T[use % 2][own, 0:P], ACT.Copy, scale=-0.125)
                        ins.then_inc(s_hi, 1)
                if proj and slot < PLANC.slots:
                    split(PLANC.ends[2 * slot])
                if attn and 1 <= slot <= NT:
                    s, nk = slot - 1, min(slot, 2)
                    use = uses.index(("a", s))
                    act.wait_ge(s_tr, tb + use + 1)
                    ring_wait(act, s_pv, s, 2, c0)
                    nc.scalar.activation(PT[s % 2][:, HI, 0:2 * P * nk], T[use % 2][:, 0:2 * P * nk],
                                         ACT.Copy).then_inc(s_hi, 1)

        def dve_window_c(w, par, attn, proj):
            v = w + 2
            g0 = GRP1 + NT * v
            tb, uses = t_base(w), t_uses(attn, proj)
            c0, st0 = CH1 + NT * w, ST1 + NT * w
            l0 = NT * w
            np_ = 1 - par
            kvset = is_int(w) and w == -2

            def rotate(t):
                heads = J[t % 2][:, 0:P].rearrange("p (h d) -> p h d", h=2)
                halves = J[t % 2][:, 0:P].rearrange("p (h s d) -> p h s d", h=2, s=2)
                cos = ROPE[:, t, 0, :].rearrange("p (o d) -> p o d", o=1).broadcast_to((P, 2, HD))
                sin = ROPE[:, t, 1, :].rearrange("p (s d) -> p s d", s=2)
                q = QR[:, t % 2, :]
                if t >= 2:
                    dve.wait_ge(s_tr, tb + uses.index(("q", t - 2)) + 1)
                elif not kvset:
                    dve.wait_ge(s_tr, tb)
                nc.vector.tensor_tensor(q.rearrange("p (h d) -> p h d", h=2), heads, cos, ALU.mult)
                for h in range(2):
                    ins = nc.vector.tensor_tensor(
                        QS[:, HD * h:HD * h + HD].rearrange("p (s d) -> p s d", s=2),
                        halves[:, h, ::-1, :], sin, ALU.mult)
                ins.then_inc(s_qr, 1)
                dve.wait_ge(s_qr, NT * v + t + 1)
                nc.vector.tensor_tensor(q, q, QS, ALU.add).then_inc(s_rope, 1)
                dve.wait_ge(s_rope, NT * v + t + 1)

            def split(tiles):
                for t in tiles:
                    dve.wait_ge(s_jhi, g0 + t + 1)
                    rotate(t)
                    if kvset:
                        nc.vector.scalar_tensor_tensor(V1[:, t, LO, :], J[t % 2][:, P:2 * P], 0.5,
                                                       V1[:, t, HI, :].bitcast(F32),
                                                       ALU.mult, ALU.subtract).then_inc(s_j, 1)
                    else:
                        nc.vector.scalar_tensor_tensor(SG1[np_][:, t, :], SG1[np_][:, t, :], 1.0,
                                                       J[t % 2][:, P:2 * P], ALU.add, ALU.mult)\
                            .then_inc(s_j, 1)

            for slot in range(PLANC.slots + 1):
                if attn and slot < NT:
                    s, nk = slot, min(slot + 1, 2)
                    dve.wait_ge(s_tr, tb + (uses.index(("a", s - 2)) + 1 if s >= 2 else 0))
                    dve.wait_ge(s_scores, c0 + s + 1)
                    for h in range(2):
                        ins = nc.vector.tensor_tensor_reduce(
                            out=L[:, s % 2, 2 * P * h:2 * P * h + P * nk],
                            in0=S[s % 2][:, 2 * P * h:2 * P * h + P * nk],
                            in1=WM[:, 2 * P - P * nk:2 * P], scale=1.0,
                            scalar=nsink[:, 2 * w + h:2 * w + h + 1], op0=ALU.add, op1=ALU.min,
                            accum_out=negm[:, s % 4, h:h + 1])
                    ins.then_inc(s_sdone, 1)
                    dve.wait_ge(s_sdone, c0 + s + 1)
                    nc.vector.tensor_tensor(snm[:, s % 4, :], negm[:, s % 4, :], sinkc[:, 2 * w:2 * w + 2],
                                            ALU.add).then_inc(s_snm, 1)
                if attn and slot >= 3:
                    s = slot - 3
                    if s == 0 and not (is_int(w) and w == 0):
                        dve.wait_ge(s_yst, 16 * NT * (PAIRS + w))
                    dve.wait_ge(s_rinv, ST1 + l0 + s + 1)
                    dve.wait_ge(s_pv, c0 + s + 1)
                    nc.vector.tensor_reduce(ysum[:].rearrange("p (h d) -> p h d", h=2),
                                            PV[:, 0:2 * P].rearrange("p (h x d) -> p h d x", h=2, x=2),
                                            mybir.AxisListType.X, ALU.add).then_inc(s_ysum, 1)
                    dve.wait_ge(s_ysum, st0 + s + 1)
                    for h in range(2):
                        ins = nc.vector.scalar_tensor_tensor(Y[:, s, HD * h:HD * h + HD],
                                                             ysum[:, HD * h:HD * h + HD],
                                                             rinv[:, s % 4, h:h + 1],
                                                             SG1[par][:, s, HD * h:HD * h + HD],
                                                             ALU.mult, ALU.mult)
                    ins.then_inc(s_y, 1)
                if proj and slot >= 1:
                    for t in rotated(slot - 1):
                        use = uses.index(("q", t))
                        dve.wait_ge(s_hi, tb + use + 1)
                        for h in range(2):
                            own = slice(HD * h, HD * h + HD)
                            other = slice(HD - HD * h, P - HD * h)
                            tok = slice(P * t, P * t + P)
                            if kvset:
                                ins = nc.vector.tensor_tensor(KX1[own, LO, h, tok], T[use % 2][own, 0:P],
                                                              KX1[own, HI, h, tok].bitcast(F32), ALU.subtract)
                            else:
                                ins = nc.vector.scalar_tensor_tensor(
                                    QZ1[np_][other, h, tok], T[use % 2][own, 0:P], -0.125,
                                    QZ1[np_][own, h, tok].bitcast(F32), ALU.mult, ALU.subtract)
                        ins.then_inc(s_lo, 1)
                if proj and slot >= 1:
                    split(PLANC.ends[2 * slot - 1])
                if proj and slot < PLANC.slots:
                    split(PLANC.ends[2 * slot])
                if attn and 1 <= slot <= NT:
                    s, nk = slot - 1, min(slot, 2)
                    use = uses.index(("a", s))
                    dve.wait_ge(s_probs, st0 + s + 1)
                    nc.vector.tensor_tensor(rinv[:, s % 4, :], rs[:, s % 4, :], es[:, s % 4, :], ALU.add)\
                        .then_inc(s_tot, 1)
                    dve.wait_ge(s_hi, tb + use + 1)
                    nc.vector.tensor_tensor(PT[s % 2][:, LO, 0:2 * P * nk], T[use % 2][:, 0:2 * P * nk],
                                            PT[s % 2][:, HI, 0:2 * P * nk].bitcast(F32),
                                            ALU.subtract).then_inc(s_lo, 1)
                    dve.wait_ge(s_tot, l0 + s + 1)
                    nc.vector.reciprocal(rinv[:, s % 4, :], rinv[:, s % 4, :]).then_inc(s_rinv, 1)

        out_phase(0, Wo0, norm_1, x)

        with nc.Block() as block:
            @block.tensor
            def _(_pe):
                for w in range(-2, PAIRS):
                    pe_window_c(w, w % 2, max(w, 0) // 4, w >= 0, w + 1 < PAIRS)

            @block.scalar
            def _(_act):
                act.dma_start(ROPE[:], c_rope.rearrange("(t p) c d -> p t c d", p=P)).then_inc(s_rope_c, 16)
                act.dma_start(WM, c_window).then_inc(s_rope_c, 16)
                for w in range(-2, PAIRS):
                    act_window_c(w, w % 2, w >= 0, w + 1 < PAIRS)

            @block.vector
            def _(_dve):
                dve.wait_ge(s_rope_c, 32)
                for w in range(-2, PAIRS):
                    dve_window_c(w, w % 2, w >= 0, w + 1 < PAIRS)

            @block.sync
            def _(_sp):
                load_w(sp, BLK1 + 1, blocks_of(BLK1 + 1))
                load_w(sp, BLK1 + 2, blocks_of(BLK1 + 2))
                sp.wait_ge(s_lo, TR1 + NT)
                sp.dma_start(KX1[HD:P, :, 0, :].bitcast(F32), KX1[0:HD, :, 0, :].bitcast(F32)).then_inc(s_kdup, 16)
                sp.dma_start(KX1[0:HD, :, 1, :].bitcast(F32), KX1[HD:P, :, 1, :].bitcast(F32)).then_inc(s_kdup, 16)
                for w in range(PAIRS):
                    if BLK1 + 3 + w <= BLK1 + PAIRS:
                        load_w(sp, BLK1 + 3 + w, blocks_of(BLK1 + 3 + w))
                    if w == PAIRS - 1:
                        for n in range(4):
                            load_wo(n, w_out_1, 1)
                    for i in range(NT):
                        sp.wait_ge(s_y, ST1 + NT * w + i + 1)
                        sp.dma_start(y_dram[1, P * i:P * i + P, P * w:P * w + P], Y[:, i, :])\
                            .then_inc(s_yst, 16)
                sp.wait_ge(s_yst, 2 * 16 * NT * PAIRS)

            @block.gpsimd
            def _(_pool):
                for v in range(1, PAIRS + 1):
                    split_w(pool, BLK1 + v, GRP1 + NT * (v - 1) if v >= 2 else None)
                pool.wait_ge(s_proj, GRP1 + NT * (PAIRS + 1))
                for n in range(4):
                    split_wo(n, Wo1, 1)

        out_phase(1, Wo1, norm_f, x1_dram)


_INS = ["x", "norm_0", "w_in_0", "rel_bias_0", "f_bias_0", "w_out_0", "norm_1", "w_in_1", "sinks_1",
        "w_out_1", "norm_f"]


def constants(np):
    causal = np.where(np.arange(P)[None, :] > np.arange(P)[:, None], BIG, 0.0).astype(np.float32)
    window = np.zeros((P, 2 * P), np.float32)
    window[:HD, :HD] = BIG
    window[:HD, 3 * HD:] = BIG
    window[HD:, :2 * HD] = BIG
    half = HD // 2
    inv = np.float32(10000.0) ** (-np.arange(half, dtype=np.float32) / np.float32(half))
    ang = np.arange(SEQ, dtype=np.float32)[:, None] * inv[None, :]
    cos, sin = np.cos(ang), np.sin(ang)
    rope = np.stack([np.concatenate([cos, cos], 1), np.concatenate([-sin, sin], 1)], 1).astype(np.float32)
    return {"c_ident": np.eye(P, dtype=np.float32), "c_causal": causal, "c_window": window, "c_rope": rope}


def kernel(**inputs):
    import numpy as _np
    import concourse.bacc as _bacc
    from concourse import mybir as _mybir
    from concourse.bass_utils import run_bass_kernel_spmd as _run

    nc = _bacc.Bacc("TRN2", target_bir_lowering=False, num_devices=1)
    arrays, args = {}, []
    given = [(name, _np.ascontiguousarray(inputs[name])) for name in _INS] + list(constants(_np).items())
    for name, a in given:
        arrays[f"in_{name}"] = a
        args.append(nc.dram_tensor(f"in_{name}", a.shape, _mybir.dt.from_np(a.dtype), kind="ExternalInput").ap())
    out = nc.dram_tensor("out", (1, SEQ, DM), F32, kind="ExternalOutput").ap()
    build_trunk(nc, *args, out)
    r = _run(nc, [arrays], core_ids=[0])
    return r.results[0]["out"]
```

```python
from contextlib import ExitStack

import concourse.bass as bass
from concourse import mybir

F32 = mybir.dt.float32
F32R = mybir.dt.float32r
ALU = mybir.AluOpType
ACT = mybir.ActivationFunctionType

P = 128
HD = 64
SEQ = 1024
DM = 1024
NT = SEQ // P
NK = DM // P
HALF = SEQ // 2
HEADS = 16
PAIRS = HEADS // 2
PAIRS_A = 4
CLIP = 256
EXT = 640
BIG = 1e30
EPS = 1e-6
W_A = 512
GATE0 = 3 * W_A + 3 * W_A + 8
F_COL = 3 * W_A + 3 * W_A
KC, VC, GATE1 = 1024, 1152, 1280

HI, LO = 0, 1
TERMS = ((HI, HI), (HI, LO), (LO, HI))


def key_tiles(kind, i):
    n = min(i + 1, {"A": 5, "B": NT, "C": 2}[kind])
    return i + 1 - n, n


def key_chunks(n):
    return [(0, n)] if n <= 4 else [(0, (n + 1) // 2), ((n + 1) // 2, n // 2)]


STEPS = {kind: [key_chunks(key_tiles(kind, s % NT)[1]) for s in range(2 * NT)] for kind in "AB"}
CHUNKS = sum(len(c) for c in STEPS["A"])
assert CHUNKS == sum(len(c) for c in STEPS["B"]) and CHUNKS % 6 == 0


def chunk0(kind, s):
    return sum(len(c) for c in STEPS[kind][:s])


def column_pair(n):
    return n // 2 + 4 * (n % 2)


def ended_group(slot):
    if slot in (2, 4, 6, 8):
        return slot // 2 - 1
    return 4 + slot - 9 if slot >= 9 else None


def build_trunk(nc, x, norm_0, w_in_0, rel_bias_0, f_bias_0, w_out_0, norm_1, w_in_1, sinks_1,
                w_out_1, norm_f, c_ident, c_causal, c_window, c_rope, out):
    x = x[0]
    out = out[0]
    ext_dram = nc.dram_tensor("ext_bias", (8, EXT), F32, kind="Internal").ap()
    cum_dram = nc.dram_tensor("cum_forget", (8, SEQ), F32, kind="Internal").ap()
    y_dram = nc.dram_tensor("y_gated", (2, SEQ, DM), F32, kind="Internal").ap()
    x1_dram = nc.dram_tensor("x_mid", (SEQ, DM), F32, kind="Internal").ap()

    ctx = ExitStack()
    with ctx:
        def sem(name):
            return ctx.enter_context(nc.semaphore(name))

        base = nc.sbuf_base
        base += (-base) % 64
        top = [base]

        def at(name, shape, dt, offset):
            return nc.alloc_sbuf_tensor_at(name, shape, dt, offset=offset)

        def put(name, shape, dt=F32):
            size = 4
            for s in shape[1:]:
                size *= s
            t = at(name, shape, dt, top[0])
            top[0] += size + (-size) % 32
            return t

        R0 = top[0]
        hT0 = at("hT0", [P, 2, NK, SEQ], F32R, R0)
        Wo0 = at("Wo0", [P, 2, NK, DM], F32R, R0)
        QZ1 = [at(f"QZ1_{b}", [P, 2, SEQ], F32R, R0 + 8192 * b) for b in range(2)]
        KX1 = at("KX1", [P, 2, 2, SEQ], F32R, R0 + 16384)
        V1 = at("V1", [P, NT, 2, P], F32R, R0 + 32768)
        SG1 = [at(f"SG1_{b}", [P, NT, P], F32, R0 + 40960 + 4096 * b) for b in range(2)]
        ROPE = at("ROPE", [P, NT, 2, HD], F32, R0 + 49152)
        R1 = R0 + 65536
        xt0 = at("xt0", [P, NT, DM], F32, R1)
        QZ0 = [at(f"QZ0_{b}", [P, 2, SEQ], F32R, R1 + 8192 * b) for b in range(2)]
        KX0 = [at(f"KX0_{b}", [P, 2, 2, SEQ], F32R, R1 + 16384 + 16384 * b) for b in range(2)]
        V0 = [at(f"V0_{b}", [P, NT, 2, P], F32R, R1 + 49152 + 8192 * b) for b in range(2)]
        SG0 = [at(f"SG0_{b}", [P, NT, P], F32, R1 + 65536 + 4096 * b) for b in range(2)]
        hT1 = at("hT1", [P, 2, NK, SEQ], F32R, R1)
        Wo1 = at("Wo1", [P, 2, NK, DM], F32R, R1)
        R2 = R1 + 73728
        Wslot = [at(f"W_{b}", [P, 2, NK, 2 * P], F32R, R2 + 16384 * b) for b in range(2)]
        WoRaw = at("WoRaw", [P, NK, DM], F32, R2)
        yT = [at(f"yT_{b}", [P, 2, NK, P], F32R, R2 + 16384 + 8192 * b) for b in range(2)]
        XR = at("XR", [P, 2, DM], F32, R1 + 65536)
        R3 = R2 + 32768
        raw = at("raw", [P, NK, 2 * P], F32, R3)
        R4 = R3 + 8192
        L = at("L", [P, 2, SEQ], F32, R4)
        YT = at("YT", [P, 2, DM], F32, R4)
        junk = at("junk", [P, DM], F32, R4)
        R5 = R4 + 8192
        PT = [at(f"PT_{b}", [P, 2, 512], F32R, R5 + 4096 * b) for b in range(2)]
        HN = at("HN", [P, 2, DM], F32, R5)
        X1 = at("X1", [P, 2, DM], F32, R5)
        R6 = R5 + 8192
        BIAS = at("BIAS", [P, 2, SEQ], F32, R6)
        GB = at("GB", [P, DM], F32, R6)
        HN1 = at("HN1", [P, 2, DM], F32, R6)
        fz = at("fz", [8, SEQ], F32, R4)
        fe = at("fe", [8, SEQ], F32, R4 + 4096)
        fa = at("fa", [8, SEQ], F32, R5)
        fl = at("fl", [8, SEQ], F32, R5 + 4096)
        Wf = at("Wf", [P, NK, 8], F32, R6 + 4096)
        WfR = at("WfR", [P, 2, NK, 8], F32R, R6 + 4096 + 512)
        extrow = at("extrow", [8, EXT], F32, R6 + 4096 + 1024)
        fb = at("fb", [8, 1], F32, R6 + 4096 + 1024 + 4 * EXT)
        R7 = R6 + 8192
        Y = at("Y", [P, NT, P], F32, R7)
        GB1 = at("GB1", [P, DM], F32, R7)
        top[0] = R7 + 4096
        ident = put("ident", [P, P])
        triR_at = top[0]
        triR = put("triR", [P, P], F32R)
        identR = put("identR", [P, P], F32R)
        HK = put("HK", [P, 384])
        QR = at("QR", [P, 2, P], F32, triR_at)
        QS = HK[:, 2 * P:3 * P]
        relc = put("relc", [P, 8])
        sinkc = put("sinkc", [P, HEADS])
        nsink = put("nsink", [P, 2, 2])
        stats_at = top[0]
        ysum = put("ysum", [P, P])
        negm = put("negm", [P, 4, 2])
        nmpart = put("nmpart", [P, 1])
        held = put("held", [1, 1])
        rs = put("rs", [P, 4, 2])
        rinv = put("rinv", [P, 4, 2])
        snm = put("snm", [P, 4, 2])
        es = put("es", [P, 4, 2])
        ss = at("ss", [P, NT], F32, stats_at + 0)
        var = at("var", [P, NT], F32, stats_at + 32)
        sd = at("sd", [P, NT], F32, stats_at + 64)
        r0 = at("r0", [P, NT], F32, stats_at + 96)
        nt1 = at("nt1", [P, NT], F32, stats_at + 128)
        nt2 = at("nt2", [P, NT], F32, stats_at + 160)
        rstd = at("rstd", [P, NT], F32, stats_at + 192)
        assert top[0] <= nc.sbuf_usable_end, (top[0], nc.sbuf_usable_end)
        WM = HK[:, 0:2 * P]
        trif = HK[:, 0:P]

        def bank(name):
            return ctx.enter_context(nc.psum_tensor(name, [P, 512], F32))

        S = [bank(f"S{i}") for i in range(3)]
        T = [bank(f"T{i}") for i in range(2)]
        J = [bank(f"J{i}") for i in range(2)]
        PV = bank("PV")

        s_x = [sem(f"x_loaded{i}") for i in range(NT)]
        s_const = sem("consts_loaded")
        s_small = sem("small_inputs_loaded")
        s_square = sem("squares_summed")
        s_var = sem("variances_ready")
        s_sqrt = sem("roots_ready")
        s_norm = sem("norm_chain")
        s_hn = sem("normed_rows_ready")
        s_ht = sem("normed_transposed")
        s_hthi = sem("hT_hi_written")
        s_htlo = sem("hT_lo_written")
        s_idr = sem("rounded_consts_ready")
        s_wf = sem("forget_weights_split")
        s_f = sem("forget_logits_ready")
        s_fa = sem("forget_chain_act")
        s_fd = sem("forget_chain_dve")
        s_cum = sem("cum_stored")
        s_extf = sem("ext_row_filled")
        s_ext = sem("ext_row_stored")
        s_raw = sem("raw_weights_loaded")
        s_wh = sem("weights_hi_written")
        s_w = sem("weights_split")
        s_gb = sem("norm_weights_loaded")
        s_jo = sem("residual_added")
        s_ytr = sem("y_transposed")
        s_ythi = sem("yT_hi_written")
        s_ytlo = sem("yT_lo_written")
        s_st = [sem(f"x1_tile_stored{b}") for b in range(2)]
        s_ot = [sem(f"out_tile_stored{b}") for b in range(2)]
        s_rope_c = sem("layer1_tables_loaded")
        s_hk = sem("hankel_loaded")
        s_biasp = sem("bias_chain")
        s_bias = sem("bias_built")
        s_ck = [sem(f"cum_row_broadcast{h}") for h in range(2)]
        s_proj = sem("projection_group_done")
        s_jhi = sem("projection_hi_written")
        s_j = sem("projection_evacuated")
        s_kdup = sem("k_duplicated")
        s_scores = sem("scores_ready")
        s_sdone = sem("rows_written")
        s_snm = sem("sink_shift_ready")
        s_probs = sem("probs_ready")
        s_tr = sem("transposed")
        s_hi = sem("transposed_hi_written")
        s_lo = sem("transposed_lo_written")
        s_pv = sem("pv_chunk_done")
        s_tot = sem("totals_ready")
        s_rinv = sem("reciprocals_ready")
        s_y = sem("y_written")
        s_ysum = sem("pv_halves_added")
        s_yst = [sem(f"y_tile_stored{i}") for i in range(NT)]
        s_qt = sem("rotated_transposed")
        s_qhi = sem("rotated_hi_written")
        s_qlo = sem("rotated_lo_written")
        s_nsk = sem("sinks_of_pair_ready")
        s_wor = [sem(f"raw_out_weights{i}") for i in range(4)]
        s_wohi = [sem(f"out_weights_hi{k}") for k in range(NK)]
        s_wolo = [sem(f"out_weights_lo{k}") for k in range(NK)]
        s_qr = sem("rope_products")
        s_rope = sem("rotated_ready")
        s_yt = [sem(f"y_tile_loaded{b}") for b in range(2)]
        s_xr = [sem(f"x_tile_loaded{b}") for b in range(2)]
        s_x1st = sem("x1_stored")
        s_mm = sem("out_projection_done")
        s_x1 = sem("x1_ready")

        def load_w(sp, n, blocks):
            if n >= 1:
                sp.wait_ge(s_w, n)
            for b, src in enumerate(blocks):
                sp.dma_start(raw[:, :, P * b:P * b + P], src).then_inc(s_raw, 16)

        def split_w(pool, n, need):
            pool.wait_ge(s_raw, 32 * (n + 1))
            if need is not None:
                pool.wait_ge(s_proj, need)
            nc.gpsimd.tensor_copy(Wslot[n % 2][:, HI], raw[:]).then_inc(s_wh, 1)
            pool.wait_ge(s_wh, n + 1)
            nc.gpsimd.tensor_tensor(Wslot[n % 2][:, LO], raw[:], Wslot[n % 2][:, HI].bitcast(F32),
                                    ALU.subtract).then_inc(s_w, 1)

        def cols(w, c):
            return w[:, c:c + P].rearrange("(k p) c -> p k c", p=P)

        def blocks_of(n):
            if n < 2 * PAIRS:
                p = column_pair(n // 2)
                o = P * p if p < PAIRS_A else 3 * W_A + P * (p - PAIRS_A)
                if n % 2 == 0:
                    return [cols(w_in_0, o), cols(w_in_0, o + W_A)]
                return [cols(w_in_0, o + 2 * W_A), cols(w_in_0, GATE0 + P * p)]
            if n == 2 * PAIRS:
                return [cols(w_in_1, KC), cols(w_in_1, VC)]
            p = column_pair(n - 2 * PAIRS - 1)
            return [cols(w_in_1, P * p), cols(w_in_1, GATE1 + P * p)]

        BLK1 = 2 * PAIRS
        GRP1 = 12 * PAIRS
        CH1 = CHUNKS * PAIRS
        ST1 = 2 * NT * PAIRS
        PER = NK * len(TERMS)
        BATCHES = 4

        def wait(eng, s, value):
            if not isinstance(value, int) or value > 0:
                eng.wait_ge(s, value)

        pe, act, dve, pool, sp = nc.tensor, nc.scalar, nc.vector, nc.gpsimd, nc.sync

        def rsqrt_chain(a, n):
            nc.vector.reciprocal(r0[:, a], sd[:, a]).then_inc(s_norm, 1)
            nc.vector.wait_ge(s_norm, 5 * n + 1)
            nc.vector.tensor_tensor(nt1[:, a], r0[:, a], r0[:, a], ALU.mult).then_inc(s_norm, 1)
            nc.vector.wait_ge(s_norm, 5 * n + 2)
            nc.vector.tensor_tensor(nt2[:, a], nt1[:, a], var[:, a], ALU.mult).then_inc(s_norm, 1)
            nc.vector.wait_ge(s_norm, 5 * n + 3)
            nc.vector.tensor_scalar(nt1[:, a], nt2[:, a], -0.5, 1.5, ALU.mult, ALU.add).then_inc(s_norm, 1)
            nc.vector.wait_ge(s_norm, 5 * n + 4)
            nc.vector.tensor_tensor(rstd[:, a], r0[:, a], nt1[:, a], ALU.mult).then_inc(s_norm, 1)
            nc.vector.wait_ge(s_norm, 5 * n + 5)

        def pe_group0(g, base, blocks, m0, m1):
            for m in range(m0, m1):
                k, (a, b) = m // len(TERMS), TERMS[m % len(TERMS)]
                if m == 0:
                    if g in (0, 4):
                        pe.wait_ge(s_w, blocks + g // 4)
                    wait(pe, s_j, base + g - 1)
                if g < 4:
                    which, half = g % 2, g // 2
                    mm = nc.tensor.matmul(J[g % 2][:], Wslot[0][:, a, k, P * which:P * which + P],
                                          hT0[:, b, k, HALF * half:HALF * half + HALF],
                                          start=(m == 0), stop=(m == PER - 1))
                else:
                    t = g - 4
                    mm = nc.tensor.matmul(J[g % 2][:, 0:2 * P], hT0[:, a, k, P * t:P * t + P],
                                          Wslot[1][:, b, k, :], start=(m == 0), stop=(m == PER - 1))
                if m == PER - 1:
                    mm.then_inc(s_proj, 1)

        def act_group0(g, base, b):
            act.wait_ge(s_proj, base + g + 1)
            if g < 4:
                which, half = g % 2, g // 2
                tok = slice(HALF * half, HALF * half + HALF)
                for h in range(2):
                    own = slice(HD * h, HD * h + HD)
                    if which == 0:
                        ins = nc.scalar.activation(QZ0[b][own, h, tok], J[g % 2][own, :], ACT.Copy,
                                                   scale=-0.125)
                    else:
                        ins = nc.scalar.activation(KX0[b][own, HI, h, tok], J[g % 2][own, :], ACT.Copy)
                ins.then_inc(s_jhi, 1)
            else:
                nc.scalar.activation(V0[b][:, g - 4, HI, :], J[g % 2][:, 0:P], ACT.Copy, scale=0.5)
                nc.scalar.activation(SG0[b][:, g - 4, :], J[g % 2][:, P:2 * P], ACT.Tanh, scale=0.5)\
                    .then_inc(s_jhi, 1)

        def dve_group0(g, base, b):
            dve.wait_ge(s_jhi, base + g + 1)
            if g < 4:
                which, half = g % 2, g // 2
                tok = slice(HALF * half, HALF * half + HALF)
                for h in range(2):
                    own = slice(HD * h, HD * h + HD)
                    other = slice(HD - HD * h, P - HD * h)
                    if which == 0:
                        ins = nc.vector.scalar_tensor_tensor(QZ0[b][other, h, tok], J[g % 2][own, :], -0.125,
                                                             QZ0[b][own, h, tok].bitcast(F32),
                                                             ALU.mult, ALU.subtract)
                    else:
                        ins = nc.vector.tensor_tensor(KX0[b][own, LO, h, tok], J[g % 2][own, :],
                                                      KX0[b][own, HI, h, tok].bitcast(F32), ALU.subtract)
                ins.then_inc(s_j, 1)
            else:
                t = g - 4
                nc.vector.scalar_tensor_tensor(V0[b][:, t, LO, :], J[g % 2][:, 0:P], 0.5,
                                               V0[b][:, t, HI, :].bitcast(F32), ALU.mult, ALU.subtract)
                nc.vector.scalar_tensor_tensor(SG0[b][:, t, :], SG0[b][:, t, :], 1.0, J[g % 2][:, P:2 * P],
                                               ALU.add, ALU.mult).then_inc(s_j, 1)

        def sp_dup0(n):
            b = n % 2
            sp.wait_ge(s_j, 12 * n + 4)
            sp.dma_start(KX0[b][HD:P, :, 0, :].bitcast(F32), KX0[b][0:HD, :, 0, :].bitcast(F32))\
                .then_inc(s_kdup, 16)
            sp.dma_start(KX0[b][0:HD, :, 1, :].bitcast(F32), KX0[b][HD:P, :, 1, :].bitcast(F32))\
                .then_inc(s_kdup, 16)

        def sp_bias(q):
            n, h = q // 2, q % 2
            if n % 2 == 0:
                wait(sp, s_bias, n + h)
                sp.dma_start(HK[:], bass.AP(ext_dram.tensor, EXT * (n + h) + CLIP + 1 - P,
                                            [[1, P], [1, 384]])).then_inc(s_hk, 16)
            else:
                wait(sp, s_sdone, CHUNKS // 2 * (q - 1))
                sp.dma_start(BIAS[:, h, :], bass.AP(cum_dram.tensor, SEQ * (n - 1 + h),
                                                    [[0, P], [1, SEQ]])).then_inc(s_ck[h], 16)

        def pool_bias(q):
            n, h = q // 2, q % 2
            a = n + h
            wait(pool, s_sdone, CHUNKS // 2 * (q - 1))
            nc.gpsimd.memset(BIAS[:, h, 0:2 * P], 0.0).then_inc(s_biasp, 1)
            pool.wait_ge(s_hk, 16 * (a + 1))
            nc.gpsimd.tensor_scalar(BIAS[:, h, 2 * P:EXT], HK[:, ::-1], -1.0, None, ALU.mult)
            pool.wait_ge(s_biasp, 3 * a + 1)
            nc.gpsimd.tensor_scalar(BIAS[:, h, 0:2 * P], BIAS[:, h, 0:2 * P], relc[:, a:a + 1], None,
                                    ALU.subtract).then_inc(s_biasp, 1)
            pool.wait_ge(s_biasp, 3 * a + 2)
            nc.gpsimd.memset(BIAS[HD:P, h, 0:HD], BIG).then_inc(s_biasp, 1)
            pool.wait_ge(s_biasp, 3 * a + 3)
            nc.gpsimd.memset(BIAS[0:HD, h, EXT - HD:EXT], BIG).then_inc(s_bias, 1)
            pool.wait_ge(s_bias, a + 1)

        TB = NT // BATCHES

        with nc.Block() as block:
            @block.sync
            def _(_sp):
                for i in range(NT):
                    sp.dma_start(xt0[:, i, :], x[P * i:P * i + P, :]).then_inc(s_x[i], 16)
                load_w(sp, 0, blocks_of(0))
                load_w(sp, 1, blocks_of(1))
                sp.wait_ge(s_extf, 2)
                sp.dma_start(ext_dram, extrow[:]).then_inc(s_ext, 16)
                sp.wait_ge(s_ext, 16)
                sp.wait_ge(s_idr, 2)
                sp_bias(0)
                load_w(sp, 2, blocks_of(2))
                sp_dup0(0)
                load_w(sp, 3, blocks_of(3))
                sp.wait_ge(s_fd, 5)
                sp.dma_start(cum_dram, fl[:]).then_inc(s_cum, 16)
                sp.wait_ge(s_cum, 16)

            @block.gpsimd
            def _(_pool):
                pool.wait_ge(s_small, 16 * 5)
                nc.gpsimd.memset(extrow[:, 513:EXT], 0.0).then_inc(s_extf, 1)
                pool.wait_ge(s_extf, 1)
                nc.gpsimd.tensor_scalar(extrow[:, 513:EXT], extrow[:, 513:EXT], extrow[:, 512:513], None,
                                        ALU.add).then_inc(s_extf, 1)
                split_w(pool, 0, None)
                nc.gpsimd.tensor_copy(WfR[:, HI], Wf[:]).then_inc(s_wf, 1)
                pool.wait_ge(s_wf, 1)
                nc.gpsimd.tensor_tensor(WfR[:, LO], Wf[:], WfR[:, HI].bitcast(F32),
                                        ALU.subtract).then_inc(s_wf, 1)
                split_w(pool, 1, None)
                split_w(pool, 2, 4)
                pool.wait_ge(s_hn, NT)
                pool_bias(0)

            @block.scalar
            def _(_act):
                act.dma_start(ident[:], c_ident).then_inc(s_const, 16)
                act.dma_start(trif, c_causal).then_inc(s_const, 16)
                act.dma_start(GB[:], bass.AP(norm_0.tensor, norm_0.offset, [[0, P], [1, DM]]))\
                    .then_inc(s_const, 16)
                act.dma_start(Wf[:], w_in_0[:, F_COL:F_COL + 8].rearrange("(k p) c -> p k c", p=P))\
                    .then_inc(s_small, 16)
                act.dma_start(extrow[:, 0:2 * CLIP + 1], rel_bias_0).then_inc(s_small, 16)
                act.dma_start(relc[:], bass.AP(rel_bias_0.tensor, rel_bias_0.offset + 2 * CLIP,
                                               [[0, P], [2 * CLIP + 1, 8]]),
                              allow_slow_non_contiguous=True).then_inc(s_small, 16)
                act.dma_start(fb[:], f_bias_0.rearrange("(h o) -> h o", o=1)).then_inc(s_small, 16)
                act.dma_start(sinkc[:], bass.AP(sinks_1.tensor, sinks_1.offset, [[0, P], [1, HEADS]]))\
                    .then_inc(s_small, 16)

                def squares(i):
                    act.wait_ge(s_x[i], 16)
                    wait(act, s_square, i)
                    nc.scalar.activation(junk[:], xt0[:, i, :], ACT.Square,
                                         accum_out=ss[:, i:i + 1]).then_inc(s_square, 1)

                def root(n):
                    act.wait_ge(s_var, n + 1)
                    nc.scalar.activation(sd[:, TB * n:TB * n + TB], var[:, TB * n:TB * n + TB], ACT.Sqrt)\
                        .then_inc(s_sqrt, 1)

                def hi(i):
                    for c in range(2):
                        act.wait_ge(s_ht, 2 * i + c + 1)
                        nc.scalar.activation(hT0[:, HI, 4 * c:4 * c + 4, P * i:P * i + P],
                                             T[c][:].rearrange("p (k t) -> p k t", k=4),
                                             ACT.Copy).then_inc(s_hthi, 1)

                act.wait_ge(s_const, 48)
                nc.scalar.activation(identR[:], ident[:], ACT.Copy).then_inc(s_idr, 1)
                nc.scalar.activation(triR[:], trif, ACT.Copy).then_inc(s_idr, 1)
                for n in range(BATCHES):
                    for i in range(TB * n, TB * n + TB):
                        squares(i)
                    for i in range(max(TB * (n - 1) - 1, 0), TB * n - 1):
                        hi(i)
                    root(n)
                for i in range(NT - TB - 1, NT):
                    hi(i)
                act.wait_ge(s_hn, NT)
                for g in range(4):
                    act_group0(g, 0, 0)
                act_group0(4, 0, 0)
                act.wait_ge(s_fd, 2)
                nc.scalar.activation(fe[:], fa[:], ACT.Exp).then_inc(s_fa, 1)
                act.wait_ge(s_fa, 1)
                nc.scalar.activation(fa[:], fe[:], ACT.Ln, bias=1.0).then_inc(s_fa, 1)
                for g in range(5, 12):
                    act_group0(g, 0, 0)

            @block.vector
            def _(_dve):
                dve.wait_ge(s_const, 48)

                def chain(n):
                    a = slice(TB * n, TB * n + TB)
                    dve.wait_ge(s_square, TB * n + TB)
                    nc.vector.tensor_scalar(var[:, a], ss[:, a], 1.0 / DM, EPS, ALU.mult, ALU.add)\
                        .then_inc(s_var, 1)
                    dve.wait_ge(s_sqrt, n + 1)
                    rsqrt_chain(a, n)

                def normed(i):
                    wait(dve, s_ht, 2 * i - 2)
                    nc.vector.scalar_tensor_tensor(HN[:, i % 2, :], xt0[:, i, :], rstd[:, i:i + 1], GB[:],
                                                   ALU.mult, ALU.mult).then_inc(s_hn, 1)

                def lo(i):
                    for c in range(2):
                        dve.wait_ge(s_hthi, 2 * i + c + 1)
                        nc.vector.tensor_tensor(hT0[:, LO, 4 * c:4 * c + 4, P * i:P * i + P],
                                                T[c][:].rearrange("p (k t) -> p k t", k=4),
                                                hT0[:, HI, 4 * c:4 * c + 4, P * i:P * i + P].bitcast(F32),
                                                ALU.subtract).then_inc(s_htlo, 1)

                for n in range(BATCHES):
                    chain(n)
                    for i in range(TB * n, TB * n + TB):
                        normed(i)
                        if i >= 1:
                            lo(i - 1)
                lo(NT - 1)
                for g in range(4):
                    dve_group0(g, 0, 0)
                for c in range(2):
                    dve.wait_ge(s_f, c + 1)
                    ins = nc.vector.tensor_scalar(fz[:, HALF * c:HALF * c + HALF], S[c][0:8, :], fb[:, 0:1],
                                                  None, ALU.add)
                ins.then_inc(s_fd, 1)
                dve.wait_ge(s_fd, 1)
                nc.vector.scalar_tensor_tensor(fa[:], fz[:], -1.0, fz[:], ALU.mult, ALU.min).then_inc(s_fd, 1)
                dve_group0(4, 0, 0)
                dve.wait_ge(s_fa, 2)
                nc.vector.scalar_tensor_tensor(fe[:], fz[:], 0.0, fa[:], ALU.min, ALU.subtract)\
                    .then_inc(s_fd, 1)
                dve.wait_ge(s_fd, 3)
                nc.vector.memset(fz[:], 1.0).then_inc(s_fd, 1)
                dve.wait_ge(s_fd, 4)
                nc.vector.tensor_tensor_scan(fl[:], fz[:], fe[:], 0.0, ALU.mult, ALU.add).then_inc(s_fd, 1)
                for g in range(5, 12):
                    dve_group0(g, 0, 0)

            @block.tensor
            def _(_pe):
                pe.wait_ge(s_const, 48)
                for i in range(NT):
                    pe.wait_ge(s_hn, i + 1)
                    for c in range(2):
                        if i >= 1:
                            pe.wait_ge(s_htlo, 2 * i - 1 + c)
                        for k in range(4):
                            mm = nc.tensor.transpose(T[c][:, P * k:P * k + P],
                                                     HN[:, i % 2, P * (4 * c + k):P * (4 * c + k) + P],
                                                     ident[:])
                        mm.then_inc(s_ht, 1)
                    if i >= NT // 2:
                        m = PER // 2 * (i % 2)
                        if i == NT // 2:
                            pe.wait_ge(s_htlo, NT)
                        pe_group0((i - NT // 2) // 2, 0, 1, m, m + PER // 2)
                pe.wait_ge(s_htlo, 2 * NT)
                for g in range(2, 4):
                    pe_group0(g, 0, 1, 0, PER)
                pe.wait_ge(s_wf, 2)
                for c in range(2):
                    for m in range(PER):
                        k, (a, b) = m // len(TERMS), TERMS[m % len(TERMS)]
                        mm = nc.tensor.matmul(S[c][0:8, :], WfR[:, a, k, :],
                                              hT0[:, b, k, HALF * c:HALF * c + HALF],
                                              start=(m == 0), stop=(m == PER - 1))
                    mm.then_inc(s_f, 1)
                for g in range(4, 12):
                    pe_group0(g, 0, 1, 0, PER)

        KIND = "AB"

        def step_back(n, b, slot, lag, first):
            if slot >= lag:
                return (n, b, slot - lag) if slot - lag < 2 * NT else None
            return None if first else (n - 1, 1 - b, 2 * NT + slot - lag)

        def pe_window0(n, b, first, last):
            def scores(n, b, s):
                kind, h, i = KIND[b], s // NT, s % NT
                k0, nk = key_tiles(kind, i)
                if s == 0:
                    pe.wait_ge(s_kdup, 32 * n + 32)
                    pe.wait_ge(s_j, 12 * n + 4)
                for e, (j0, nj) in enumerate(STEPS[kind][s]):
                    c = chunk0(kind, s) + e
                    wait(pe, s_sdone, CHUNKS * n + c - 2)
                    o = S[c % 3][:, 0:P * nj]
                    q = QZ0[b][:, h, P * i:P * i + P]
                    diagonal = kind == "B" and j0 + nj == nk
                    for hl in range(2):
                        mm = nc.tensor.matmul(o, q, KX0[b][:, hl, h, P * (k0 + j0):P * (k0 + j0 + nj)],
                                              start=(hl == HI), stop=(hl == LO and not diagonal))
                    if diagonal:
                        mm = nc.tensor.matmul(S[c % 3][:, P * (nj - 1):P * nj], identR[:], triR[:],
                                              start=False, stop=True)
                    mm.then_inc(s_scores, 1)

            def transposes(n, b, s):
                kind = KIND[b]
                pe.wait_ge(s_probs, 2 * NT * n + s + 1)
                for e, (j0, nj) in enumerate(STEPS[kind][s]):
                    c = chunk0(kind, s) + e
                    wait(pe, s_lo, CHUNKS * n + c - 1)
                    for t in range(nj):
                        mm = nc.tensor.transpose(T[c % 2][:, P * t:P * t + P],
                                                 L[:, s % 2, P * (j0 + t):P * (j0 + t) + P], ident[:])
                    mm.then_inc(s_tr, 1)

            def times_v(n, b, s):
                kind, h, i = KIND[b], s // NT, s % NT
                k0, nk = key_tiles(kind, i)
                pe.wait_ge(s_j, 12 * n + 5 + i)
                wait(pe, s_y, 2 * NT * n + s)
                for e, (j0, nj) in enumerate(STEPS[kind][s]):
                    c = chunk0(kind, s) + e
                    pe.wait_ge(s_lo, CHUNKS * n + c + 1)
                    for t in range(nj):
                        for pa in range(2):
                            mm = nc.tensor.matmul(PV[:, 0:P], PT[c % 2][:, pa, P * t:P * t + P],
                                                  V0[b][:, k0 + j0 + t, :, HD * h:HD * h + HD],
                                                  start=(j0 + t == 0 and pa == HI),
                                                  stop=(j0 + t == nk - 1 and pa == LO))
                    mm.then_inc(s_pv, 1)

            def project(slot, part):
                if last:
                    return
                if slot < NT:
                    m0 = PER // 4 * (2 * (slot % 2) + part)
                    pe_group0(slot // 2, 12 * (n + 1), 2 * (n + 1) + 1, m0, m0 + PER // 4)
                else:
                    m0 = PER // 2 * part
                    pe_group0(4 + slot - NT, 12 * (n + 1), 2 * (n + 1) + 1, m0, m0 + PER // 2)

            for slot in range(2 * NT + (2 if last else 0)):
                if slot < 2 * NT:
                    scores(n, b, slot)
                    project(slot, 0)
                step = step_back(n, b, slot, 2, first)
                if step:
                    times_v(*step)
                step = step_back(n, b, slot, 1, first)
                if step:
                    transposes(*step)
                if slot < 2 * NT:
                    project(slot, 1)

        def act_window0(n, b, first, last):
            def exps(n, b, s):
                kind = KIND[b]
                nk = key_tiles(kind, s % NT)[1]
                act.wait_ge(s_sdone, CHUNKS * n + chunk0(kind, s + 1))
                nc.scalar.activation(L[:, s % 2, 0:P * nk], L[:, s % 2, 0:P * nk], ACT.Exp,
                                     bias=negm[:, s % 4, 0:1], scale=-1.0,
                                     accum_out=rs[:, s % 4, 0:1]).then_inc(s_probs, 1)

            def hi(n, b, s):
                kind = KIND[b]
                for e, (j0, nj) in enumerate(STEPS[kind][s]):
                    c = chunk0(kind, s) + e
                    act.wait_ge(s_tr, CHUNKS * n + c + 1)
                    wait(act, s_pv, CHUNKS * n + c - 1)
                    nc.scalar.activation(PT[c % 2][:, HI, 0:P * nj], T[c % 2][:, 0:P * nj],
                                         ACT.Copy).then_inc(s_hi, 1)

            for slot in range(2 * NT + (2 if last else 0)):
                if slot == 0 and not first:
                    act_group0(11, 12 * n, b)
                if not last and ended_group(slot) is not None:
                    act_group0(ended_group(slot), 12 * (n + 1), 1 - b)
                step = step_back(n, b, slot, 1, first)
                if step and last:
                    hi(*step)
                if slot < 2 * NT:
                    exps(n, b, slot)
                if step and not last:
                    hi(*step)
                if last and slot % 3 == 2 and slot // 3 < len(WO_WINDOW):
                    act_wo(Wo0, WO_WINDOW[slot // 3], 0)

        def dve_holds_wait(n):
            if not isinstance(n, int):
                nc.vector.memset(held[:], 0.0)

        def dve_window0(n, b, first, last):
            def rows(n, b, s):
                kind, h, i = KIND[b], s // NT, s % NT
                nk = key_tiles(kind, i)[1]
                if i == 0:
                    if kind == "A":
                        dve.wait_ge(s_bias, n + h + 1)
                    else:
                        dve.wait_ge(s_ck[h], 8 * n + 8)
                before = chunk0(kind, s - 1) if s >= 2 else \
                    chunk0(KIND[1 - b], 2 * NT + s - 1) - CHUNKS
                wait(dve, s_tr, CHUNKS * n + before)
                b0 = EXT - P * nk if kind == "A" else 0
                for e, (j0, nj) in enumerate(STEPS[kind][s]):
                    c = chunk0(kind, s) + e
                    final = e == len(STEPS[kind][s]) - 1
                    dve.wait_ge(s_scores, CHUNKS * n + c + 1)
                    if e == 1:
                        dve.wait_ge(s_sdone, CHUNKS * n + c)
                    dve_holds_wait(n)
                    nc.vector.tensor_tensor_reduce(
                        out=L[:, s % 2, P * j0:P * (j0 + nj)], in0=S[c % 3][:, 0:P * nj],
                        in1=BIAS[:, h, b0 + P * j0:b0 + P * (j0 + nj)], scale=1.0,
                        scalar=nmpart[:] if e == 1 else 3e38, op0=ALU.add, op1=ALU.min,
                        accum_out=negm[:, s % 4, 0:1] if final else nmpart[:]).then_inc(s_sdone, 1)

            def lo(n, b, s):
                kind = KIND[b]
                dve.wait_ge(s_probs, 2 * NT * n + s + 1)
                nc.vector.reciprocal(rinv[:, s % 4, 0:1], rs[:, s % 4, 0:1]).then_inc(s_rinv, 1)
                for e, (j0, nj) in enumerate(STEPS[kind][s]):
                    c = chunk0(kind, s) + e
                    dve.wait_ge(s_hi, CHUNKS * n + c + 1)
                    nc.vector.tensor_tensor(PT[c % 2][:, LO, 0:P * nj], T[c % 2][:, 0:P * nj],
                                            PT[c % 2][:, HI, 0:P * nj].bitcast(F32),
                                            ALU.subtract).then_inc(s_lo, 1)

            def gated(n, b, s):
                kind, h, i = KIND[b], s // NT, s % NT
                st = 2 * NT * n + s
                dve.wait_ge(s_pv, CHUNKS * n + chunk0(kind, s + 1))
                nc.vector.tensor_reduce(ysum[:, 0:HD], PV[:, 0:P].rearrange("p (x d) -> p d x", x=2),
                                        mybir.AxisListType.X, ALU.add).then_inc(s_ysum, 1)
                if h == 0:
                    wait(dve, s_yst[i], 16 * n)
                dve.wait_ge(s_rinv, st + 1)
                dve.wait_ge(s_ysum, st + 1)
                nc.vector.scalar_tensor_tensor(Y[:, i, HD * h:HD * h + HD], ysum[:, 0:HD],
                                               rinv[:, s % 4, 0:1],
                                               SG0[b][:, i, HD * h:HD * h + HD],
                                               ALU.mult, ALU.mult).then_inc(s_y, 1)

            for slot in range(2 * NT + (3 if last else 0)):
                step = step_back(n, b, slot, 3, first)
                if step:
                    gated(*step)
                if slot < 2 * NT:
                    rows(n, b, slot)
                if slot == 0 and not first:
                    dve_group0(11, 12 * n, b)
                if not last and ended_group(slot) is not None:
                    dve_group0(ended_group(slot), 12 * (n + 1), 1 - b)
                step = step_back(n, b, slot, 1, first)
                if step:
                    lo(*step)
                if last and slot % 3 == 2 and slot // 3 < len(WO_WINDOW):
                    dve_wo(Wo0, WO_WINDOW[slot // 3], 0)

        WO_POOL = (0, 2, 4, 6)
        WO_WINDOW = (1, 3, 5, 7)

        def act_wo(Wo, k, layer):
            act.wait_ge(s_wor[k // 2], 16 * (layer + 1))
            nc.scalar.activation(Wo[:, HI, k, :], WoRaw[:, k, :], ACT.Copy).then_inc(s_wohi[k], 1)

        def dve_wo(Wo, k, layer):
            dve.wait_ge(s_wohi[k], layer + 1)
            nc.vector.tensor_tensor(Wo[:, LO, k, :], WoRaw[:, k, :], Wo[:, HI, k, :].bitcast(F32),
                                    ALU.subtract).then_inc(s_wolo[k], 1)

        def pool_wo(Wo, k, layer):
            pool.wait_ge(s_wor[k // 2], 16 * (layer + 1))
            nc.gpsimd.tensor_copy(Wo[:, HI, k, :], WoRaw[:, k, :]).then_inc(s_wohi[k], 1)
            pool.wait_ge(s_wohi[k], layer + 1)
            nc.gpsimd.tensor_tensor(Wo[:, LO, k, :], WoRaw[:, k, :], Wo[:, HI, k, :].bitcast(F32),
                                    ALU.subtract).then_inc(s_wolo[k], 1)

        def sp_wo(w_out, q):
            sp.dma_start(WoRaw[:, 2 * q:2 * q + 2, :],
                         w_out[2 * P * q:2 * P * q + 2 * P, :].rearrange("(k p) n -> p k n", p=P))\
                .then_inc(s_wor[q], 16)

        def rounds(eng, window):
            window(0, 0, True, False)
            window(1, 1, False, False)
            with eng.Fori(1, PAIRS // 2 - 1) as a:
                window(2 * a, 0, False, False)
                window(2 * a + 1, 1, False, False)
            window(PAIRS - 2, 0, False, False)
            window(PAIRS - 1, 1, False, True)

        with nc.Block() as block:
            @block.tensor
            def _(_pe):
                rounds(pe, pe_window0)

            @block.scalar
            def _(_act):
                rounds(act, act_window0)

            @block.vector
            def _(_dve):
                rounds(dve, dve_window0)

            @block.sync
            def _(_sp):
                sp_bias(1)
                for n in range(PAIRS):
                    p = column_pair(n)
                    if 2 * n + 4 < 2 * PAIRS:
                        load_w(sp, 2 * n + 4, blocks_of(2 * n + 4))
                    if n + 1 < PAIRS:
                        sp_bias(2 * n + 2)
                        sp_dup0(n + 1)
                    if 2 * n + 5 < 2 * PAIRS:
                        load_w(sp, 2 * n + 5, blocks_of(2 * n + 5))
                    if n == PAIRS - 1:
                        sp.wait_ge(s_proj, GRP1)
                        for q in range(4):
                            sp_wo(w_out_0, q)
                    for i in range(NT):
                        sp.wait_ge(s_y, 2 * NT * n + NT + i + 1)
                        sp.dma_start(y_dram[0, P * i:P * i + P, P * p:P * p + P], Y[:, i, :])\
                            .then_inc(s_yst[i], 16)
                    if n + 1 < PAIRS:
                        sp_bias(2 * n + 3)
                for i in range(NT):
                    sp.wait_ge(s_yst[i], 16 * PAIRS)

            @block.gpsimd
            def _(_pool):
                pool_bias(1)
                split_w(pool, 3, 12)
                for n in range(PAIRS):
                    if n % 2 == 1 and n + 1 < PAIRS:
                        pool_bias(2 * n + 2)
                    if 2 * n + 4 < 2 * PAIRS:
                        split_w(pool, 2 * n + 4, 12 * (n + 1) + 4)
                    if n % 2 == 1 and n + 1 < PAIRS:
                        pool_bias(2 * n + 3)
                    if 2 * n + 5 < 2 * PAIRS:
                        split_w(pool, 2 * n + 5, 12 * (n + 1) + 12)
                pool.wait_ge(s_proj, GRP1)
                for k in WO_POOL:
                    pool_wo(Wo0, k, 0)

        def out_phase(layer, Wo, w_norm, residual):
            b16, b8 = 16 * layer, 8 * layer
            last = layer == 1

            with nc.Block() as block:
                @block.tensor
                def _(_pe):
                    def y_transposes(i):
                        pe.wait_ge(s_yt[i % 2], 16 * (4 * layer + i // 2 + 1))
                        for c in range(2):
                            if i >= 1:
                                pe.wait_ge(s_ytlo, b16 + 2 * i - 1 + c)
                            for k in range(4):
                                mm = nc.tensor.transpose(T[c][:, P * k:P * k + P],
                                                         YT[:, i % 2, P * (4 * c + k):P * (4 * c + k) + P],
                                                         ident[:])
                            mm.then_inc(s_ytr, 1)

                    def product(i, c):
                        if c == 0:
                            pe.wait_ge(s_ytlo, b16 + 2 * i + 2)
                        if i >= 1:
                            pe.wait_ge(s_jo, b16 + 2 * i - 1 + c)
                        for k in range(NK):
                            if i == 0 and c == 0:
                                pe.wait_ge(s_wolo[k], layer + 1)
                            for n, (a, b) in enumerate(TERMS):
                                mm = nc.tensor.matmul(J[c][:], yT[i % 2][:, a, k, :],
                                                      Wo[:, b, k, HALF * c:HALF * c + HALF],
                                                      start=(k == 0 and n == 0),
                                                      stop=(k == NK - 1 and n == 2))
                        mm.then_inc(s_mm, 1)

                    def h_transposes(i):
                        pe.wait_ge(s_hn, 8 + i + 1)
                        for c in range(2):
                            if i >= 1:
                                pe.wait_ge(s_htlo, 16 + 2 * i - 1 + c)
                            for k in range(4):
                                mm = nc.tensor.transpose(S[c][:, P * k:P * k + P],
                                                         HN1[:, i % 2, P * (4 * c + k):P * (4 * c + k) + P],
                                                         ident[:])
                            mm.then_inc(s_ht, 1)

                    for j in range(NT + 2):
                        if j < NT:
                            y_transposes(j)
                        if 1 <= j <= NT:
                            product(j - 1, 0)
                            product(j - 1, 1)
                        if j >= 2 and not last:
                            h_transposes(j - 2)

                @block.scalar
                def _(_act):
                    act.dma_start(GB1[:], bass.AP(w_norm.tensor, w_norm.offset, [[0, P], [1, DM]]))\
                        .then_inc(s_gb, 16)
                    for j in range(NT + 2):
                        if j < NT:
                            if j >= 2:
                                act.wait_ge(s_mm, b16 + 2 * j - 2)
                            for c in range(2):
                                act.wait_ge(s_ytr, b16 + 2 * j + c + 1)
                                nc.scalar.activation(yT[j % 2][:, HI, 4 * c:4 * c + 4, :],
                                                     T[c][:].rearrange("p (k t) -> p k t", k=4),
                                                     ACT.Copy).then_inc(s_ythi, 1)
                        if j >= 2 and not last:
                            i = j - 2
                            for c in range(2):
                                act.wait_ge(s_ht, 16 + 2 * i + c + 1)
                                nc.scalar.activation(hT1[:, HI, 4 * c:4 * c + 4, P * i:P * i + P],
                                                     S[c][:].rearrange("p (k t) -> p k t", k=4),
                                                     ACT.Copy).then_inc(s_hthi, 1)
                        if 1 <= j <= NT:
                            i = j - 1
                            act.wait_ge(s_jo, b16 + 2 * i + 2)
                            if not last:
                                act.dma_start(x1_dram[P * i:P * i + P, :], X1[:, i % 2, :])\
                                    .then_inc(s_st[i % 2], 16)
                            if i >= 2 and last:
                                act.wait_ge(s_ot[i % 2], 16 * (i // 2))
                            nc.scalar.activation(HN1[:, i % 2, :], X1[:, i % 2, :], ACT.Square,
                                                 accum_out=ss[:, i:i + 1]).then_inc(s_square, 1)
                            act.wait_ge(s_var, BATCHES + b8 + i + 1)
                            nc.scalar.activation(sd[:, i:i + 1], var[:, i:i + 1], ACT.Sqrt)\
                                .then_inc(s_sqrt, 1)

                @block.vector
                def _(_dve):
                    dve.wait_ge(s_gb, 16 * (layer + 1))
                    for j in range(NT + 2):
                        if j < NT:
                            for c in range(2):
                                dve.wait_ge(s_ythi, b16 + 2 * j + c + 1)
                                nc.vector.tensor_tensor(yT[j % 2][:, LO, 4 * c:4 * c + 4, :],
                                                        T[c][:].rearrange("p (k t) -> p k t", k=4),
                                                        yT[j % 2][:, HI, 4 * c:4 * c + 4, :].bitcast(F32),
                                                        ALU.subtract).then_inc(s_ytlo, 1)
                        if j >= 2 and not last:
                            i = j - 2
                            for c in range(2):
                                dve.wait_ge(s_hthi, 16 + 2 * i + c + 1)
                                nc.vector.tensor_tensor(hT1[:, LO, 4 * c:4 * c + 4, P * i:P * i + P],
                                                        S[c][:].rearrange("p (k t) -> p k t", k=4),
                                                        hT1[:, HI, 4 * c:4 * c + 4, P * i:P * i + P]
                                                        .bitcast(F32), ALU.subtract).then_inc(s_htlo, 1)
                        if 1 <= j <= NT:
                            i = j - 1
                            dve.wait_ge(s_xr[i % 2], 16 * (4 * layer + i // 2 + 1))
                            if i >= 2 and not last:
                                dve.wait_ge(s_st[i % 2], 16 * (i // 2))
                            for c in range(2):
                                dve.wait_ge(s_mm, b16 + 2 * i + c + 1)
                                nc.vector.tensor_tensor(X1[:, i % 2, HALF * c:HALF * c + HALF], J[c][:],
                                                        XR[:, i % 2, HALF * c:HALF * c + HALF],
                                                        ALU.add).then_inc(s_jo, 1)
                            dve.wait_ge(s_square, 8 + b8 + i + 1)
                            nc.vector.tensor_scalar(var[:, i:i + 1], ss[:, i:i + 1], 1.0 / DM, EPS,
                                                    ALU.mult, ALU.add).then_inc(s_var, 1)
                            dve.wait_ge(s_sqrt, BATCHES + b8 + i + 1)
                            rsqrt_chain(slice(i, i + 1), BATCHES + b8 + i)
                            if i >= 2 and not last:
                                dve.wait_ge(s_ht, 16 + 2 * i - 2)
                            nc.vector.scalar_tensor_tensor(HN1[:, i % 2, :], X1[:, i % 2, :],
                                                           rstd[:, i:i + 1], GB1[:], ALU.mult,
                                                           ALU.mult).then_inc(s_hn, 1)

                @block.sync
                def _(_sp):
                    def loads(i):
                        if i >= 2:
                            sp.wait_ge(s_ytr, b16 + 2 * i - 2)
                        sp.dma_start(YT[:, i % 2, :], y_dram[layer, P * i:P * i + P, :])\
                            .then_inc(s_yt[i % 2], 16)
                        if i >= 2:
                            sp.wait_ge(s_jo, b16 + 2 * i - 2)
                        sp.dma_start(XR[:, i % 2, :], residual[P * i:P * i + P, :])\
                            .then_inc(s_xr[i % 2], 16)

                    loads(0)
                    loads(1)
                    if not last:
                        load_w(sp, BLK1, blocks_of(BLK1))
                    for i in range(2, NT):
                        loads(i)
                    for b in range(2):
                        sp.wait_ge(s_ot[b] if last else s_st[b], 16 * 4)

                @block.gpsimd
                def _(_pool):
                    if not last:
                        split_w(pool, BLK1, GRP1)
                    for i in range(NT if last else 0):
                        pool.wait_ge(s_hn, 16 + i + 1)
                        pool.dma_start(out[P * i:P * i + P, :], HN1[:, i % 2, :]).then_inc(s_ot[i % 2], 16)

        out_phase(0, Wo0, norm_1, x)

        LEAD = 4

        def pe_group1(m, wslot, tile, part):
            for r in range(PER // 2 * part, PER // 2 * (part + 1)):
                k, (a, b) = r // len(TERMS), TERMS[r % len(TERMS)]
                if r == 0:
                    pe.wait_ge(s_j, GRP1 + m - 1)
                mm = nc.tensor.matmul(J[tile % 2][:, 0:2 * P], hT1[:, a, k, P * tile:P * tile + P],
                                      Wslot[wslot][:, b, k, :], start=(r == 0), stop=(r == PER - 1))
                if r == PER - 1:
                    mm.then_inc(s_proj, 1)

        def pe_rotated(m, tile):
            pe.wait_ge(s_rope, m + 1)
            wait(pe, s_qlo, m)
            nc.tensor.transpose(T[1][:, 0:P], QR[:, tile % 2, :], ident[:]).then_inc(s_qt, 1)

        def act_group1(m, tile, b):
            act.wait_ge(s_proj, GRP1 + m + 1)
            if b is None:
                nc.scalar.activation(V1[:, tile, HI, :], J[tile % 2][:, P:2 * P], ACT.Copy, scale=0.5)\
                    .then_inc(s_jhi, 1)
            else:
                nc.scalar.activation(SG1[b][:, tile, :], J[tile % 2][:, P:2 * P], ACT.Tanh, scale=0.5)\
                    .then_inc(s_jhi, 1)

        def act_rotated(m, tile, b):
            act.wait_ge(s_qt, m + 1)
            tok = slice(P * tile, P * tile + P)
            for h in range(2):
                own = slice(HD * h, HD * h + HD)
                if b is None:
                    ins = nc.scalar.activation(KX1[own, HI, h, tok], T[1][own, 0:P], ACT.Copy)
                else:
                    ins = nc.scalar.activation(QZ1[b][own, h, tok], T[1][own, 0:P], ACT.Copy,
                                               scale=-0.125)
            ins.then_inc(s_qhi, 1)

        def dve_group1(m, tile, b):
            dve.wait_ge(s_jhi, GRP1 + m + 1)
            wait(dve, s_qt, m - 1)
            heads = J[tile % 2][:, 0:P].rearrange("p (h d) -> p h d", h=2)
            halves = J[tile % 2][:, 0:P].rearrange("p (h s d) -> p h s d", h=2, s=2)
            cos = ROPE[:, tile, 0, :].rearrange("p (o d) -> p o d", o=1).broadcast_to((P, 2, HD))
            sin = ROPE[:, tile, 1, :].rearrange("p (s d) -> p s d", s=2)
            q = QR[:, tile % 2, :]
            wait(dve, s_rope, m)
            nc.vector.tensor_tensor(q.rearrange("p (h d) -> p h d", h=2), heads, cos, ALU.mult)
            for h in range(2):
                ins = nc.vector.tensor_tensor(
                    QS[:, HD * h:HD * h + HD].rearrange("p (s d) -> p s d", s=2),
                    halves[:, h, ::-1, :], sin, ALU.mult)
            ins.then_inc(s_qr, 1)
            if b is None:
                nc.vector.scalar_tensor_tensor(V1[:, tile, LO, :], J[tile % 2][:, P:2 * P], 0.5,
                                               V1[:, tile, HI, :].bitcast(F32),
                                               ALU.mult, ALU.subtract).then_inc(s_j, 1)
            else:
                nc.vector.scalar_tensor_tensor(SG1[b][:, tile, :], SG1[b][:, tile, :], 1.0,
                                               J[tile % 2][:, P:2 * P], ALU.add, ALU.mult)\
                    .then_inc(s_j, 1)
            dve.wait_ge(s_qr, m + 1)
            nc.vector.tensor_tensor(q, q, QS, ALU.add).then_inc(s_rope, 1)

        def dve_rotated(m, tile, b):
            dve.wait_ge(s_qhi, m + 1)
            tok = slice(P * tile, P * tile + P)
            for h in range(2):
                own = slice(HD * h, HD * h + HD)
                other = slice(HD - HD * h, P - HD * h)
                if b is None:
                    ins = nc.vector.tensor_tensor(KX1[own, LO, h, tok], T[1][own, 0:P],
                                                  KX1[own, HI, h, tok].bitcast(F32), ALU.subtract)
                else:
                    ins = nc.vector.scalar_tensor_tensor(
                        QZ1[b][other, h, tok], T[1][own, 0:P], -0.125,
                        QZ1[b][own, h, tok].bitcast(F32), ALU.mult, ALU.subtract)
            ins.then_inc(s_qlo, 1)

        LEADIN = NT + LEAD

        def group_of(n, b, s, ago, last):
            q = s + LEAD - ago
            if last and q >= NT:
                return None
            return NT + NT * n + q, q % NT, (b + q // NT) % 2

        def lead_group(v):
            return v, v % NT, None if v < NT else 0

        def back1(n, b, s, lag, first):
            if s >= lag:
                return (n, b, s - lag) if s - lag < NT else None
            return None if first else (n - 1, 1 - b, NT + s - lag)

        def pe_window1(n, b, first, last):
            def scores(n, b, s):
                k0, nk = key_tiles("C", s)
                pe.wait_ge(s_qlo, NT + NT * n + s + 1)
                wait(pe, s_sdone, CH1 + NT * n + s - 1)
                for h in range(2):
                    for hl in range(2):
                        mm = nc.tensor.matmul(S[s % 2][:, 2 * P * h:2 * P * h + P * nk],
                                              QZ1[b][:, h, P * s:P * s + P],
                                              KX1[:, hl, b, P * k0:P * (k0 + nk)],
                                              start=(hl == HI), stop=(hl == LO))
                mm.then_inc(s_scores, 1)

            def transposes(n, b, s):
                nk = key_tiles("C", s)[1]
                pe.wait_ge(s_probs, ST1 + NT * n + s + 1)
                pe.wait_ge(s_lo, CH1 + NT * n + s)
                for h in range(2):
                    for t in range(nk):
                        o = P * (nk * h + t)
                        mm = nc.tensor.transpose(T[0][:, o:o + P],
                                                 L[:, s % 2, 2 * P * h + P * t:2 * P * h + P * t + P],
                                                 ident[:])
                mm.then_inc(s_tr, 1)

            def times_v(n, b, s):
                k0, nk = key_tiles("C", s)
                pe.wait_ge(s_y, ST1 + NT * n + s)
                pe.wait_ge(s_lo, CH1 + NT * n + s + 1)
                for h in range(2):
                    for t in range(nk):
                        for pa in range(2):
                            mm = nc.tensor.matmul(PV[:, P * h:P * h + P],
                                                  PT[s % 2][:, pa, P * (nk * h + t):P * (nk * h + t) + P],
                                                  V1[:, k0 + t, :, HD * b:HD * b + HD],
                                                  start=(t == 0 and pa == HI), stop=(t == nk - 1 and pa == LO))
                mm.then_inc(s_pv, 1)

            for s in range(NT + (2 if last else 0)):
                group = group_of(n, b, s, 0, last)
                if s < NT:
                    scores(n, b, s)
                if group:
                    m, tile, buf = group
                    if tile == 0:
                        pe.wait_ge(s_w, BLK1 + 2 + n + s // LEAD)
                    pe_group1(m, 1 - buf, tile, 0)
                step = back1(n, b, s, 1, first)
                if step:
                    transposes(*step)
                if group:
                    pe_group1(m, 1 - buf, tile, 1)
                step = back1(n, b, s, 2, first)
                if step:
                    times_v(*step)
                group = group_of(n, b, s, 1, last)
                if group:
                    pe_rotated(group[0], group[1])

        def act_window1(n, b, first, last):
            def exps(n, b, s):
                nk = key_tiles("C", s)[1]
                act.wait_ge(s_snm, NT * n + s + 1)
                for h in range(2):
                    r = L[:, s % 2, 2 * P * h:2 * P * h + P * nk]
                    nc.scalar.activation(r, r, ACT.Exp, bias=negm[:, s % 4, h:h + 1], scale=-1.0,
                                         accum_out=rs[:, s % 4, h:h + 1])
                nc.scalar.activation(es[:, s % 4, :], snm[:, s % 4, :], ACT.Exp).then_inc(s_probs, 1)

            def hi(n, b, s):
                nk = key_tiles("C", s)[1]
                act.wait_ge(s_tr, CH1 + NT * n + s + 1)
                act.wait_ge(s_pv, CH1 + NT * n + s - 1)
                nc.scalar.activation(PT[s % 2][:, HI, 0:2 * P * nk], T[0][:, 0:2 * P * nk],
                                     ACT.Copy).then_inc(s_hi, 1)

            for s in range(NT + (2 if last else 0)):
                group = group_of(n, b, s, 1, last)
                if group:
                    act_group1(*group)
                group = group_of(n, b, s, 2, last)
                if group:
                    act_rotated(*group)
                if s < NT:
                    exps(n, b, s)
                step = back1(n, b, s, 1, first)
                if step:
                    hi(*step)

        def dve_window1(n, b, first, last):
            def rows(n, b, s):
                nk = key_tiles("C", s)[1]
                if s == 0:
                    p = n + 7 * b
                    nc.vector.tensor_scalar(nsink[:, b, :], sinkc[:, bass.ds(p, 2)], -1.0, None, ALU.mult)\
                        .then_inc(s_nsk, 1)
                    dve.wait_ge(s_nsk, n + 1)
                wait(dve, s_tr, CH1 + NT * n + s - 1)
                dve.wait_ge(s_scores, CH1 + NT * n + s + 1)
                dve_holds_wait(n)
                for h in range(2):
                    ins = nc.vector.tensor_tensor_reduce(
                        out=L[:, s % 2, 2 * P * h:2 * P * h + P * nk],
                        in0=S[s % 2][:, 2 * P * h:2 * P * h + P * nk],
                        in1=WM[:, 2 * P - P * nk:2 * P], scale=1.0,
                        scalar=nsink[:, b, h:h + 1], op0=ALU.add, op1=ALU.min,
                        accum_out=negm[:, s % 4, h:h + 1])
                ins.then_inc(s_sdone, 1)
                dve.wait_ge(s_sdone, CH1 + NT * n + s + 1)
                nc.vector.tensor_tensor(snm[:, s % 4, :], negm[:, s % 4, :], nsink[:, b, :],
                                        ALU.subtract).then_inc(s_snm, 1)

            def lo(n, b, s):
                nk = key_tiles("C", s)[1]
                dve.wait_ge(s_probs, ST1 + NT * n + s + 1)
                nc.vector.tensor_tensor(rinv[:, s % 4, :], rs[:, s % 4, :], es[:, s % 4, :], ALU.add)\
                    .then_inc(s_tot, 1)
                dve.wait_ge(s_hi, CH1 + NT * n + s + 1)
                nc.vector.tensor_tensor(PT[s % 2][:, LO, 0:2 * P * nk], T[0][:, 0:2 * P * nk],
                                        PT[s % 2][:, HI, 0:2 * P * nk].bitcast(F32),
                                        ALU.subtract).then_inc(s_lo, 1)
                dve.wait_ge(s_tot, NT * n + s + 1)
                nc.vector.reciprocal(rinv[:, s % 4, :], rinv[:, s % 4, :]).then_inc(s_rinv, 1)

            def gated(n, b, s):
                st = ST1 + NT * n + s
                dve.wait_ge(s_pv, CH1 + NT * n + s + 1)
                nc.vector.tensor_reduce(ysum[:].rearrange("p (h d) -> p h d", h=2),
                                        PV[:, 0:2 * P].rearrange("p (h x d) -> p h d x", h=2, x=2),
                                        mybir.AxisListType.X, ALU.add).then_inc(s_ysum, 1)
                dve.wait_ge(s_yst[s], 16 * (PAIRS + n))
                dve.wait_ge(s_rinv, st + 1)
                dve.wait_ge(s_ysum, st + 1)
                for h in range(2):
                    ins = nc.vector.scalar_tensor_tensor(Y[:, s, HD * h:HD * h + HD],
                                                         ysum[:, HD * h:HD * h + HD],
                                                         rinv[:, s % 4, h:h + 1],
                                                         SG1[b][:, s, HD * h:HD * h + HD],
                                                         ALU.mult, ALU.mult)
                ins.then_inc(s_y, 1)

            for s in range(NT + (3 if last else 0)):
                group = group_of(n, b, s, 1, last)
                if group:
                    dve_group1(*group)
                if s < NT:
                    rows(n, b, s)
                group = group_of(n, b, s, 2, last)
                if group:
                    dve_rotated(*group)
                step = back1(n, b, s, 3, first)
                if step:
                    gated(*step)
                step = back1(n, b, s, 1, first)
                if step:
                    lo(*step)

        with nc.Block() as block:
            @block.tensor
            def _(_pe):
                pe.wait_ge(s_w, BLK1 + 1)
                for v in range(LEADIN):
                    if v == NT:
                        pe.wait_ge(s_w, BLK1 + 2)
                    for part in range(2):
                        pe_group1(v, v // NT, v % NT, part)
                    if v >= 1:
                        pe_rotated(v - 1, (v - 1) % NT)
                pe.wait_ge(s_kdup, 32 * PAIRS + 32)
                rounds(pe, pe_window1)

            @block.scalar
            def _(_act):
                act.dma_start(ROPE[:], c_rope.rearrange("(t p) c d -> p t c d", p=P)).then_inc(s_rope_c, 16)
                act.dma_start(WM, c_window).then_inc(s_rope_c, 16)
                for v in range(LEADIN):
                    if v >= 1:
                        act_group1(*lead_group(v - 1))
                    if v >= 2:
                        act_rotated(*lead_group(v - 2))
                rounds(act, act_window1)
                act.wait_ge(s_proj, GRP1 + NT * (PAIRS + 1))
                for k in WO_WINDOW:
                    act_wo(Wo1, k, 1)

            @block.vector
            def _(_dve):
                dve.wait_ge(s_rope_c, 32)
                for v in range(LEADIN):
                    if v >= 1:
                        dve_group1(*lead_group(v - 1))
                    if v >= 2:
                        dve_rotated(*lead_group(v - 2))
                rounds(dve, dve_window1)
                for k in WO_WINDOW:
                    dve_wo(Wo1, k, 1)

            @block.sync
            def _(_sp):
                load_w(sp, BLK1 + 1, blocks_of(BLK1 + 1))
                load_w(sp, BLK1 + 2, blocks_of(BLK1 + 2))
                sp.wait_ge(s_qlo, NT)
                sp.dma_start(KX1[HD:P, :, 0, :].bitcast(F32), KX1[0:HD, :, 0, :].bitcast(F32))\
                    .then_inc(s_kdup, 16)
                sp.dma_start(KX1[0:HD, :, 1, :].bitcast(F32), KX1[HD:P, :, 1, :].bitcast(F32))\
                    .then_inc(s_kdup, 16)
                for n in range(PAIRS):
                    p = column_pair(n)
                    if n + 2 < PAIRS:
                        load_w(sp, BLK1 + 3 + n, blocks_of(BLK1 + 3 + n))
                    if n == PAIRS - 1:
                        sp.wait_ge(s_proj, GRP1 + NT * (PAIRS + 1))
                        for q in range(4):
                            sp_wo(w_out_1, q)
                    for i in range(NT):
                        sp.wait_ge(s_y, ST1 + NT * n + i + 1)
                        sp.dma_start(y_dram[1, P * i:P * i + P, P * p:P * p + P], Y[:, i, :])\
                            .then_inc(s_yst[i], 16)
                for i in range(NT):
                    sp.wait_ge(s_yst[i], 2 * 16 * PAIRS)

            @block.gpsimd
            def _(_pool):
                for n in range(PAIRS):
                    split_w(pool, BLK1 + 1 + n, GRP1 + NT * n)
                pool.wait_ge(s_proj, GRP1 + NT * (PAIRS + 1))
                for k in WO_POOL:
                    pool_wo(Wo1, k, 1)

        out_phase(1, Wo1, norm_f, x1_dram)


_INS = ["x", "norm_0", "w_in_0", "rel_bias_0", "f_bias_0", "w_out_0", "norm_1", "w_in_1", "sinks_1",
        "w_out_1", "norm_f"]


def constants(np):
    causal = np.where(np.arange(P)[None, :] > np.arange(P)[:, None], BIG, 0.0).astype(np.float32)
    window = np.zeros((P, 2 * P), np.float32)
    window[:HD, :HD] = BIG
    window[:HD, 3 * HD:] = BIG
    window[HD:, :2 * HD] = BIG
    half = HD // 2
    inv = np.float32(10000.0) ** (-np.arange(half, dtype=np.float32) / np.float32(half))
    ang = np.arange(SEQ, dtype=np.float32)[:, None] * inv[None, :]
    cos, sin = np.cos(ang), np.sin(ang)
    rope = np.stack([np.concatenate([cos, cos], 1), np.concatenate([-sin, sin], 1)], 1).astype(np.float32)
    return {"c_ident": np.eye(P, dtype=np.float32), "c_causal": causal, "c_window": window, "c_rope": rope}


def kernel(**inputs):
    import numpy as _np
    import concourse.bacc as _bacc
    from concourse import mybir as _mybir
    from concourse.bass_utils import run_bass_kernel_spmd as _run

    nc = _bacc.Bacc("TRN2", target_bir_lowering=False, num_devices=1)
    arrays, args = {}, []
    given = [(name, _np.ascontiguousarray(inputs[name])) for name in _INS] + list(constants(_np).items())
    for name, a in given:
        arrays[f"in_{name}"] = a
        args.append(nc.dram_tensor(f"in_{name}", a.shape, _mybir.dt.from_np(a.dtype), kind="ExternalInput").ap())
    out = nc.dram_tensor("out", (1, SEQ, DM), F32, kind="ExternalOutput").ap()
    build_trunk(nc, *args, out)
    r = _run(nc, [arrays], core_ids=[0])
    return r.results[0]["out"]
```

```python
from contextlib import ExitStack

import concourse.bass as bass
from concourse import mybir

F32 = mybir.dt.float32
F32R = mybir.dt.float32r
ALU = mybir.AluOpType
ACT = mybir.ActivationFunctionType

P = 128
HD = 64
SEQ = 1024
DM = 1024
NT = SEQ // P
NK = DM // P
HALF = SEQ // 2
HEADS = 16
PAIRS = HEADS // 2
HALF_PAIRS = PAIRS // 2
CLIP = 256
EXT = 640
BIG = 1e30
EPS = 1e-6
W_A = 512
GATE0 = 3 * W_A + 3 * W_A + 8
F_COL = 3 * W_A + 3 * W_A
KC, VC, GATE1 = 1024, 1152, 1280

HI, LO = 0, 1
TERMS = ((HI, HI), (HI, LO), (LO, HI))


def key_tiles(kind, i):
    n = min(i + 1, {"A": 5, "B": NT, "C": 2}[kind])
    return i + 1 - n, n


def key_chunks(n):
    return [(0, n)] if n <= 4 else [(0, (n + 1) // 2), ((n + 1) // 2, n // 2)]


STEPS = {kind: [key_chunks(key_tiles(kind, s % NT)[1]) for s in range(2 * NT)] for kind in "AB"}
CHUNKS = sum(len(c) for c in STEPS["A"])
assert CHUNKS == sum(len(c) for c in STEPS["B"]) and CHUNKS % 6 == 0


def chunk0(kind, s):
    return sum(len(c) for c in STEPS[kind][:s])


def ended_group(slot):
    if slot in (2, 4, 6, 8):
        return slot // 2 - 1
    return 4 + slot - 9 if slot >= 9 else None


def build_trunk(nc, x, norm_0, w_in_0, rel_bias_0, f_bias_0, w_out_0, norm_1, w_in_1, sinks_1,
                w_out_1, norm_f, c_ident, c_causal, c_window, c_rope, out):
    x = x[0]
    out = out[0]
    ext_dram = nc.dram_tensor("ext_bias", (8, EXT), F32, kind="Internal").ap()
    cum_dram = nc.dram_tensor("cum_forget", (8, SEQ), F32, kind="Internal").ap()
    y_dram = nc.dram_tensor("y_gated", (2, SEQ, DM), F32, kind="Internal").ap()
    x1_dram = nc.dram_tensor("x_mid", (SEQ, DM), F32, kind="Internal").ap()

    ctx = ExitStack()
    with ctx:
        def sem(name):
            return ctx.enter_context(nc.semaphore(name))

        base = nc.sbuf_base
        base += (-base) % 64
        top = [base]

        def at(name, shape, dt, offset):
            return nc.alloc_sbuf_tensor_at(name, shape, dt, offset=offset)

        def put(name, shape, dt=F32):
            size = 4
            for s in shape[1:]:
                size *= s
            t = at(name, shape, dt, top[0])
            top[0] += size + (-size) % 32
            return t

        R0 = top[0]
        hT0 = at("hT0", [P, 2, NK, SEQ], F32R, R0)
        Wo0 = at("Wo0", [P, 2, NK, DM], F32R, R0)
        QZ1 = [at(f"QZ1_{b}", [P, 2, SEQ], F32R, R0 + 8192 * b) for b in range(2)]
        KX1 = at("KX1", [P, 2, 2, SEQ], F32R, R0 + 16384)
        V1 = at("V1", [P, NT, 2, P], F32R, R0 + 32768)
        SG1 = [at(f"SG1_{b}", [P, NT, P], F32, R0 + 40960 + 4096 * b) for b in range(2)]
        ROPE = at("ROPE", [P, NT, 2, HD], F32, R0 + 49152)
        R1 = R0 + 65536
        xt0 = at("xt0", [P, NT, DM], F32, R1)
        QZ0 = [at(f"QZ0_{b}", [P, 2, SEQ], F32R, R1 + 8192 * b) for b in range(2)]
        KX0 = [at(f"KX0_{b}", [P, 2, 2, SEQ], F32R, R1 + 16384 + 16384 * b) for b in range(2)]
        V0 = [at(f"V0_{b}", [P, NT, 2, P], F32R, R1 + 49152 + 8192 * b) for b in range(2)]
        SG0 = [at(f"SG0_{b}", [P, NT, P], F32, R1 + 65536 + 4096 * b) for b in range(2)]
        hT1 = at("hT1", [P, 2, NK, SEQ], F32R, R1)
        Wo1 = at("Wo1", [P, 2, NK, DM], F32R, R1)
        R2 = R1 + 73728
        Wslot = [at(f"W_{b}", [P, 2, NK, 2 * P], F32R, R2 + 16384 * b) for b in range(2)]
        WoRaw = at("WoRaw", [P, NK, DM], F32, R2)
        yT = [at(f"yT_{b}", [P, 2, NK, P], F32R, R2 + 16384 + 8192 * b) for b in range(2)]
        XR = at("XR", [P, 2, DM], F32, R1 + 65536)
        R3 = R2 + 32768
        raw = at("raw", [P, NK, 2 * P], F32, R3)
        YT = at("YT", [P, 2, DM], F32, R3)
        R4 = R3 + 8192
        L = at("L", [P, 2, SEQ], F32, R4)
        raw_kv = at("raw_kv", [P, NK, 2 * P], F32, R4)
        junk = at("junk", [P, DM], F32, R4)
        R5 = R4 + 8192
        PT = [at(f"PT_{b}", [P, 2, 512], F32R, R5 + 4096 * b) for b in range(2)]
        HN = at("HN", [P, 2, DM], F32, R5)
        X1 = at("X1", [P, 2, DM], F32, R5)
        R6 = R5 + 8192
        BIAS = at("BIAS", [P, 2, SEQ], F32, R6)
        GB = at("GB", [P, DM], F32, R6)
        HN1 = at("HN1", [P, 2, DM], F32, R6)
        fz = at("fz", [8, SEQ], F32, R4)
        fe = at("fe", [8, SEQ], F32, R4 + 4096)
        fa = at("fa", [8, SEQ], F32, R5)
        fl = at("fl", [8, SEQ], F32, R5 + 4096)
        Wf = at("Wf", [P, NK, 8], F32, R6 + 4096)
        WfR = at("WfR", [P, 2, NK, 8], F32R, R6 + 4096 + 512)
        extrow = at("extrow", [8, EXT], F32, R6 + 4096 + 1024)
        fb = at("fb", [8, 1], F32, R6 + 4096 + 1024 + 4 * EXT)
        R7 = R6 + 8192
        Y = at("Y", [P, NT, P], F32, R7)
        GB1 = at("GB1", [P, DM], F32, R7)
        top[0] = R7 + 4096
        ident = put("ident", [P, P])
        triR_at = top[0]
        triR = put("triR", [P, P], F32R)
        identR = put("identR", [P, P], F32R)
        HK = put("HK", [P, 384])
        QR = at("QR", [P, 2, P], F32, triR_at)
        QS = HK[:, 2 * P:3 * P]
        relc = put("relc", [P, 8])
        sinkc = put("sinkc", [P, HEADS])
        nsink = put("nsink", [P, 2, 2])
        stats_at = top[0]
        ysum = put("ysum", [P, P])
        negm = put("negm", [P, 4, 2])
        nmpart = put("nmpart", [P, 1])
        held = put("held", [1, 1])
        rs = put("rs", [P, 4, 2])
        rinv = put("rinv", [P, 4, 2])
        snm = put("snm", [P, 4, 2])
        es = put("es", [P, 4, 2])
        ss = at("ss", [P, NT], F32, stats_at + 0)
        var = at("var", [P, NT], F32, stats_at + 32)
        sd = at("sd", [P, NT], F32, stats_at + 64)
        r0 = at("r0", [P, NT], F32, stats_at + 96)
        nt1 = at("nt1", [P, NT], F32, stats_at + 128)
        nt2 = at("nt2", [P, NT], F32, stats_at + 160)
        rstd = at("rstd", [P, NT], F32, stats_at + 192)
        assert top[0] <= nc.sbuf_usable_end, (top[0], nc.sbuf_usable_end)
        WM = HK[:, 0:2 * P]
        trif = HK[:, 0:P]

        def bank(name):
            return ctx.enter_context(nc.psum_tensor(name, [P, 512], F32))

        S = [bank(f"S{i}") for i in range(3)]
        T = [bank(f"T{i}") for i in range(2)]
        J = [bank(f"J{i}") for i in range(2)]
        PV = bank("PV")

        s_x = [sem(f"x_loaded{i}") for i in range(NT)]
        s_const = sem("consts_loaded")
        s_small = sem("small_inputs_loaded")
        s_square = sem("squares_summed")
        s_var = sem("variances_ready")
        s_sqrt = sem("roots_ready")
        s_norm = sem("norm_chain")
        s_hn = sem("normed_rows_ready")
        s_ht = sem("normed_transposed")
        s_hthi = sem("hT_hi_written")
        s_htlo = sem("hT_lo_written")
        s_idr = sem("rounded_consts_ready")
        s_wf = sem("forget_weights_split")
        s_f = sem("forget_logits_ready")
        s_fa = sem("forget_chain_act")
        s_fd = sem("forget_chain_dve")
        s_cum = sem("cum_stored")
        s_extf = sem("ext_row_filled")
        s_ext = sem("ext_row_stored")
        s_raw = sem("raw_weights_loaded")
        s_wh = sem("weights_hi_written")
        s_w = sem("weights_split")
        s_gb = sem("norm_weights_loaded")
        s_jo = sem("residual_added")
        s_ytr = sem("y_transposed")
        s_ythi = sem("yT_hi_written")
        s_ytlo = sem("yT_lo_written")
        s_st = [sem(f"x1_tile_stored{b}") for b in range(2)]
        s_ot = [sem(f"out_tile_stored{b}") for b in range(2)]
        s_rope_c = sem("layer1_tables_loaded")
        s_hk = sem("hankel_loaded")
        s_biasp = sem("bias_chain")
        s_bias = sem("bias_built")
        s_ck = [sem(f"cum_row_broadcast{h}") for h in range(2)]
        s_proj = sem("projection_group_done")
        s_jhi = sem("projection_hi_written")
        s_j = sem("projection_evacuated")
        s_kdup = sem("k_duplicated")
        s_scores = sem("scores_ready")
        s_sdone = sem("rows_written")
        s_snm = sem("sink_shift_ready")
        s_probs = sem("probs_ready")
        s_tr = sem("transposed")
        s_hi = sem("transposed_hi_written")
        s_lo = sem("transposed_lo_written")
        s_pv = sem("pv_chunk_done")
        s_tot = sem("totals_ready")
        s_rinv = sem("reciprocals_ready")
        s_y = sem("y_written")
        s_ysum = sem("pv_halves_added")
        s_yst = [sem(f"y_tile_stored{i}") for i in range(NT)]
        s_qt = sem("rotated_transposed")
        s_qhi = sem("rotated_hi_written")
        s_qlo = sem("rotated_lo_written")
        s_nsk = sem("sinks_of_pair_ready")
        s_wor = [sem(f"raw_out_weights{i}") for i in range(4)]
        s_wohi = [sem(f"out_weights_hi{k}") for k in range(NK)]
        s_wolo = [sem(f"out_weights_lo{k}") for k in range(NK)]
        s_qr = sem("rope_products")
        s_rope = sem("rotated_ready")
        s_yt = [sem(f"y_tile_loaded{b}") for b in range(2)]
        s_xr = [sem(f"x_tile_loaded{b}") for b in range(2)]
        s_mm = sem("out_projection_done")

        def load_w(n, blocks):
            wait(sp, s_w, n)
            for b, src in enumerate(blocks):
                stage = raw_kv if is_window(n, BLK1) else raw
                sp.dma_start(stage[:, :, P * b:P * b + P], src).then_inc(s_raw, 16)

        def split_w(pool, n, need):
            pool.wait_ge(s_raw, 32 * (n + 1))
            if need is not None:
                pool.wait_ge(s_proj, need)
            stage = raw_kv if n == BLK1 else raw
            nc.gpsimd.tensor_copy(Wslot[n % 2][:, HI], stage[:]).then_inc(s_wh, 1)
            pool.wait_ge(s_wh, n + 1)
            nc.gpsimd.tensor_tensor(Wslot[n % 2][:, LO], stage[:], Wslot[n % 2][:, HI].bitcast(F32),
                                    ALU.subtract).then_inc(s_w, 1)

        def pair_offset(n, b):
            return P // 2 * (n - b)

        def cols(w, c):
            return w[:, bass.ds(c, P)].rearrange("(k p) c -> p k c", p=P)

        def qk_blocks(n, b):
            o = pair_offset(n, b) + 3 * W_A * b
            return [cols(w_in_0, o), cols(w_in_0, o + W_A)]

        def vg_blocks(n, b):
            return [cols(w_in_0, pair_offset(n, b) + 3 * W_A * b + 2 * W_A),
                    cols(w_in_0, pair_offset(n, b) + GATE0 + W_A * b)]

        def qg_blocks(n, b):
            o = pair_offset(n, b) + P * HALF_PAIRS * b
            return [cols(w_in_1, o), cols(w_in_1, o + GATE1)]

        def is_window(n, which):
            return isinstance(n, int) and n == which

        def comes_before(n, which):
            return not isinstance(n, int) or n < which

        def store_y(layer, n, b, i):
            sp.dma_start(y_dram[layer, P * i:P * i + P, bass.ds(pair_offset(n, b) + P * HALF_PAIRS * b, P)],
                         Y[:, i, :]).then_inc(s_yst[i], 16)

        BLK1 = 2 * PAIRS
        GRP1 = 12 * PAIRS
        CH1 = CHUNKS * PAIRS
        ST1 = 2 * NT * PAIRS
        PER = NK * len(TERMS)
        BATCHES = 4

        def wait(eng, s, value):
            if not isinstance(value, int) or value > 0:
                eng.wait_ge(s, value)

        pe, act, dve, pool, sp = nc.tensor, nc.scalar, nc.vector, nc.gpsimd, nc.sync

        def rsqrt_chain(a, n):
            nc.vector.reciprocal(r0[:, a], sd[:, a]).then_inc(s_norm, 1)
            nc.vector.wait_ge(s_norm, 5 * n + 1)
            nc.vector.tensor_tensor(nt1[:, a], r0[:, a], r0[:, a], ALU.mult).then_inc(s_norm, 1)
            nc.vector.wait_ge(s_norm, 5 * n + 2)
            nc.vector.tensor_tensor(nt2[:, a], nt1[:, a], var[:, a], ALU.mult).then_inc(s_norm, 1)
            nc.vector.wait_ge(s_norm, 5 * n + 3)
            nc.vector.tensor_scalar(nt1[:, a], nt2[:, a], -0.5, 1.5, ALU.mult, ALU.add).then_inc(s_norm, 1)
            nc.vector.wait_ge(s_norm, 5 * n + 4)
            nc.vector.tensor_tensor(rstd[:, a], r0[:, a], nt1[:, a], ALU.mult).then_inc(s_norm, 1)
            nc.vector.wait_ge(s_norm, 5 * n + 5)

        def pe_group0(g, base, blocks, m0, m1):
            for m in range(m0, m1):
                k, (a, b) = m // len(TERMS), TERMS[m % len(TERMS)]
                if m == 0:
                    if g in (0, 4):
                        pe.wait_ge(s_w, blocks + g // 4)
                    wait(pe, s_j, base + g - 1)
                if g < 4:
                    which, half = g % 2, g // 2
                    mm = nc.tensor.matmul(J[g % 2][:], Wslot[0][:, a, k, P * which:P * which + P],
                                          hT0[:, b, k, HALF * half:HALF * half + HALF],
                                          start=(m == 0), stop=(m == PER - 1))
                else:
                    t = g - 4
                    mm = nc.tensor.matmul(J[g % 2][:, 0:2 * P], hT0[:, a, k, P * t:P * t + P],
                                          Wslot[1][:, b, k, :], start=(m == 0), stop=(m == PER - 1))
                if m == PER - 1:
                    mm.then_inc(s_proj, 1)

        def act_group0(g, base, b):
            act.wait_ge(s_proj, base + g + 1)
            if g < 4:
                which, half = g % 2, g // 2
                tok = slice(HALF * half, HALF * half + HALF)
                for h in range(2):
                    own = slice(HD * h, HD * h + HD)
                    if which == 0:
                        ins = nc.scalar.activation(QZ0[b][own, h, tok], J[g % 2][own, :], ACT.Copy,
                                                   scale=-0.125)
                    else:
                        ins = nc.scalar.activation(KX0[b][own, HI, h, tok], J[g % 2][own, :], ACT.Copy)
                ins.then_inc(s_jhi, 1)
            else:
                nc.scalar.activation(V0[b][:, g - 4, HI, :], J[g % 2][:, 0:P], ACT.Copy, scale=0.5)
                nc.scalar.activation(SG0[b][:, g - 4, :], J[g % 2][:, P:2 * P], ACT.Tanh, scale=0.5)\
                    .then_inc(s_jhi, 1)

        def dve_group0(g, base, b):
            dve.wait_ge(s_jhi, base + g + 1)
            if g < 4:
                which, half = g % 2, g // 2
                tok = slice(HALF * half, HALF * half + HALF)
                for h in range(2):
                    own = slice(HD * h, HD * h + HD)
                    other = slice(HD - HD * h, P - HD * h)
                    if which == 0:
                        ins = nc.vector.scalar_tensor_tensor(QZ0[b][other, h, tok], J[g % 2][own, :], -0.125,
                                                             QZ0[b][own, h, tok].bitcast(F32),
                                                             ALU.mult, ALU.subtract)
                    else:
                        ins = nc.vector.tensor_tensor(KX0[b][own, LO, h, tok], J[g % 2][own, :],
                                                      KX0[b][own, HI, h, tok].bitcast(F32), ALU.subtract)
                ins.then_inc(s_j, 1)
            else:
                t = g - 4
                nc.vector.scalar_tensor_tensor(V0[b][:, t, LO, :], J[g % 2][:, 0:P], 0.5,
                                               V0[b][:, t, HI, :].bitcast(F32), ALU.mult, ALU.subtract)
                nc.vector.scalar_tensor_tensor(SG0[b][:, t, :], SG0[b][:, t, :], 1.0, J[g % 2][:, P:2 * P],
                                               ALU.add, ALU.mult).then_inc(s_j, 1)

        def sp_dup0(n, b):
            sp.wait_ge(s_j, 12 * n + 4)
            sp.dma_start(KX0[b][HD:P, :, 0, :].bitcast(F32), KX0[b][0:HD, :, 0, :].bitcast(F32))\
                .then_inc(s_kdup, 16)
            sp.dma_start(KX0[b][0:HD, :, 1, :].bitcast(F32), KX0[b][HD:P, :, 1, :].bitcast(F32))\
                .then_inc(s_kdup, 16)

        def sp_bias(n, b, h):
            if b == 0:
                wait(sp, s_bias, n + h)
                sp.dma_start(HK[:], bass.AP(ext_dram.tensor, EXT * (n + h) + CLIP + 1 - P,
                                            [[1, P], [1, 384]])).then_inc(s_hk, 16)
            else:
                wait(sp, s_sdone, CHUNKS * (n - 1) + CHUNKS // 2 * (h + 1))
                sp.dma_start(BIAS[:, h, :], bass.AP(cum_dram.tensor, SEQ * (n - 1 + h),
                                                    [[0, P], [1, SEQ]])).then_inc(s_ck[h], 16)

        def pool_bias(q):
            n, h = q // 2, q % 2
            a = n + h
            wait(pool, s_sdone, CHUNKS // 2 * (q - 1))
            nc.gpsimd.memset(BIAS[:, h, 0:2 * P], 0.0).then_inc(s_biasp, 1)
            pool.wait_ge(s_hk, 16 * (a + 1))
            nc.gpsimd.tensor_scalar(BIAS[:, h, 2 * P:EXT], HK[:, ::-1], -1.0, None, ALU.mult)
            pool.wait_ge(s_biasp, 3 * a + 1)
            nc.gpsimd.tensor_scalar(BIAS[:, h, 0:2 * P], BIAS[:, h, 0:2 * P], relc[:, a:a + 1], None,
                                    ALU.subtract).then_inc(s_biasp, 1)
            pool.wait_ge(s_biasp, 3 * a + 2)
            nc.gpsimd.memset(BIAS[HD:P, h, 0:HD], BIG).then_inc(s_biasp, 1)
            pool.wait_ge(s_biasp, 3 * a + 3)
            nc.gpsimd.memset(BIAS[0:HD, h, EXT - HD:EXT], BIG).then_inc(s_bias, 1)
            pool.wait_ge(s_bias, a + 1)

        TB = NT // BATCHES

        with nc.Block() as block:
            @block.sync
            def _(_sp):
                for i in range(NT):
                    sp.dma_start(xt0[:, i, :], x[P * i:P * i + P, :]).then_inc(s_x[i], 16)
                load_w(0, qk_blocks(0, 0))
                sp.dma_start(Wf[:], w_in_0[:, F_COL:F_COL + 8].rearrange("(k p) c -> p k c", p=P))\
                    .then_inc(s_small, 16)
                sp.dma_start(extrow[:, 0:2 * CLIP + 1], rel_bias_0).then_inc(s_small, 16)
                sp.dma_start(relc[:], bass.AP(rel_bias_0.tensor, rel_bias_0.offset + 2 * CLIP,
                                              [[0, P], [2 * CLIP + 1, 8]]),
                             allow_slow_non_contiguous=True).then_inc(s_small, 16)
                sp.dma_start(fb[:], f_bias_0.rearrange("(h o) -> h o", o=1)).then_inc(s_small, 16)
                sp.dma_start(sinkc[:], bass.AP(sinks_1.tensor, sinks_1.offset, [[0, P], [1, HEADS]]))\
                    .then_inc(s_small, 16)
                load_w(1, vg_blocks(0, 0))
                sp.wait_ge(s_extf, 2)
                sp.dma_start(ext_dram, extrow[:]).then_inc(s_ext, 16)
                sp.wait_ge(s_ext, 16)
                sp.wait_ge(s_idr, 2)
                sp_bias(0, 0, 0)
                load_w(2, qk_blocks(1, 1))
                sp_dup0(0, 0)
                load_w(3, vg_blocks(1, 1))
                sp.wait_ge(s_fd, 5)
                sp.dma_start(cum_dram, fl[:]).then_inc(s_cum, 16)
                sp.wait_ge(s_cum, 16)

            @block.gpsimd
            def _(_pool):
                split_w(pool, 0, None)
                pool.wait_ge(s_small, 16 * 5)
                nc.gpsimd.memset(extrow[:, 513:EXT], 0.0).then_inc(s_extf, 1)
                pool.wait_ge(s_extf, 1)
                nc.gpsimd.tensor_scalar(extrow[:, 513:EXT], extrow[:, 513:EXT], extrow[:, 512:513], None,
                                        ALU.add).then_inc(s_extf, 1)
                nc.gpsimd.tensor_copy(WfR[:, HI], Wf[:]).then_inc(s_wf, 1)
                pool.wait_ge(s_wf, 1)
                nc.gpsimd.tensor_tensor(WfR[:, LO], Wf[:], WfR[:, HI].bitcast(F32),
                                        ALU.subtract).then_inc(s_wf, 1)
                split_w(pool, 1, None)
                split_w(pool, 2, 4)
                pool.wait_ge(s_hn, NT)
                pool_bias(0)

            @block.scalar
            def _(_act):
                act.dma_start(ident[:], c_ident).then_inc(s_const, 16)
                act.dma_start(trif, c_causal).then_inc(s_const, 16)
                act.dma_start(GB[:], bass.AP(norm_0.tensor, norm_0.offset, [[0, P], [1, DM]]))\
                    .then_inc(s_const, 16)

                def squares(i):
                    act.wait_ge(s_x[i], 16)
                    wait(act, s_square, i)
                    nc.scalar.activation(junk[:], xt0[:, i, :], ACT.Square,
                                         accum_out=ss[:, i:i + 1]).then_inc(s_square, 1)

                def root(n):
                    act.wait_ge(s_var, n + 1)
                    nc.scalar.activation(sd[:, TB * n:TB * n + TB], var[:, TB * n:TB * n + TB], ACT.Sqrt)\
                        .then_inc(s_sqrt, 1)

                def hi(i):
                    for c in range(2):
                        act.wait_ge(s_ht, 2 * i + c + 1)
                        nc.scalar.activation(hT0[:, HI, 4 * c:4 * c + 4, P * i:P * i + P],
                                             T[c][:].rearrange("p (k t) -> p k t", k=4),
                                             ACT.Copy).then_inc(s_hthi, 1)

                for n in range(BATCHES):
                    for i in range(TB * n, TB * n + TB):
                        squares(i)
                    for i in range(max(TB * (n - 1) - 1, 0), TB * n - 1):
                        hi(i)
                    root(n)
                for i in range(NT - TB - 1, NT):
                    hi(i)
                act.wait_ge(s_const, 48)
                nc.scalar.activation(identR[:], ident[:], ACT.Copy).then_inc(s_idr, 1)
                nc.scalar.activation(triR[:], trif, ACT.Copy).then_inc(s_idr, 1)
                act.wait_ge(s_hn, NT)
                for g in range(2):
                    act_group0(g, 0, 0)
                act.wait_ge(s_fd, 2)
                nc.scalar.activation(fe[:], fa[:], ACT.Exp).then_inc(s_fa, 1)
                act.wait_ge(s_fa, 1)
                nc.scalar.activation(fa[:], fe[:], ACT.Ln, bias=1.0).then_inc(s_fa, 1)
                for g in range(2, 12):
                    act_group0(g, 0, 0)

            @block.vector
            def _(_dve):
                dve.wait_ge(s_const, 48)

                def chain(n):
                    a = slice(TB * n, TB * n + TB)
                    dve.wait_ge(s_square, TB * n + TB)
                    nc.vector.tensor_scalar(var[:, a], ss[:, a], 1.0 / DM, EPS, ALU.mult, ALU.add)\
                        .then_inc(s_var, 1)
                    dve.wait_ge(s_sqrt, n + 1)
                    rsqrt_chain(a, n)

                def normed(i):
                    wait(dve, s_ht, 2 * i - 2)
                    nc.vector.scalar_tensor_tensor(HN[:, i % 2, :], xt0[:, i, :], rstd[:, i:i + 1], GB[:],
                                                   ALU.mult, ALU.mult).then_inc(s_hn, 1)

                def lo(i):
                    for c in range(2):
                        dve.wait_ge(s_hthi, 2 * i + c + 1)
                        nc.vector.tensor_tensor(hT0[:, LO, 4 * c:4 * c + 4, P * i:P * i + P],
                                                T[c][:].rearrange("p (k t) -> p k t", k=4),
                                                hT0[:, HI, 4 * c:4 * c + 4, P * i:P * i + P].bitcast(F32),
                                                ALU.subtract).then_inc(s_htlo, 1)

                for n in range(BATCHES):
                    chain(n)
                    for i in range(TB * n, TB * n + TB):
                        normed(i)
                        if i >= 1:
                            lo(i - 1)
                lo(NT - 1)
                for g in range(2):
                    dve_group0(g, 0, 0)
                for c in range(2):
                    dve.wait_ge(s_f, c + 1)
                    ins = nc.vector.tensor_scalar(fz[:, HALF * c:HALF * c + HALF], S[c][0:8, :], fb[:, 0:1],
                                                  None, ALU.add)
                ins.then_inc(s_fd, 1)
                dve.wait_ge(s_fd, 1)
                nc.vector.scalar_tensor_tensor(fa[:], fz[:], -1.0, fz[:], ALU.mult, ALU.min).then_inc(s_fd, 1)
                dve.wait_ge(s_fa, 2)
                nc.vector.scalar_tensor_tensor(fe[:], fz[:], 0.0, fa[:], ALU.min, ALU.subtract)\
                    .then_inc(s_fd, 1)
                dve.wait_ge(s_fd, 3)
                nc.vector.memset(fz[:], 1.0).then_inc(s_fd, 1)
                dve.wait_ge(s_fd, 4)
                nc.vector.tensor_tensor_scan(fl[:], fz[:], fe[:], 0.0, ALU.mult, ALU.add).then_inc(s_fd, 1)
                for g in range(2, 12):
                    dve_group0(g, 0, 0)

            @block.tensor
            def _(_pe):
                pe.wait_ge(s_const, 48)
                for i in range(NT):
                    pe.wait_ge(s_hn, i + 1)
                    for c in range(2):
                        if i >= 1:
                            pe.wait_ge(s_htlo, 2 * i - 1 + c)
                        for k in range(4):
                            mm = nc.tensor.transpose(T[c][:, P * k:P * k + P],
                                                     HN[:, i % 2, P * (4 * c + k):P * (4 * c + k) + P],
                                                     ident[:])
                        mm.then_inc(s_ht, 1)
                    if i >= NT // 2:
                        m = PER // 2 * (i % 2)
                        if i == NT // 2:
                            pe.wait_ge(s_htlo, NT)
                        pe_group0((i - NT // 2) // 2, 0, 1, m, m + PER // 2)
                pe.wait_ge(s_htlo, 2 * NT)
                pe.wait_ge(s_wf, 2)
                for c in range(2):
                    for m in range(PER):
                        k, (a, b) = m // len(TERMS), TERMS[m % len(TERMS)]
                        mm = nc.tensor.matmul(S[c][0:8, :], WfR[:, a, k, :],
                                              hT0[:, b, k, HALF * c:HALF * c + HALF],
                                              start=(m == 0), stop=(m == PER - 1))
                    mm.then_inc(s_f, 1)
                for g in range(2, 12):
                    pe_group0(g, 0, 1, 0, PER)

        KIND = "AB"

        def step_back(n, b, slot, lag, first):
            if slot >= lag:
                return (n, b, slot - lag) if slot - lag < 2 * NT else None
            return None if first else (n - 1, 1 - b, 2 * NT + slot - lag)

        def pe_window0(n, b, first, last):
            def scores(n, b, s):
                kind, h, i = KIND[b], s // NT, s % NT
                k0, nk = key_tiles(kind, i)
                if s == 0:
                    pe.wait_ge(s_kdup, 32 * n + 32)
                    pe.wait_ge(s_j, 12 * n + 4)
                for e, (j0, nj) in enumerate(STEPS[kind][s]):
                    c = chunk0(kind, s) + e
                    wait(pe, s_sdone, CHUNKS * n + c - 2)
                    o = S[c % 3][:, 0:P * nj]
                    q = QZ0[b][:, h, P * i:P * i + P]
                    diagonal = kind == "B" and j0 + nj == nk
                    for hl in range(2):
                        mm = nc.tensor.matmul(o, q, KX0[b][:, hl, h, P * (k0 + j0):P * (k0 + j0 + nj)],
                                              start=(hl == HI), stop=(hl == LO and not diagonal))
                    if diagonal:
                        mm = nc.tensor.matmul(S[c % 3][:, P * (nj - 1):P * nj], identR[:], triR[:],
                                              start=False, stop=True)
                    mm.then_inc(s_scores, 1)

            def transposes(n, b, s):
                kind = KIND[b]
                pe.wait_ge(s_probs, 2 * NT * n + s + 1)
                for e, (j0, nj) in enumerate(STEPS[kind][s]):
                    c = chunk0(kind, s) + e
                    wait(pe, s_lo, CHUNKS * n + c - 1)
                    for t in range(nj):
                        mm = nc.tensor.transpose(T[c % 2][:, P * t:P * t + P],
                                                 L[:, s % 2, P * (j0 + t):P * (j0 + t) + P], ident[:])
                    mm.then_inc(s_tr, 1)

            def times_v(n, b, s):
                kind, h, i = KIND[b], s // NT, s % NT
                k0, nk = key_tiles(kind, i)
                pe.wait_ge(s_j, 12 * n + 5 + i)
                wait(pe, s_y, 2 * NT * n + s)
                for e, (j0, nj) in enumerate(STEPS[kind][s]):
                    c = chunk0(kind, s) + e
                    pe.wait_ge(s_lo, CHUNKS * n + c + 1)
                    for t in range(nj):
                        for pa in range(2):
                            mm = nc.tensor.matmul(PV[:, 0:P], PT[c % 2][:, pa, P * t:P * t + P],
                                                  V0[b][:, k0 + j0 + t, :, HD * h:HD * h + HD],
                                                  start=(j0 + t == 0 and pa == HI),
                                                  stop=(j0 + t == nk - 1 and pa == LO))
                    mm.then_inc(s_pv, 1)

            def project(slot, part):
                if last:
                    return
                if slot < NT:
                    m0 = PER // 4 * (2 * (slot % 2) + part)
                    pe_group0(slot // 2, 12 * (n + 1), 2 * (n + 1) + 1, m0, m0 + PER // 4)
                else:
                    m0 = PER // 2 * part
                    pe_group0(4 + slot - NT, 12 * (n + 1), 2 * (n + 1) + 1, m0, m0 + PER // 2)

            for slot in range(2 * NT + (2 if last else 0)):
                if slot < 2 * NT:
                    scores(n, b, slot)
                    project(slot, 0)
                step = step_back(n, b, slot, 2, first)
                if step:
                    times_v(*step)
                step = step_back(n, b, slot, 1, first)
                if step:
                    transposes(*step)
                if slot < 2 * NT:
                    project(slot, 1)

        def act_window0(n, b, first, last):
            def exps(n, b, s):
                kind = KIND[b]
                nk = key_tiles(kind, s % NT)[1]
                act.wait_ge(s_sdone, CHUNKS * n + chunk0(kind, s + 1))
                nc.scalar.activation(L[:, s % 2, 0:P * nk], L[:, s % 2, 0:P * nk], ACT.Exp,
                                     bias=negm[:, s % 4, 0:1], scale=-1.0,
                                     accum_out=rs[:, s % 4, 0:1]).then_inc(s_probs, 1)

            def hi(n, b, s):
                kind = KIND[b]
                for e, (j0, nj) in enumerate(STEPS[kind][s]):
                    c = chunk0(kind, s) + e
                    act.wait_ge(s_tr, CHUNKS * n + c + 1)
                    wait(act, s_pv, CHUNKS * n + c - 1)
                    nc.scalar.activation(PT[c % 2][:, HI, 0:P * nj], T[c % 2][:, 0:P * nj],
                                         ACT.Copy).then_inc(s_hi, 1)

            for slot in range(2 * NT + (2 if last else 0)):
                if slot == 0 and not first:
                    act_group0(11, 12 * n, b)
                if not last and ended_group(slot) is not None:
                    act_group0(ended_group(slot), 12 * (n + 1), 1 - b)
                step = step_back(n, b, slot, 1, first)
                if step and last:
                    hi(*step)
                if slot < 2 * NT:
                    exps(n, b, slot)
                if step and not last:
                    hi(*step)
                if last and 0 <= slot - WO0_SLOT < len(WO0_OTHERS):
                    act_wo(Wo0, WO0_OTHERS[slot - WO0_SLOT], 0)

        def dve_holds_wait(n):
            if not isinstance(n, int):
                nc.vector.memset(held[:], 0.0)

        def dve_window0(n, b, first, last):
            def rows(n, b, s):
                kind, h, i = KIND[b], s // NT, s % NT
                nk = key_tiles(kind, i)[1]
                if i == 0:
                    if kind == "A":
                        dve.wait_ge(s_bias, n + h + 1)
                    else:
                        dve.wait_ge(s_ck[h], 8 * n + 8)
                before = chunk0(kind, s - 1) if s >= 2 else \
                    chunk0(KIND[1 - b], 2 * NT + s - 1) - CHUNKS
                wait(dve, s_tr, CHUNKS * n + before)
                b0 = EXT - P * nk if kind == "A" else 0
                for e, (j0, nj) in enumerate(STEPS[kind][s]):
                    c = chunk0(kind, s) + e
                    final = e == len(STEPS[kind][s]) - 1
                    dve.wait_ge(s_scores, CHUNKS * n + c + 1)
                    if e == 1:
                        dve.wait_ge(s_sdone, CHUNKS * n + c)
                    dve_holds_wait(n)
                    nc.vector.tensor_tensor_reduce(
                        out=L[:, s % 2, P * j0:P * (j0 + nj)], in0=S[c % 3][:, 0:P * nj],
                        in1=BIAS[:, h, b0 + P * j0:b0 + P * (j0 + nj)], scale=1.0,
                        scalar=nmpart[:] if e == 1 else 3e38, op0=ALU.add, op1=ALU.min,
                        accum_out=negm[:, s % 4, 0:1] if final else nmpart[:]).then_inc(s_sdone, 1)

            def lo(n, b, s):
                kind = KIND[b]
                dve.wait_ge(s_probs, 2 * NT * n + s + 1)
                nc.vector.reciprocal(rinv[:, s % 4, 0:1], rs[:, s % 4, 0:1]).then_inc(s_rinv, 1)
                for e, (j0, nj) in enumerate(STEPS[kind][s]):
                    c = chunk0(kind, s) + e
                    dve.wait_ge(s_hi, CHUNKS * n + c + 1)
                    nc.vector.tensor_tensor(PT[c % 2][:, LO, 0:P * nj], T[c % 2][:, 0:P * nj],
                                            PT[c % 2][:, HI, 0:P * nj].bitcast(F32),
                                            ALU.subtract).then_inc(s_lo, 1)

            def gated(n, b, s):
                kind, h, i = KIND[b], s // NT, s % NT
                st = 2 * NT * n + s
                dve.wait_ge(s_pv, CHUNKS * n + chunk0(kind, s + 1))
                nc.vector.tensor_reduce(ysum[:, 0:HD], PV[:, 0:P].rearrange("p (x d) -> p d x", x=2),
                                        mybir.AxisListType.X, ALU.add).then_inc(s_ysum, 1)
                if h == 0:
                    wait(dve, s_yst[i], 16 * n)
                dve.wait_ge(s_rinv, st + 1)
                dve.wait_ge(s_ysum, st + 1)
                nc.vector.scalar_tensor_tensor(Y[:, i, HD * h:HD * h + HD], ysum[:, 0:HD],
                                               rinv[:, s % 4, 0:1],
                                               SG0[b][:, i, HD * h:HD * h + HD],
                                               ALU.mult, ALU.mult).then_inc(s_y, 1)

            for slot in range(2 * NT + (2 if last else 0)):
                step = step_back(n, b, slot, 3, first)
                if step and (slot == 0 or not last):
                    gated(*step)
                if slot < 2 * NT:
                    rows(n, b, slot)
                step = step_back(n, b, slot, 2, first)
                if step and last:
                    gated(*step)
                if slot == 0 and not first:
                    dve_group0(11, 12 * n, b)
                if not last and ended_group(slot) is not None:
                    dve_group0(ended_group(slot), 12 * (n + 1), 1 - b)
                step = step_back(n, b, slot, 1, first)
                if step:
                    lo(*step)
                if last and 0 <= slot - WO0_SLOT - 1 < len(WO0_OTHERS):
                    dve_wo(Wo0, WO0_OTHERS[slot - WO0_SLOT - 1], 0)

        def load_y(layer, i):
            sp.wait_ge(s_yst[i], 16 * PAIRS * (layer + 1))
            sp.dma_start(YT[:, i % 2, :], y_dram[layer, P * i:P * i + P, :]).then_inc(s_yt[i % 2], 16)

        WO0_POOL, WO0_OTHERS = (0, 1, 2, 3, 4), (5, 6, 7)
        WO1_POOL, WO1_OTHERS = (4, 5, 3), (6, 7, 0, 1, 2)
        WO0_SLOT = NT

        def act_wo(Wo, k, layer):
            act.wait_ge(s_wor[k // 2], 16 * (layer + 1))
            nc.scalar.activation(Wo[:, HI, k, :], WoRaw[:, k, :], ACT.Copy).then_inc(s_wohi[k], 1)

        def dve_wo(Wo, k, layer):
            dve.wait_ge(s_wohi[k], layer + 1)
            nc.vector.tensor_tensor(Wo[:, LO, k, :], WoRaw[:, k, :], Wo[:, HI, k, :].bitcast(F32),
                                    ALU.subtract).then_inc(s_wolo[k], 1)

        def pool_wo(Wo, k, layer):
            pool.wait_ge(s_wor[k // 2], 16 * (layer + 1))
            nc.gpsimd.tensor_copy(Wo[:, HI, k, :], WoRaw[:, k, :]).then_inc(s_wohi[k], 1)
            pool.wait_ge(s_wohi[k], layer + 1)
            nc.gpsimd.tensor_tensor(Wo[:, LO, k, :], WoRaw[:, k, :], Wo[:, HI, k, :].bitcast(F32),
                                    ALU.subtract).then_inc(s_wolo[k], 1)

        def sp_wo(w_out, q):
            sp.dma_start(WoRaw[:, 2 * q:2 * q + 2, :],
                         w_out[2 * P * q:2 * P * q + 2 * P, :].rearrange("(k p) n -> p k n", p=P))\
                .then_inc(s_wor[q], 16)

        def rounds(eng, window):
            window(0, 0, True, False)
            window(1, 1, False, False)
            with eng.Fori(1, HALF_PAIRS - 1) as a:
                window(2 * a, 0, False, False)
                window(2 * a + 1, 1, False, False)
            window(PAIRS - 2, 0, False, False)
            window(PAIRS - 1, 1, False, True)

        def sp_window0(n, b, first, last):
            if comes_before(n, PAIRS - 2):
                load_w(2 * n + 4, qk_blocks(n + 2, b))
            if not last:
                sp_bias(n + 1, 1 - b, 0)
                sp_dup0(n + 1, 1 - b)
            if comes_before(n, PAIRS - 2):
                load_w(2 * n + 5, vg_blocks(n + 2, b))
            if is_window(n, PAIRS - 2):
                sp.wait_ge(s_proj, GRP1 - 8)
                sp_wo(w_out_0, 0)
                sp_wo(w_out_0, 1)
            if last:
                sp.wait_ge(s_proj, GRP1)
                sp_wo(w_out_0, 2)
                sp_wo(w_out_0, 3)
                sp.wait_ge(s_w, BLK1)
            for i in range(NT):
                if last and i in (3, 4):
                    load_y(0, i - 3)
                sp.wait_ge(s_y, 2 * NT * n + NT + i + 1)
                store_y(0, n, b, i)
            if not last:
                sp_bias(n + 1, 1 - b, 1)

        with nc.Block() as block:
            @block.tensor
            def _(_pe):
                rounds(pe, pe_window0)

            @block.scalar
            def _(_act):
                rounds(act, act_window0)

            @block.vector
            def _(_dve):
                rounds(dve, dve_window0)

            @block.sync
            def _(_sp):
                sp_bias(0, 0, 1)
                rounds(sp, sp_window0)

            @block.gpsimd
            def _(_pool):
                pool_bias(1)
                split_w(pool, 3, 12)
                for n in range(PAIRS):
                    if n % 2 == 1 and n + 1 < PAIRS:
                        pool_bias(2 * n + 2)
                    if 2 * n + 4 < 2 * PAIRS:
                        split_w(pool, 2 * n + 4, 12 * (n + 1) + 4)
                    if n % 2 == 1 and n + 1 < PAIRS:
                        pool_bias(2 * n + 3)
                    if 2 * n + 5 < 2 * PAIRS:
                        split_w(pool, 2 * n + 5, 12 * (n + 1) + 12)
                pool.wait_ge(s_proj, GRP1)
                for k in WO0_POOL:
                    pool_wo(Wo0, k, 0)

        LEAD = 4
        EARLY = 2

        def pe_group1(m, wslot, tile, part):
            for r in range(PER // 2 * part, PER // 2 * (part + 1)):
                k, (a, b) = r // len(TERMS), TERMS[r % len(TERMS)]
                if r == 0:
                    pe.wait_ge(s_j, GRP1 + m - 1)
                mm = nc.tensor.matmul(J[tile % 2][:, 0:2 * P], hT1[:, a, k, P * tile:P * tile + P],
                                      Wslot[wslot][:, b, k, :], start=(r == 0), stop=(r == PER - 1))
                if r == PER - 1:
                    mm.then_inc(s_proj, 1)

        def out_phase(layer, Wo, w_norm, residual):
            b16, b8 = 16 * layer, 8 * layer
            last = layer == 1

            with nc.Block() as block:
                @block.tensor
                def _(_pe):
                    def y_transposes(i):
                        pe.wait_ge(s_yt[i % 2], 16 * (4 * layer + i // 2 + 1))
                        for c in range(2):
                            if i >= 1:
                                pe.wait_ge(s_ytlo, b16 + 2 * i - 1 + c)
                            for k in range(4):
                                mm = nc.tensor.transpose(T[c][:, P * k:P * k + P],
                                                         YT[:, i % 2, P * (4 * c + k):P * (4 * c + k) + P],
                                                         ident[:])
                            mm.then_inc(s_ytr, 1)

                    def product(i, c):
                        if c == 0:
                            pe.wait_ge(s_ytlo, b16 + 2 * i + 2)
                        if i >= 1:
                            pe.wait_ge(s_jo, b16 + 2 * i - 1 + c)
                        for k in range(NK):
                            if i == 0 and c == 0:
                                pe.wait_ge(s_wolo[k], layer + 1)
                            for n, (a, b) in enumerate(TERMS):
                                mm = nc.tensor.matmul(J[c][:], yT[i % 2][:, a, k, :],
                                                      Wo[:, b, k, HALF * c:HALF * c + HALF],
                                                      start=(k == 0 and n == 0),
                                                      stop=(k == NK - 1 and n == 2))
                        mm.then_inc(s_mm, 1)

                    def h_transposes(i):
                        pe.wait_ge(s_hn, 8 + i + 1)
                        for c in range(2):
                            if i >= 1:
                                pe.wait_ge(s_htlo, 16 + 2 * i - 1 + c)
                            for k in range(4):
                                mm = nc.tensor.transpose(S[c][:, P * k:P * k + P],
                                                         HN1[:, i % 2, P * (4 * c + k):P * (4 * c + k) + P],
                                                         ident[:])
                            mm.then_inc(s_ht, 1)

                    for j in range(NT + 2):
                        if j < NT:
                            y_transposes(j)
                        if 1 <= j <= NT:
                            product(j - 1, 0)
                            product(j - 1, 1)
                        if j == NT + 1 and not last:
                            pe.wait_ge(s_w, BLK1 + 1)
                            pe.wait_ge(s_jo, 2 * NT)
                            pe.wait_ge(s_htlo, 2 * NT + 2 * EARLY)
                            for m in range(EARLY):
                                pe_group1(m, 0, m, 0)
                                pe_group1(m, 0, m, 1)
                        if j >= 2 and not last:
                            h_transposes(j - 2)

                @block.scalar
                def _(_act):
                    for j in range(NT + 2):
                        if j < NT:
                            if j >= 2:
                                act.wait_ge(s_mm, b16 + 2 * j - 2)
                            for c in range(2):
                                act.wait_ge(s_ytr, b16 + 2 * j + c + 1)
                                nc.scalar.activation(yT[j % 2][:, HI, 4 * c:4 * c + 4, :],
                                                     T[c][:].rearrange("p (k t) -> p k t", k=4),
                                                     ACT.Copy).then_inc(s_ythi, 1)
                        if j >= 2 and not last:
                            i = j - 2
                            for c in range(2):
                                act.wait_ge(s_ht, 16 + 2 * i + c + 1)
                                nc.scalar.activation(hT1[:, HI, 4 * c:4 * c + 4, P * i:P * i + P],
                                                     S[c][:].rearrange("p (k t) -> p k t", k=4),
                                                     ACT.Copy).then_inc(s_hthi, 1)
                        if 1 <= j <= NT:
                            i = j - 1
                            act.wait_ge(s_jo, b16 + 2 * i + 2)
                            if not last:
                                act.dma_start(x1_dram[P * i:P * i + P, :], X1[:, i % 2, :])\
                                    .then_inc(s_st[i % 2], 16)
                            if i >= 2 and last:
                                act.wait_ge(s_ot[i % 2], 16 * (i // 2))
                            nc.scalar.activation(HN1[:, i % 2, :], X1[:, i % 2, :], ACT.Square,
                                                 accum_out=ss[:, i:i + 1]).then_inc(s_square, 1)
                            act.wait_ge(s_var, BATCHES + b8 + i + 1)
                            nc.scalar.activation(sd[:, i:i + 1], var[:, i:i + 1], ACT.Sqrt)\
                                .then_inc(s_sqrt, 1)

                @block.vector
                def _(_dve):
                    for j in range(NT + 2):
                        if j < NT:
                            for c in range(2):
                                dve.wait_ge(s_ythi, b16 + 2 * j + c + 1)
                                nc.vector.tensor_tensor(yT[j % 2][:, LO, 4 * c:4 * c + 4, :],
                                                        T[c][:].rearrange("p (k t) -> p k t", k=4),
                                                        yT[j % 2][:, HI, 4 * c:4 * c + 4, :].bitcast(F32),
                                                        ALU.subtract).then_inc(s_ytlo, 1)
                        if 1 <= j <= NT:
                            i = j - 1
                            dve.wait_ge(s_xr[i % 2], 16 * (4 * layer + i // 2 + 1))
                            if i >= 2 and not last:
                                dve.wait_ge(s_st[i % 2], 16 * (i // 2))
                            for c in range(2):
                                dve.wait_ge(s_mm, b16 + 2 * i + c + 1)
                                nc.vector.tensor_tensor(X1[:, i % 2, HALF * c:HALF * c + HALF], J[c][:],
                                                        XR[:, i % 2, HALF * c:HALF * c + HALF],
                                                        ALU.add).then_inc(s_jo, 1)
                        if j >= 2 and not last:
                            i = j - 2
                            for c in range(2):
                                dve.wait_ge(s_hthi, 16 + 2 * i + c + 1)
                                nc.vector.tensor_tensor(hT1[:, LO, 4 * c:4 * c + 4, P * i:P * i + P],
                                                        S[c][:].rearrange("p (k t) -> p k t", k=4),
                                                        hT1[:, HI, 4 * c:4 * c + 4, P * i:P * i + P]
                                                        .bitcast(F32), ALU.subtract).then_inc(s_htlo, 1)
                        if 1 <= j <= NT:
                            i = j - 1
                            dve.wait_ge(s_square, 8 + b8 + i + 1)
                            nc.vector.tensor_scalar(var[:, i:i + 1], ss[:, i:i + 1], 1.0 / DM, EPS,
                                                    ALU.mult, ALU.add).then_inc(s_var, 1)
                            dve.wait_ge(s_sqrt, BATCHES + b8 + i + 1)
                            rsqrt_chain(slice(i, i + 1), BATCHES + b8 + i)
                            if i == 0:
                                dve.wait_ge(s_gb, 16 * (layer + 1))
                            if i >= 2 and not last:
                                dve.wait_ge(s_ht, 16 + 2 * i - 2)
                            nc.vector.scalar_tensor_tensor(HN1[:, i % 2, :], X1[:, i % 2, :],
                                                           rstd[:, i:i + 1], GB1[:], ALU.mult,
                                                           ALU.mult).then_inc(s_hn, 1)

                @block.sync
                def _(_sp):
                    def loads(i):
                        if i >= 2:
                            sp.wait_ge(s_ytr, b16 + 2 * i - 2)
                            load_y(layer, i)
                            sp.wait_ge(s_jo, b16 + 2 * i - 2)
                        sp.dma_start(XR[:, i % 2, :], residual[P * i:P * i + P, :])\
                            .then_inc(s_xr[i % 2], 16)

                    loads(0)
                    loads(1)
                    for i in range(NT):
                        sp.wait_ge(s_yst[i], 16 * PAIRS * (layer + 1))
                    sp.dma_start(GB1[:], bass.AP(w_norm.tensor, w_norm.offset, [[0, P], [1, DM]]))\
                        .then_inc(s_gb, 16)
                    if not last:
                        load_w(BLK1, [cols(w_in_1, KC), cols(w_in_1, VC)])
                    for i in range(2, NT):
                        loads(i)
                    if not last:
                        sp.dma_start(WM, c_window).then_inc(s_rope_c, 16)
                        sp.wait_ge(s_mm, 2 * NT)
                        sp.dma_start(ROPE[:], c_rope.rearrange("(t p) c d -> p t c d", p=P))\
                            .then_inc(s_rope_c, 16)
                    for b in range(2):
                        sp.wait_ge(s_ot[b] if last else s_st[b], 16 * 4)

                @block.gpsimd
                def _(_pool):
                    if not last:
                        split_w(pool, BLK1, GRP1)
                    for i in range(NT if last else 0):
                        pool.wait_ge(s_hn, 16 + i + 1)
                        pool.dma_start(out[P * i:P * i + P, :], HN1[:, i % 2, :]).then_inc(s_ot[i % 2], 16)

        out_phase(0, Wo0, norm_1, x)

        def pe_rotated(m, tile):
            pe.wait_ge(s_rope, m + 1)
            wait(pe, s_qlo, m)
            nc.tensor.transpose(T[1][:, 0:P], QR[:, tile % 2, :], ident[:]).then_inc(s_qt, 1)

        def act_group1(m, tile, b):
            act.wait_ge(s_proj, GRP1 + m + 1)
            if b is None:
                nc.scalar.activation(V1[:, tile, HI, :], J[tile % 2][:, P:2 * P], ACT.Copy, scale=0.5)\
                    .then_inc(s_jhi, 1)
            else:
                nc.scalar.activation(SG1[b][:, tile, :], J[tile % 2][:, P:2 * P], ACT.Tanh, scale=0.5)\
                    .then_inc(s_jhi, 1)

        def act_rotated(m, tile, b):
            act.wait_ge(s_qt, m + 1)
            tok = slice(P * tile, P * tile + P)
            for h in range(2):
                own = slice(HD * h, HD * h + HD)
                if b is None:
                    ins = nc.scalar.activation(KX1[own, HI, h, tok], T[1][own, 0:P], ACT.Copy)
                else:
                    ins = nc.scalar.activation(QZ1[b][own, h, tok], T[1][own, 0:P], ACT.Copy,
                                               scale=-0.125)
            ins.then_inc(s_qhi, 1)

        def dve_group1(m, tile, b):
            dve.wait_ge(s_jhi, GRP1 + m + 1)
            wait(dve, s_qt, m - 1)
            heads = J[tile % 2][:, 0:P].rearrange("p (h d) -> p h d", h=2)
            halves = J[tile % 2][:, 0:P].rearrange("p (h s d) -> p h s d", h=2, s=2)
            cos = ROPE[:, tile, 0, :].rearrange("p (o d) -> p o d", o=1).broadcast_to((P, 2, HD))
            sin = ROPE[:, tile, 1, :].rearrange("p (s d) -> p s d", s=2)
            q = QR[:, tile % 2, :]
            wait(dve, s_rope, m)
            nc.vector.tensor_tensor(q.rearrange("p (h d) -> p h d", h=2), heads, cos, ALU.mult)
            for h in range(2):
                ins = nc.vector.tensor_tensor(
                    QS[:, HD * h:HD * h + HD].rearrange("p (s d) -> p s d", s=2),
                    halves[:, h, ::-1, :], sin, ALU.mult)
            ins.then_inc(s_qr, 1)
            if b is None:
                nc.vector.scalar_tensor_tensor(V1[:, tile, LO, :], J[tile % 2][:, P:2 * P], 0.5,
                                               V1[:, tile, HI, :].bitcast(F32),
                                               ALU.mult, ALU.subtract).then_inc(s_j, 1)
            else:
                nc.vector.scalar_tensor_tensor(SG1[b][:, tile, :], SG1[b][:, tile, :], 1.0,
                                               J[tile % 2][:, P:2 * P], ALU.add, ALU.mult)\
                    .then_inc(s_j, 1)
            dve.wait_ge(s_qr, m + 1)
            nc.vector.tensor_tensor(q, q, QS, ALU.add).then_inc(s_rope, 1)

        def dve_rotated(m, tile, b):
            dve.wait_ge(s_qhi, m + 1)
            tok = slice(P * tile, P * tile + P)
            for h in range(2):
                own = slice(HD * h, HD * h + HD)
                other = slice(HD - HD * h, P - HD * h)
                if b is None:
                    ins = nc.vector.tensor_tensor(KX1[own, LO, h, tok], T[1][own, 0:P],
                                                  KX1[own, HI, h, tok].bitcast(F32), ALU.subtract)
                else:
                    ins = nc.vector.scalar_tensor_tensor(
                        QZ1[b][other, h, tok], T[1][own, 0:P], -0.125,
                        QZ1[b][own, h, tok].bitcast(F32), ALU.mult, ALU.subtract)
            ins.then_inc(s_qlo, 1)

        LEADIN = NT + LEAD

        def group_of(n, b, s, ago, last):
            q = s + LEAD - ago
            if last and q >= NT:
                return None
            return NT + NT * n + q, q % NT, (b + q // NT) % 2

        def lead_group(v):
            return v, v % NT, None if v < NT else 0

        def back1(n, b, s, lag, first):
            if s >= lag:
                return (n, b, s - lag) if s - lag < NT else None
            return None if first else (n - 1, 1 - b, NT + s - lag)

        def pe_window1(n, b, first, last):
            def scores(n, b, s):
                k0, nk = key_tiles("C", s)
                pe.wait_ge(s_qlo, NT + NT * n + s + 1)
                wait(pe, s_sdone, CH1 + NT * n + s - 1)
                for h in range(2):
                    for hl in range(2):
                        mm = nc.tensor.matmul(S[s % 2][:, 2 * P * h:2 * P * h + P * nk],
                                              QZ1[b][:, h, P * s:P * s + P],
                                              KX1[:, hl, b, P * k0:P * (k0 + nk)],
                                              start=(hl == HI), stop=(hl == LO))
                mm.then_inc(s_scores, 1)

            def transposes(n, b, s):
                nk = key_tiles("C", s)[1]
                pe.wait_ge(s_probs, ST1 + NT * n + s + 1)
                pe.wait_ge(s_lo, CH1 + NT * n + s)
                for h in range(2):
                    for t in range(nk):
                        o = P * (nk * h + t)
                        mm = nc.tensor.transpose(T[0][:, o:o + P],
                                                 L[:, s % 2, 2 * P * h + P * t:2 * P * h + P * t + P],
                                                 ident[:])
                mm.then_inc(s_tr, 1)

            def times_v(n, b, s):
                k0, nk = key_tiles("C", s)
                pe.wait_ge(s_y, ST1 + NT * n + s)
                pe.wait_ge(s_lo, CH1 + NT * n + s + 1)
                for h in range(2):
                    for t in range(nk):
                        for pa in range(2):
                            mm = nc.tensor.matmul(PV[:, P * h:P * h + P],
                                                  PT[s % 2][:, pa, P * (nk * h + t):P * (nk * h + t) + P],
                                                  V1[:, k0 + t, :, HD * b:HD * b + HD],
                                                  start=(t == 0 and pa == HI), stop=(t == nk - 1 and pa == LO))
                mm.then_inc(s_pv, 1)

            for s in range(NT + (2 if last else 0)):
                group = group_of(n, b, s, 0, last)
                if s < NT:
                    scores(n, b, s)
                if group:
                    m, tile, buf = group
                    if tile == 0:
                        pe.wait_ge(s_w, BLK1 + 2 + n + s // LEAD)
                    pe_group1(m, 1 - buf, tile, 0)
                step = back1(n, b, s, 2, first)
                if step and last and s >= LEAD:
                    times_v(*step)
                step = back1(n, b, s, 1, first)
                if step:
                    transposes(*step)
                if group:
                    pe_group1(m, 1 - buf, tile, 1)
                step = back1(n, b, s, 2, first)
                if step and not (last and s >= LEAD):
                    times_v(*step)
                group = group_of(n, b, s, 1, last)
                if group:
                    pe_rotated(group[0], group[1])

        def act_window1(n, b, first, last):
            def exps(n, b, s):
                nk = key_tiles("C", s)[1]
                act.wait_ge(s_snm, NT * n + s + 1)
                for h in range(2):
                    r = L[:, s % 2, 2 * P * h:2 * P * h + P * nk]
                    nc.scalar.activation(r, r, ACT.Exp, bias=negm[:, s % 4, h:h + 1], scale=-1.0,
                                         accum_out=rs[:, s % 4, h:h + 1])
                nc.scalar.activation(es[:, s % 4, :], snm[:, s % 4, :], ACT.Exp).then_inc(s_probs, 1)

            def hi(n, b, s):
                nk = key_tiles("C", s)[1]
                act.wait_ge(s_tr, CH1 + NT * n + s + 1)
                act.wait_ge(s_pv, CH1 + NT * n + s - 1)
                nc.scalar.activation(PT[s % 2][:, HI, 0:2 * P * nk], T[0][:, 0:2 * P * nk],
                                     ACT.Copy).then_inc(s_hi, 1)

            for s in range(NT + (2 if last else 0)):
                group = group_of(n, b, s, 1, last)
                if group:
                    act_group1(*group)
                group = group_of(n, b, s, 2, last)
                if group:
                    act_rotated(*group)
                step = back1(n, b, s, 1, first)
                if step and last and s > LEAD:
                    hi(*step)
                if s < NT:
                    exps(n, b, s)
                if step and not (last and s > LEAD):
                    hi(*step)
                if last and 0 <= s - LEAD < len(WO1_OTHERS):
                    if s == LEAD:
                        act.wait_ge(s_proj, GRP1 + NT * (PAIRS + 1))
                    act_wo(Wo1, WO1_OTHERS[s - LEAD], 1)

        def dve_window1(n, b, first, last):
            def rows(n, b, s):
                nk = key_tiles("C", s)[1]
                if s == 0:
                    p = n + 7 * b
                    nc.vector.tensor_scalar(nsink[:, b, :], sinkc[:, bass.ds(p, 2)], -1.0, None, ALU.mult)\
                        .then_inc(s_nsk, 1)
                    dve.wait_ge(s_nsk, n + 1)
                wait(dve, s_tr, CH1 + NT * n + s - 1)
                dve.wait_ge(s_scores, CH1 + NT * n + s + 1)
                dve_holds_wait(n)
                for h in range(2):
                    ins = nc.vector.tensor_tensor_reduce(
                        out=L[:, s % 2, 2 * P * h:2 * P * h + P * nk],
                        in0=S[s % 2][:, 2 * P * h:2 * P * h + P * nk],
                        in1=WM[:, 2 * P - P * nk:2 * P], scale=1.0,
                        scalar=nsink[:, b, h:h + 1], op0=ALU.add, op1=ALU.min,
                        accum_out=negm[:, s % 4, h:h + 1])
                ins.then_inc(s_sdone, 1)
                dve.wait_ge(s_sdone, CH1 + NT * n + s + 1)
                nc.vector.tensor_tensor(snm[:, s % 4, :], negm[:, s % 4, :], nsink[:, b, :],
                                        ALU.subtract).then_inc(s_snm, 1)

            def lo(n, b, s):
                nk = key_tiles("C", s)[1]
                dve.wait_ge(s_probs, ST1 + NT * n + s + 1)
                nc.vector.tensor_tensor(rinv[:, s % 4, :], rs[:, s % 4, :], es[:, s % 4, :], ALU.add)\
                    .then_inc(s_tot, 1)
                dve.wait_ge(s_hi, CH1 + NT * n + s + 1)
                nc.vector.tensor_tensor(PT[s % 2][:, LO, 0:2 * P * nk], T[0][:, 0:2 * P * nk],
                                        PT[s % 2][:, HI, 0:2 * P * nk].bitcast(F32),
                                        ALU.subtract).then_inc(s_lo, 1)
                dve.wait_ge(s_tot, NT * n + s + 1)
                nc.vector.reciprocal(rinv[:, s % 4, :], rinv[:, s % 4, :]).then_inc(s_rinv, 1)

            def gated(n, b, s):
                st = ST1 + NT * n + s
                dve.wait_ge(s_pv, CH1 + NT * n + s + 1)
                nc.vector.tensor_reduce(ysum[:].rearrange("p (h d) -> p h d", h=2),
                                        PV[:, 0:2 * P].rearrange("p (h x d) -> p h d x", h=2, x=2),
                                        mybir.AxisListType.X, ALU.add).then_inc(s_ysum, 1)
                dve.wait_ge(s_yst[s], 16 * (PAIRS + n))
                dve.wait_ge(s_rinv, st + 1)
                dve.wait_ge(s_ysum, st + 1)
                for h in range(2):
                    ins = nc.vector.scalar_tensor_tensor(Y[:, s, HD * h:HD * h + HD],
                                                         ysum[:, HD * h:HD * h + HD],
                                                         rinv[:, s % 4, h:h + 1],
                                                         SG1[b][:, s, HD * h:HD * h + HD],
                                                         ALU.mult, ALU.mult)
                ins.then_inc(s_y, 1)

            for s in range(NT + (2 if last else 0)):
                group = group_of(n, b, s, 1, last)
                if group:
                    dve_group1(*group)
                if s < NT:
                    rows(n, b, s)
                group = group_of(n, b, s, 2, last)
                if group:
                    dve_rotated(*group)
                step = back1(n, b, s, 3, first)
                if step and (s <= LEAD or not last):
                    gated(*step)
                step = back1(n, b, s, 2, first)
                if step and s >= LEAD and last:
                    gated(*step)
                step = back1(n, b, s, 1, first)
                if step:
                    lo(*step)
                if last and 0 <= s - LEAD - 1 < len(WO1_OTHERS):
                    dve_wo(Wo1, WO1_OTHERS[s - LEAD - 1], 1)

        def sp_window1(n, b, first, last):
            if comes_before(n, PAIRS - 2):
                load_w(BLK1 + 3 + n, qg_blocks(n + 2, b))
            if last:
                sp.wait_ge(s_proj, GRP1 + NT * (PAIRS + 1))
                sp_wo(w_out_1, 0)
                sp_wo(w_out_1, 1)
                sp.wait_ge(s_w, BLK1 + 1 + PAIRS)
            for i in range(NT):
                if last and i in (3, 4):
                    load_y(1, i - 3)
                if is_window(n, PAIRS - 2) and i == LEAD:
                    sp.wait_ge(s_proj, GRP1 + NT * PAIRS)
                    sp_wo(w_out_1, 2)
                    sp_wo(w_out_1, 3)
                sp.wait_ge(s_y, ST1 + NT * n + i + 1)
                store_y(1, n, b, i)

        with nc.Block() as block:
            @block.tensor
            def _(_pe):
                pe.wait_ge(s_w, BLK1 + 1)
                for v in range(LEADIN):
                    if v == NT:
                        pe.wait_ge(s_w, BLK1 + 2)
                    for part in range(2 if v >= EARLY else 0):
                        pe_group1(v, v // NT, v % NT, part)
                    if v >= 1:
                        pe_rotated(v - 1, (v - 1) % NT)
                pe.wait_ge(s_kdup, 32 * PAIRS + 32)
                rounds(pe, pe_window1)

            @block.scalar
            def _(_act):
                for v in range(LEADIN):
                    if v >= 1:
                        act_group1(*lead_group(v - 1))
                    if v >= 2:
                        act_rotated(*lead_group(v - 2))
                rounds(act, act_window1)

            @block.vector
            def _(_dve):
                dve.wait_ge(s_rope_c, 32)
                for v in range(LEADIN):
                    if v >= 1:
                        dve_group1(*lead_group(v - 1))
                    if v >= 2:
                        dve_rotated(*lead_group(v - 2))
                rounds(dve, dve_window1)

            @block.sync
            def _(_sp):
                load_w(BLK1 + 1, qg_blocks(0, 0))
                load_w(BLK1 + 2, qg_blocks(1, 1))
                sp.wait_ge(s_qlo, NT)
                sp.dma_start(KX1[HD:P, :, 0, :].bitcast(F32), KX1[0:HD, :, 0, :].bitcast(F32))\
                    .then_inc(s_kdup, 16)
                sp.dma_start(KX1[0:HD, :, 1, :].bitcast(F32), KX1[HD:P, :, 1, :].bitcast(F32))\
                    .then_inc(s_kdup, 16)
                rounds(sp, sp_window1)

            @block.gpsimd
            def _(_pool):
                for n in range(PAIRS):
                    split_w(pool, BLK1 + 1 + n, GRP1 + NT * n)
                pool.wait_ge(s_proj, GRP1 + NT * (PAIRS + 1))
                for k in WO1_POOL:
                    pool_wo(Wo1, k, 1)

        out_phase(1, Wo1, norm_f, x1_dram)


_INS = ["x", "norm_0", "w_in_0", "rel_bias_0", "f_bias_0", "w_out_0", "norm_1", "w_in_1", "sinks_1",
        "w_out_1", "norm_f"]


def constants(np):
    causal = np.where(np.arange(P)[None, :] > np.arange(P)[:, None], BIG, 0.0).astype(np.float32)
    window = np.zeros((P, 2 * P), np.float32)
    window[:HD, :HD] = BIG
    window[:HD, 3 * HD:] = BIG
    window[HD:, :2 * HD] = BIG
    half = HD // 2
    inv = np.float32(10000.0) ** (-np.arange(half, dtype=np.float32) / np.float32(half))
    ang = np.arange(SEQ, dtype=np.float32)[:, None] * inv[None, :]
    cos, sin = np.cos(ang), np.sin(ang)
    rope = np.stack([np.concatenate([cos, cos], 1), np.concatenate([-sin, sin], 1)], 1).astype(np.float32)
    return {"c_ident": np.eye(P, dtype=np.float32), "c_causal": causal, "c_window": window, "c_rope": rope}


def kernel(**inputs):
    import numpy as _np
    import concourse.bacc as _bacc
    from concourse import mybir as _mybir
    from concourse.bass_utils import run_bass_kernel_spmd as _run

    nc = _bacc.Bacc("TRN2", target_bir_lowering=False, num_devices=1)
    arrays, args = {}, []
    given = [(name, _np.ascontiguousarray(inputs[name])) for name in _INS] + list(constants(_np).items())
    for name, a in given:
        arrays[f"in_{name}"] = a
        args.append(nc.dram_tensor(f"in_{name}", a.shape, _mybir.dt.from_np(a.dtype), kind="ExternalInput").ap())
    out = nc.dram_tensor("out", (1, SEQ, DM), F32, kind="ExternalOutput").ap()
    build_trunk(nc, *args, out)
    r = _run(nc, [arrays], core_ids=[0])
    return r.results[0]["out"]
```
